# Optimizing a Trainium2 kernel written in Bass

```python
import math
import jax
import jax.numpy as jnp
from jax import lax
import numpy as np

D_MODEL = 1024
BATCH = 1
SEQ = 512
DEPTH = 1
DEC_BATCH = 8
DEC_SEQ = 1
PAST_LEN = 2048
PAGE_SIZE = 128

A_HEAD_DIM = 64
A_INNER = D_MODEL
A_HEADS = A_INNER // A_HEAD_DIM
A_GROUPS = 2
A_STATE = 128
A_CONV = 4
A_CONV_DIM = A_INNER + 2 * A_GROUPS * A_STATE
A_CHUNK = 64
B_KEY_DIM = 128
B_VAL_DIM = 128
B_HEADS = D_MODEL // B_VAL_DIM
B_FORGET = B_HEADS * B_KEY_DIM
B_INNER = B_HEADS * B_VAL_DIM
B_CHUNK = 64
C_GROUPS = ((128, 1), (512, 4), (2048, 16))
C_HEADS_PER_GROUP = 4
C_HEADS = C_HEADS_PER_GROUP * len(C_GROUPS)
C_HEAD_DIM = 64
C_WIDTH = C_HEADS * C_HEAD_DIM
C_OUT = C_HEADS_PER_GROUP * C_HEAD_DIM
REL_BUCKETS = 32
REL_MAX_DIST = 2048
N_EXPERTS = 32
TOP_K = 4
D_FF = D_MODEL
SWIGLU_ALPHA = 1.702
SWIGLU_LIMIT = 7.0
MOE_BLOCK = 128
MOE_BLOCK_SMALL = 8
DEEPNORM_ALPHA = (2.0 * DEPTH) ** 0.25
DEEPNORM_BETA = (8.0 * DEPTH) ** -0.25
LN_EPS = 1e-5
RMS_EPS = 1e-5
NEG_BIG = -1e30
LOG_FLOOR = 1e-30

IN_WIDTHS = (A_INNER, A_CONV_DIM, A_HEADS, B_FORGET, B_FORGET, B_INNER, B_INNER, C_WIDTH, C_WIDTH, C_WIDTH, 3 * D_MODEL)
IN_DIM = sum(IN_WIDTHS)

kernel_name = 'hybrid_ssd_hgrn2_dilated_moe_step'

def _layernorm(x, g, b):
    xf = x.astype(jnp.float32)
    mu = jnp.mean(xf, -1, keepdims=True)
    var = jnp.mean(jnp.square(xf - mu), -1, keepdims=True)
    return ((xf - mu) * lax.rsqrt(var + LN_EPS) * g.astype(jnp.float32) + b.astype(jnp.float32)).astype(x.dtype)

def _rms(xf):
    return xf * lax.rsqrt(jnp.mean(jnp.square(xf), -1, keepdims=True) + RMS_EPS)

def _pad_time(x, length, axis=1):
    pad = length - x.shape[axis]
    if pad == 0:
        return x
    widths = [(0, 0)] * x.ndim
    widths[axis] = (0, pad)
    return jnp.pad(x, widths)

def _segsum(a):
    t = a.shape[-1]
    c = jnp.cumsum(a, axis=-1)
    d = c[..., :, None] - c[..., None, :]
    return jnp.where(jnp.tril(jnp.ones((t, t), dtype=bool)), d, NEG_BIG)

def _ssd(x, dt, a, bm, cm, h0):
    n, L, H, P = x.shape
    G, NS = bm.shape[2], bm.shape[3]
    R = H // G
    Q = min(A_CHUNK, L)
    nc = -(-L // Q)
    Lp = nc * Q
    xd = _pad_time(x.astype(jnp.float32) * dt[..., None], Lp).reshape(n, nc, Q, G, R, P)
    la = _pad_time(dt * a, Lp).reshape(n, nc, Q, G, R).transpose(0, 3, 4, 1, 2)
    bm = _pad_time(bm.astype(jnp.float32), Lp).reshape(n, nc, Q, G, NS)
    cm = _pad_time(cm.astype(jnp.float32), Lp).reshape(n, nc, Q, G, NS)
    acum = jnp.cumsum(la, axis=-1)
    lmat = jnp.exp(_segsum(la))
    y_diag = jnp.einsum('bclgn,bcsgn,bgrcls,bcsgrp->bclgrp', cm, bm, lmat, xd)
    decay_in = jnp.exp(acum[..., -1:] - acum)
    local = jnp.einsum('bclgn,bgrcl,bclgrp->bcgrpn', bm, decay_in, xd)
    h0r = h0.astype(jnp.float32).reshape(n, 1, G, R, P, NS)
    states = jnp.concatenate([h0r, local], axis=1)
    tot = jnp.pad(acum[..., -1], ((0, 0), (0, 0), (0, 0), (1, 0)))
    states = jnp.einsum('bgrzc,bcgrpn->bzgrpn', jnp.exp(_segsum(tot)), states)
    y_off = jnp.einsum('bclgn,bcgrpn,bgrcl->bclgrp', cm, states[:, :-1], jnp.exp(acum))
    y = (y_diag + y_off).reshape(n, Lp, H, P)[:, :L]
    return y, states[:, -1].reshape(n, H, P, NS)

def _mamba2(z, xbc, dt_raw, conv_buf, h0, conv_w, conv_b, dt_bias, a_log, d_skip, norm_g):
    n, L, _ = xbc.shape
    xpad = jnp.concatenate([conv_buf.astype(xbc.dtype), xbc], axis=1)
    conv = conv_b
    for j in range(A_CONV):
        conv = conv + xpad[:, j:j + L] * conv_w[j]
    conv = jax.nn.silu(conv)
    new_buf = xpad[:, L:]
    gn = A_GROUPS * A_STATE
    xs = conv[..., :A_INNER].reshape(n, L, A_HEADS, A_HEAD_DIM)
    bm = conv[..., A_INNER:A_INNER + gn].reshape(n, L, A_GROUPS, A_STATE)
    cm = conv[..., A_INNER + gn:].reshape(n, L, A_GROUPS, A_STATE)
    dt = jax.nn.softplus(dt_raw.astype(jnp.float32) + dt_bias.astype(jnp.float32))
    a = -jnp.exp(a_log.astype(jnp.float32))
    y, h_new = _ssd(xs, dt, a, bm, cm, h0)
    y = y + d_skip.astype(jnp.float32)[:, None] * xs.astype(jnp.float32)
    y = y.reshape(n, L, A_INNER) * jax.nn.silu(z.astype(jnp.float32))
    y = _rms(y.reshape(n, L, A_GROUPS, A_INNER // A_GROUPS)).reshape(n, L, A_INNER) * norm_g.astype(jnp.float32)
    return y.astype(z.dtype), new_buf, h_new

def _hgrn2_chunk(S, inp):
    q, k, v, g = inp
    b = jnp.cumsum(g, axis=2)
    Q = q.shape[2]
    causal = jnp.tril(jnp.ones((Q, Q), dtype=bool))[:, :, None]
    rel = jnp.exp(jnp.where(causal, b[:, :, :, None, :] - b[:, :, None, :, :], NEG_BIG))
    att = jnp.einsum('nhtk,nhsk,nhtsk->nhts', q, k, rel)
    o = jnp.einsum('nhts,nhsv->nhtv', att, v) + jnp.einsum('nhtk,nhkv->nhtv', q * jnp.exp(b), S)
    b_last = b[:, :, -1]
    S_new = jnp.exp(b_last)[..., None] * S + jnp.einsum('nhsk,nhsv->nhkv', k * jnp.exp(b_last[:, :, None] - b), v)
    return S_new, o

def _hgrn2(q_raw, f_raw, i_raw, g_raw, S0, lb, norm_g):
    f32 = jnp.float32
    n, L, _ = q_raw.shape
    H, K, V = B_HEADS, B_KEY_DIM, B_VAL_DIM
    lbf = lb.astype(f32).reshape(H, K)
    f = f_raw.astype(f32).reshape(n, L, H, K)
    q = jax.nn.silu(q_raw.astype(f32)).reshape(n, L, H, K) * (K ** -0.5)
    logf = jnp.log(jnp.maximum(lbf + (1.0 - lbf) * jax.nn.sigmoid(f), LOG_FLOOR))
    k = (1.0 - lbf) * jax.nn.sigmoid(-f)
    v = i_raw.astype(f32).reshape(n, L, H, V)
    Q = min(B_CHUNK, L)
    nc = -(-L // Q)
    Lp = nc * Q

    def chunks(t):
        return _pad_time(t, Lp).reshape(n, nc, Q, H, t.shape[-1]).transpose(1, 0, 3, 2, 4)

    S_new, o = lax.scan(_hgrn2_chunk, S0.astype(f32), (chunks(q), chunks(k), chunks(v), chunks(logf)))
    o = o.transpose(1, 0, 3, 2, 4).reshape(n, Lp, H, V)[:, :L]
    gate = jax.nn.silu(g_raw.astype(f32)).reshape(n, L, H, V)
    y = _rms(o) * norm_g.astype(f32) * gate
    return y.reshape(n, L, B_INNER).astype(q_raw.dtype), S_new

def _t5_bucket(dist):
    exact = REL_BUCKETS // 2
    d = jnp.maximum(dist, 1).astype(jnp.float32)
    large = exact + (jnp.log(d / exact) / math.log(REL_MAX_DIST / exact) * (REL_BUCKETS - exact)).astype(jnp.int32)
    large = jnp.clip(large, 0, REL_BUCKETS - 1)
    return jnp.where(dist < exact, dist, large)

def _dilated_prompt(q, k, v, tab, window, dilation):
    f32 = jnp.float32
    n, S, h, d = q.shape
    span = window // dilation
    lq = -(-S // dilation)
    sp = lq * dilation
    nb = -(-lq // span)
    lb = nb * span

    def to_blocks(t):
        t = _pad_time(t.astype(f32), sp).reshape(n, lq, dilation, h, d).transpose(0, 2, 1, 3, 4)
        return _pad_time(t, lb, axis=2).reshape(n, dilation, nb, span, h, d)

    def with_prev(t):
        prev = jnp.pad(t[:, :, :-1], ((0, 0), (0, 0), (1, 0), (0, 0), (0, 0), (0, 0)))
        return jnp.concatenate([prev, t], axis=3)

    qb = to_blocks(q)
    kk = with_prev(to_blocks(k))
    vv = with_prev(to_blocks(v))
    qi = jnp.arange(span)[:, None]
    kj = jnp.arange(2 * span)[None, :]
    rel = qi + span - kj
    band = (rel >= 0) & (rel <= span)
    bias = tab.astype(f32)[_t5_bucket(jnp.maximum(rel, 0) * dilation)].transpose(2, 0, 1)
    after_start = (jnp.arange(nb)[:, None, None] > 0) | (kj[None] >= span)
    mask = (band[None] & after_start)[None, None, :, None]
    s = jnp.einsum('bcnqhd,bcnkhd->bcnhqk', qb, kk) * (d ** -0.5) + bias
    s = jnp.where(mask, s, NEG_BIG)
    m = jnp.max(s, -1, keepdims=True)
    p = jnp.exp(s - m)
    den = jnp.sum(p, -1, keepdims=True)
    o = jnp.einsum('bcnhqk,bcnkhd->bcnqhd', p / den, vv)
    lse = (m + jnp.log(den))[..., 0].swapaxes(3, 4)

    def from_blocks(t):
        t = t.reshape(n, dilation, lb, *t.shape[4:])[:, :, :lq]
        t = jnp.moveaxis(t, 1, 2)
        return t.reshape(n, sp, *t.shape[3:])[:, :S]

    return from_blocks(o), from_blocks(lse)

def _dilated_sample(q, k, v, kv_buf, tab, window, dilation):
    f32 = jnp.float32
    n, T, h, d = q.shape
    wb = kv_buf.shape[1]
    kall = jnp.concatenate([kv_buf[:, :, 0].astype(f32), k.astype(f32)], axis=1)
    vall = jnp.concatenate([kv_buf[:, :, 1].astype(f32), v.astype(f32)], axis=1)
    offs = jnp.arange(window // dilation + 1) * dilation
    idx = wb + jnp.arange(T)[:, None] - offs[None, :]
    valid = idx >= 0
    idx = jnp.maximum(idx, 0)
    kg = kall[:, idx]
    vg = vall[:, idx]
    bias = tab.astype(f32)[_t5_bucket(offs)].T
    s = jnp.einsum('bthd,btjhd->bthj', q.astype(f32), kg) * (d ** -0.5) + bias
    s = jnp.where(valid[None, :, None, :], s, NEG_BIG)
    m = jnp.max(s, -1, keepdims=True)
    p = jnp.exp(s - m)
    den = jnp.sum(p, -1, keepdims=True)
    o = jnp.einsum('bthj,btjhd->bthd', p / den, vg)
    return o, (m + jnp.log(den))[..., 0]

def _dilated_mixer(cq, ck, cv, rel_bias, kv_bufs):
    n, L, _ = cq.shape
    q = cq.reshape(n, L, C_HEADS, C_HEAD_DIM)
    k = ck.reshape(n, L, C_HEADS, C_HEAD_DIM)
    v = cv.reshape(n, L, C_HEADS, C_HEAD_DIM)
    outs, lses, kv_new = [], [], []
    for g, (window, dilation) in enumerate(C_GROUPS):
        hs = slice(g * C_HEADS_PER_GROUP, (g + 1) * C_HEADS_PER_GROUP)
        qg, kg, vg = q[:, :, hs], k[:, :, hs], v[:, :, hs]
        tab = rel_bias[:, hs]
        rows = jnp.stack([kg, vg], axis=2)
        if kv_bufs is None:
            o, lse = _dilated_prompt(qg, kg, vg, tab, window, dilation)
            kv_new.append(rows[:, L - min(window, L):])
        else:
            o, lse = _dilated_sample(qg, kg, vg, kv_bufs[g], tab, window, dilation)
            kv_new.append(rows)
        outs.append(o)
        lses.append(lse)
    wts = jax.nn.softmax(jnp.stack(lses, 0), axis=0)
    o = wts[0][..., None] * outs[0] + wts[1][..., None] * outs[1] + wts[2][..., None] * outs[2]
    return o.reshape(n, L, C_OUT).astype(cq.dtype), kv_new

def _moe(h, router_w, router_b, w1, b1, w2, b2):
    n_tok, d = h.shape
    logits = (h @ router_w + router_b).astype(jnp.float32)
    top_v, top_e = lax.top_k(logits, TOP_K)
    gates = jax.nn.softmax(top_v, axis=-1)
    m = n_tok * TOP_K
    blk = MOE_BLOCK if m >= MOE_BLOCK * N_EXPERTS else MOE_BLOCK_SMALL
    n_blocks = -(-m // blk) + N_EXPERTS
    rows = n_blocks * blk
    flat_e = top_e.reshape(-1)
    order = jnp.argsort(flat_e)
    se = flat_e[order]
    counts = jnp.zeros((N_EXPERTS,), jnp.int32).at[flat_e].add(1)
    padded = (counts + blk - 1) // blk * blk
    start = jnp.cumsum(counts) - counts
    pend = jnp.cumsum(padded)
    pstart = pend - padded
    dest = pstart[se] + jnp.arange(m, dtype=jnp.int32) - start[se]
    tok = (jnp.arange(m, dtype=jnp.int32) // TOP_K)[order]
    buf_tok = jnp.zeros((rows,), jnp.int32).at[dest].set(tok)
    buf_gate = jnp.zeros((rows,), jnp.float32).at[dest].set(gates.reshape(-1)[order])
    block_e = jnp.minimum(jnp.searchsorted(pend, jnp.arange(n_blocks, dtype=jnp.int32) * blk, side='right'), N_EXPERTS - 1)
    xb = h[buf_tok].reshape(n_blocks, blk, d)

    def expert_block(args):
        xe, e = args
        u = xe @ w1[e] + b1[e]
        glu = jnp.minimum(u[..., ::2], SWIGLU_LIMIT)
        lin = jnp.clip(u[..., 1::2], -SWIGLU_LIMIT, SWIGLU_LIMIT)
        act = glu * jax.nn.sigmoid(SWIGLU_ALPHA * glu) * (lin + 1.0)
        return act @ w2[e] + b2[e]

    yb = lax.map(expert_block, (xb, block_e))
    y = jnp.zeros((n_tok, d), jnp.float32).at[buf_tok].add(yb.reshape(rows, d).astype(jnp.float32) * buf_gate[:, None])
    return y.astype(h.dtype)

def _layer(x, prm, lb, rel_bias, conv_buf, ssm0, hgrn0, kv_bufs):
    n, L, D = x.shape
    u = x @ prm['w_in']
    (z, xbc, dt_raw, bq, bf, bi, bg, cq, ck, cv, gates) = jnp.split(u, np.cumsum(IN_WIDTHS)[:-1].tolist(), axis=-1)
    ya, conv_new, ssm_new = _mamba2(z, xbc, dt_raw, conv_buf, ssm0, prm['conv_w'], prm['conv_b'], prm['dt_bias'],
                                    prm['a_log'], prm['d_skip'], prm['ssm_norm_g'])
    yb, hgrn_new = _hgrn2(bq, bf, bi, bg, hgrn0, lb, prm['hgrn_norm_g'])
    yc, kv_new = _dilated_mixer(cq, ck, cv, rel_bias, kv_bufs)
    ga, gb, gc = jnp.split(jax.nn.sigmoid(gates), 3, axis=-1)
    merged = ga * (ya @ prm['w_branch_a']) + gb * (yb @ prm['w_branch_b']) + gc * (yc @ prm['w_branch_c'])
    x = _layernorm(DEEPNORM_ALPHA * x + merged @ prm['w_out'], prm['ln1_g'], prm['ln1_b'])
    f = _moe(x.reshape(n * L, D), prm['router_w'], prm['router_b'], prm['moe_w1'], prm['moe_b1'],
             prm['moe_w2'], prm['moe_b2']).reshape(n, L, D)
    x = _layernorm(DEEPNORM_ALPHA * x + f, prm['ln2_g'], prm['ln2_b'])
    return x, (conv_new, ssm_new, hgrn_new, kv_new[0], kv_new[1], kv_new[2])

def _stack(states, i):
    return jnp.stack([s[i] for s in states], axis=0)

def setup_inputs(seed: int = 0) -> dict:
    key = jax.random.key(seed)
    keys = iter(jax.random.split(key, 48))
    f32 = jnp.float32

    def normal(shape, scale):
        return jax.random.normal(next(keys), shape, f32) * scale

    def gain(shape):
        return 1.0 + normal(shape, 0.02)

    def kv_shape(w):
        return (DEPTH, DEC_BATCH, min(w, PAST_LEN), 2, C_HEADS_PER_GROUP, C_HEAD_DIM)

    dt0 = jnp.exp(jax.random.uniform(next(keys), (DEPTH, A_HEADS), f32, math.log(1e-3), math.log(1e-1)))
    a_log = jnp.log(jax.random.uniform(next(keys), (DEPTH, A_HEADS), f32, 1.0, 16.0))
    return {
        'x_prompt': normal((BATCH, SEQ, D_MODEL), 1.0),
        'x_sample': normal((DEC_BATCH, DEC_SEQ, D_MODEL), 1.0),
        'state_conv': normal((DEPTH, DEC_BATCH, A_CONV - 1, A_CONV_DIM), 1.0),
        'state_ssm': normal((DEPTH, DEC_BATCH, A_HEADS, A_HEAD_DIM, A_STATE), 0.1),
        'state_hgrn': normal((DEPTH, DEC_BATCH, B_HEADS, B_KEY_DIM, B_VAL_DIM), 0.5),
        'cache_kv_w128': normal(kv_shape(C_GROUPS[0][0]), 1.0),
        'cache_kv_w512': normal(kv_shape(C_GROUPS[1][0]), 1.0),
        'cache_kv_w2048': normal(kv_shape(C_GROUPS[2][0]), 1.0),
        'w_in': normal((DEPTH, D_MODEL, IN_DIM), D_MODEL ** -0.5),
        'conv_w': normal((DEPTH, A_CONV, A_CONV_DIM), A_CONV ** -0.5),
        'conv_b': normal((DEPTH, A_CONV_DIM), 0.01),
        'dt_bias': dt0 + jnp.log(-jnp.expm1(-dt0)),
        'a_log': a_log,
        'd_skip': gain((DEPTH, A_HEADS)),
        'ssm_norm_g': gain((DEPTH, A_INNER)),
        'hgrn_lb': normal((DEPTH, B_FORGET), 0.5),
        'hgrn_norm_g': gain((DEPTH, B_VAL_DIM)),
        'rel_bias': normal((REL_BUCKETS, C_HEADS), 0.2),
        'w_branch_a': normal((DEPTH, A_INNER, D_MODEL), A_INNER ** -0.5),
        'w_branch_b': normal((DEPTH, B_INNER, D_MODEL), B_INNER ** -0.5),
        'w_branch_c': normal((DEPTH, C_OUT, D_MODEL), C_OUT ** -0.5),
        'w_out': normal((DEPTH, D_MODEL, D_MODEL), DEEPNORM_BETA * D_MODEL ** -0.5),
        'ln1_g': gain((DEPTH, D_MODEL)),
        'ln1_b': normal((DEPTH, D_MODEL), 0.01),
        'router_w': normal((DEPTH, D_MODEL, N_EXPERTS), D_MODEL ** -0.5),
        'router_b': normal((DEPTH, N_EXPERTS), 0.01),
        'moe_w1': normal((DEPTH, N_EXPERTS, D_MODEL, 2 * D_FF), D_MODEL ** -0.5),
        'moe_b1': normal((DEPTH, N_EXPERTS, 2 * D_FF), 0.01),
        'moe_w2': normal((DEPTH, N_EXPERTS, D_FF, D_MODEL), DEEPNORM_BETA * D_FF ** -0.5),
        'moe_b2': normal((DEPTH, N_EXPERTS, D_MODEL), 0.01),
        'ln2_g': gain((DEPTH, D_MODEL)),
        'ln2_b': normal((DEPTH, D_MODEL), 0.01),
    }

def reference(x_prompt, x_sample, state_conv, state_ssm, state_hgrn, cache_kv_w128, cache_kv_w512, cache_kv_w2048,
              w_in, conv_w, conv_b, dt_bias, a_log, d_skip, ssm_norm_g, hgrn_lb, hgrn_norm_g, rel_bias,
              w_branch_a, w_branch_b, w_branch_c, w_out, ln1_g, ln1_b, router_w, router_b,
              moe_w1, moe_b1, moe_w2, moe_b2, ln2_g, ln2_b):
    p_lb = jax.nn.softmax(hgrn_lb.astype(jnp.float32), axis=0)
    lower_bounds = jnp.cumsum(p_lb, axis=0) - p_lb[0]
    yp, ys = x_prompt, x_sample
    st_p, st_s = [], []
    for l in range(DEPTH):
        prm = {'w_in': w_in[l], 'conv_w': conv_w[l], 'conv_b': conv_b[l], 'dt_bias': dt_bias[l], 'a_log': a_log[l],
               'd_skip': d_skip[l], 'ssm_norm_g': ssm_norm_g[l], 'hgrn_norm_g': hgrn_norm_g[l],
               'w_branch_a': w_branch_a[l], 'w_branch_b': w_branch_b[l], 'w_branch_c': w_branch_c[l],
               'w_out': w_out[l], 'ln1_g': ln1_g[l], 'ln1_b': ln1_b[l], 'router_w': router_w[l],
               'router_b': router_b[l], 'moe_w1': moe_w1[l], 'moe_b1': moe_b1[l], 'moe_w2': moe_w2[l],
               'moe_b2': moe_b2[l], 'ln2_g': ln2_g[l], 'ln2_b': ln2_b[l]}
        nb = yp.shape[0]
        conv0 = jnp.zeros((nb, A_CONV - 1, A_CONV_DIM), yp.dtype)
        ssm0 = jnp.zeros((nb, A_HEADS, A_HEAD_DIM, A_STATE), jnp.float32)
        hgrn0 = jnp.zeros((nb, B_HEADS, B_KEY_DIM, B_VAL_DIM), jnp.float32)
        yp, sp = _layer(yp, prm, lower_bounds[l], rel_bias, conv0, ssm0, hgrn0, None)
        ys, ss = _layer(ys, prm, lower_bounds[l], rel_bias, state_conv[l], state_ssm[l], state_hgrn[l],
                        (cache_kv_w128[l], cache_kv_w512[l], cache_kv_w2048[l]))
        st_p.append(sp)
        st_s.append(ss)
    return (yp, ys, _stack(st_p, 0), _stack(st_s, 0), _stack(st_p, 1), _stack(st_s, 1), _stack(st_p, 2), _stack(st_s, 2),
            _stack(st_p, 3), _stack(st_s, 3), _stack(st_p, 4), _stack(st_s, 4), _stack(st_p, 5), _stack(st_s, 5))


_drawn_inputs = setup_inputs


def setup_inputs(seed=0):
    import zlib

    import numpy as np

    out = dict(_drawn_inputs(seed))
    spreads = {}
    factors = {'cache_kv_w128': 4.262,
     'cache_kv_w512': 4.144,
     'cache_kv_w2048': 4.417,
     'conv_b': 3.101,
     'd_skip': 6.444,
     'ssm_norm_g': 4.995,
     'hgrn_norm_g': 6.077,
     'rel_bias': 4.526,
     'router_b': 3.259,
     'moe_b1': 8.0,
     'moe_b2': 8.0,
     'ln2_g': 2.745,
     'ln2_b': 5.791}
    for name, (base, spread) in spreads.items():
        noise = np.random.default_rng([zlib.crc32(name.encode()), seed]).standard_normal(out[name].shape)
        drawn = base * np.exp(spread * noise) if base else spread * noise
        out[name] = jnp.asarray(drawn.astype(out[name].dtype))
    for name, factor in factors.items():
        out[name] = (out[name] * factor).astype(out[name].dtype)
    return out
```

```python
from contextlib import ExitStack

import concourse.bass as bass
from concourse import mybir

F32 = mybir.dt.float32
U32 = mybir.dt.uint32
ALU = mybir.AluOpType
ACT = mybir.ActivationFunctionType
AX = mybir.AxisListType

D = 1024
KT = D // 128
TP = 512
TS = 8
T = TP + TS
NC = TP // 128
HALF = T // 2
AH, AP_, AN, AG = 16, 64, 128, 2
ACH = D + 2 * AG * AN
AM = ACH // 128
BH, BK = 8, 128
CH, CD, CG, CHG = 12, 64, 3, 4
CW = CH * CD
NE, TOPK, FF = 32, 4, 1024
EPS = 1e-5
ALPHA = 2.0 ** 0.25
NEG = -1e30
Z0 = 0
XBC0 = Z0 + D
DT0 = XBC0 + ACH
BQ0 = DT0 + AH
BF0 = BQ0 + D
BI0 = BF0 + D
BG0 = BI0 + D
CQ0 = BG0 + D
CK0 = CQ0 + CW
CV0 = CK0 + CW
GT0 = CV0 + CW

SLOT = 4096
SLOTS = 9
LEVELS = (128, 64, 32, 16, 8, 4, 2)


class Stage:

    def __init__(self, nc, ctx, name):
        self.nc, self.name, self.sems = nc, name, []
        ctx.callback(self.release)

    def sem(self, name):
        self.sems.append(self.nc.alloc_semaphore(f"{self.name}_{name}"))
        return self.sems[-1]

    def release(self):
        self.nc.clear_and_free_semaphores(self.sems)
        self.nc.all_engine_barrier()


def linker(eng, sem):
    count = [0]

    def link(ins):
        count[0] += 1
        ins.then_inc(sem, 1)
        eng.wait_ge(sem, count[0])
    return link


def bc(ap, n):
    return ap.unsqueeze(len(ap.shape)).broadcast_to(list(ap.shape) + [n])


def bmid(ap, n):
    return ap.unsqueeze(1).broadcast_to([ap.shape[0], n, ap.shape[1]])


class Mem:

    def __init__(self, nc, ctx):
        def sb(name, shape, dt=F32):
            return ctx.enter_context(nc.sbuf_tensor(name, shape, dt))
        self.arena = sb("arena", [128, SLOTS * SLOT])
        self.xT = sb("xT", [128, KT, T])
        self.yaT = sb("yaT", [128, KT, T])
        self.ybT = sb("ybT", [128, KT, T])
        self.ycT = sb("ycT", [128, 2, T])
        self.ident = sb("ident", [128, 128])
        self.tri = sb("tri", [128, 128])
        self.ones = sb("ones", [128, 128])
        self.work = sb("work", [128, 1600])
        self.bank = ctx.enter_context(nc.psum_tensor("bank", [128, 8, 512], F32))

    def slot(self, i, n=SLOT):
        return self.arena[:, i * SLOT:i * SLOT + n]


def load_x(nc, m, t):
    with ExitStack() as ctx:
        st = Stage(nc, ctx, "x")
        s_const, s_x, s_tr, s_ev, s_ea = (st.sem(n) for n in ("const", "x", "tr", "ev", "ea"))
        xp = m.slot(0).rearrange("p (c d) -> p c d", c=NC)
        xs = m.slot(1)[0:TS, 0:D]
        block = ctx.enter_context(nc.Block())

        @block.sync
        def _(sp):
            for dst, name in ((m.ident, "c_ident"), (m.tri, "c_tri"), (m.ones, "c_ones")):
                sp.dma_start(dst[:], t[name]).then_inc(s_const, 16)
            for c in range(NC):
                sp.dma_start(xp[:, c, :], t["x_prompt"][0, c * 128:(c + 1) * 128, :]).then_inc(s_x, 16)
            sp.dma_start(xs, t["x_sample"][:, 0, :]).then_inc(s_x, 16)

        @block.tensor
        def _(pe):
            pe.wait_ge(s_const, 48)
            pe.wait_ge(s_x, 16 * (NC + 1))
            for c in range(NC):
                for h in range(2):
                    n = 2 * c + h
                    for j in range(4):
                        k = 4 * h + j
                        last = pe.transpose(m.bank[:, n, j * 128:(j + 1) * 128], xp[:, c, k * 128:(k + 1) * 128], m.ident[:])
                    last.then_inc(s_tr, 1)
            pe.wait_ge(s_ev, 1)
            for k in range(KT):
                last = pe.transpose(m.bank[:, 0, k * TS:(k + 1) * TS], xs[:, k * 128:(k + 1) * 128], m.ident[0:TS, 0:TS])
            last.then_inc(s_tr, 1)

        @block.vector
        def _(dve):
            for n in range(0, 8, 2):
                dve.wait_ge(s_tr, n + 1)
                dve.tensor_copy(m.xT[:, 0:4, n // 2 * 128:(n // 2 + 1) * 128],
                                m.bank[:, n, :].rearrange("p (j q) -> p j q", j=4)).then_inc(s_ev, 1)
            dve.wait_ge(s_tr, 9)
            dve.tensor_copy(m.xT[:, :, TP:T], m.bank[:, 0, 0:KT * TS].rearrange("p (k q) -> p k q", k=KT)).then_inc(s_ev, 1)

        @block.scalar
        def _(act):
            for n in range(1, 8, 2):
                act.wait_ge(s_tr, n + 1)
                act.copy(m.xT[:, 4:8, n // 2 * 128:(n // 2 + 1) * 128],
                         m.bank[:, n, :].rearrange("p (j q) -> p j q", j=4)).then_inc(s_ea, 1)


def project(nc, m, t, name, chunks, units, ring):
    with ExitStack() as ctx:
        st = Stage(nc, ctx, name)
        s_w = [st.sem(f"w{i}") for i in range(len(ring))]
        s_u, s_ev, s_ea = st.sem("u"), st.sem("ev"), st.sem("ea")
        last_unit = [max(i for i, u in enumerate(units) if u[0] == c) for c in range(len(chunks))]
        wt = [r[:, 0:KT * n].rearrange("p (k n) -> p k n", k=KT)
              for r, n in ((ring[c % len(ring)], chunks[c][1]) for c in range(len(chunks)))]
        block = ctx.enter_context(nc.Block())

        @block.sync
        def _(sp):
            for c, (c0, n) in enumerate(chunks):
                if c >= len(ring):
                    sp.wait_ge(s_u, last_unit[c - len(ring)] + 1)
                sp.dma_start(wt[c], t["w_in"][0, :, c0:c0 + n].rearrange("(k p) n -> p k n", p=128))\
                    .then_inc(s_w[c % len(ring)], 16)

        @block.tensor
        def _(pe):
            at = -1
            for i, (c, form, off, n, a, b, _) in enumerate(units):
                if c != at:
                    pe.wait_ge(s_w[c % len(ring)], 16 * (c // len(ring) + 1))
                    at = c
                if i >= 8:
                    pe.wait_ge(s_ea if i % 2 else s_ev, (i - 8) // 2 + 1)
                for k in range(KT):
                    w, x = wt[c][:, k, off:off + n], m.xT[:, k, a:b]
                    if form == "chan":
                        last = pe.matmul(m.bank[0:n, i % 8, 0:b - a], w, x, start=(k == 0), stop=(k == KT - 1))
                    else:
                        last = pe.matmul(m.bank[0:b - a, i % 8, 0:n], x, w, start=(k == 0), stop=(k == KT - 1))
                last.then_inc(s_u, 1)

        def evacuate(eng, copy, odd, s_done):
            for i, u in enumerate(units):
                if i % 2 != odd:
                    continue
                eng.wait_ge(s_u, i + 1)
                for dst, rows, a, b in u[6]:
                    src = m.bank[0:rows, i % 8, a:b]
                    if len(dst.shape) == 3:
                        src = src.rearrange("p (i r) -> p i r", r=dst.shape[2])
                    last = copy(dst, src)
                last.then_inc(s_done, 1)

        @block.vector
        def _(dve):
            evacuate(dve, dve.tensor_copy, 0, s_ev)

        @block.scalar
        def _(act):
            evacuate(act, act.copy, 1, s_ea)


def chan_units(chunk, off, dst_p, dst_s):
    return [(chunk, "chan", off, 128, 0, HALF, [(dst_p[:, 0:HALF], 128, 0, HALF)]),
            (chunk, "chan", off, 128, HALF, T, [(dst_p[:, HALF:TP], 128, 0, TP - HALF), (dst_s, 128, TP - HALF, HALF)])]


def tok_units(chunk, off, n, dst):
    return [(chunk, "tok", off, n, c * 128, (c + 1) * 128, [(dst(c), 128, 0, n)]) for c in range(NC)]


def mixer_a(nc, m, t, o):
    raw = m.arena[:, 0:AM * 515].rearrange("p (m q) -> p m q", m=AM)
    raws = m.arena[:, AM * 515:AM * 515 + AM * TS].rearrange("p (m q) -> p m q", m=AM)
    zs = m.arena[:, AM * 523:AM * 523 + 64].rearrange("p (m q) -> p m q", m=KT)
    dtr = m.arena[:, AM * 523 + 64:AM * 523 + 128].rearrange("p (c h) -> p c h", c=NC)
    dts_raw = m.arena[0:AH, AM * 523 + 128:AM * 523 + 136]
    z = m.slot(2).rearrange("p (c d) -> p c d", c=NC)
    chunks = [(XBC0 + 512 * i, 512) for i in range(3)] + [(Z0, 512), (Z0 + 512, 512), (DT0, AH)]
    units = []
    for c in range(3):
        for j in range(4):
            units += chan_units(c, 128 * j, raw[:, 4 * c + j, 3:515], raws[:, 4 * c + j, :])
    for c in range(2):
        units += tok_units(3 + c, 0, 512, lambda k, c=c: z[:, k, 512 * c:512 * c + 512])
        for j in range(4):
            units.append((3 + c, "chan", 128 * j, 128, TP, T, [(zs[:, 4 * c + j, :], 128, 0, TS)]))
    units += tok_units(5, 0, AH, lambda k: dtr[:, k, :])
    units.append((5, "chan", 0, AH, TP, T, [(dts_raw, AH, 0, TS)]))
    project(nc, m, t, "pa", chunks, units, [m.slot(i) for i in (3, 4, 5, 6)])

    with ExitStack() as ctx:
        st = Stage(nc, ctx, "a")
        xc = m.arena[:, 3 * SLOT:3 * SLOT + AM * 512].rearrange("p (m q) -> p m q", m=AM)
        o0 = 3 * SLOT + AM * 512
        par = m.arena[:, o0:o0 + AM * 29].rearrange("p (m j) -> p m j", m=AM)
        o0 += AM * 29
        xcs = m.arena[:, o0:o0 + AM * TS].rearrange("p (m q) -> p m q", m=AM)
        o0 += AM * TS
        tmps = m.arena[:, o0:o0 + AM * TS].rearrange("p (m q) -> p m q", m=AM)
        o0 += AM * TS
        stag = m.arena[:, o0:o0 + AM * 11].rearrange("p (m q) -> p m q", m=AM)
        o0 += AM * 11
        ex = m.arena[:, o0:o0 + 8 * 17].rearrange("p (m q) -> p m q", m=8)
        o0 += 8 * 17
        us = m.arena[:, o0:o0 + 64].rearrange("p (m b) -> p m b", m=8)
        o0 += 64
        ys = m.arena[:, o0:o0 + 64].rearrange("p (m b) -> p m b", m=8)
        o0 += 64
        gs = m.arena[:, o0:o0 + 64].rearrange("p (m b) -> p m b", m=8)
        o0 += 64
        ngT = m.arena[:, o0:o0 + 8]
        o0 += 8
        dsm = m.arena[0:AH, o0:o0 + 40]
        o0 += 40
        assert o0 <= 5 * SLOT
        xtok = m.slot(5).rearrange("p (c d) -> p c d", c=NC)
        xdt = m.slot(6).rearrange("p (c d) -> p c d", c=NC)
        s8 = m.slot(8)
        sc = s8[:, 0:1024].rearrange("p (i q) -> p i q", i=2 * NC)
        btok = s8[:, 1024:2048].rearrange("p (c g n) -> p c g n", c=NC, g=AG)
        stT = s8[:, 2048:3072].rearrange("p (g q) -> p g q", g=AG)
        xdd = s8[:, 3072:4096].rearrange("p (g q) -> p g q", g=AG)
        y = m.work[:, 0:1024].rearrange("p (g q) -> p g q", g=AG)
        mt = m.slot(7)[:, 0:2048].rearrange("p (i q) -> p i q", i=4)
        gn = m.slot(7)[:, 2048:3072]
        junk = m.slot(7)[:, 3072:4096]
        w0 = 1024
        dt = m.work[:, w0:w0 + 64]
        la = m.work[:, w0 + 64:w0 + 128]
        nacum = m.work[:, w0 + 128:w0 + 192]
        eac = m.work[:, w0 + 192:w0 + 256]
        dec = m.work[:, w0 + 256:w0 + 320]
        etot = m.work[:, w0 + 320:w0 + 384]
        dtb = m.work[:, w0 + 384:w0 + 400]
        aneg = m.work[:, w0 + 400:w0 + 416]
        dsk = m.work[:, w0 + 416:w0 + 432]
        rs = m.work[:, w0 + 432:w0 + 440]
        tmp64 = m.work[:, w0 + 440:w0 + 504]
        rows = m.slot(5)[0:29, 0:ACH]
        csb = m.slot(6)[0:11, 0:ACH]
        ngrow = m.slot(6)[0:8, ACH:ACH + 128]

        s_ld, s_par, s_tp, s_tq, s_cs, s_out = (st.sem(n) for n in ("ld", "par", "tp", "tq", "cs", "out"))
        s_v, s_a = st.sem("v"), st.sem("a")
        s_conv, s_silu, s_dt1, s_dt2, s_la, s_cum = (st.sem(n) for n in ("conv", "silu", "dt1", "dt2", "la", "cum"))
        s_xt, s_xe, s_xa, s_sc, s_scm = (st.sem(n) for n in ("xt", "xe", "xa", "sc", "scm"))
        s_l, s_ld1, s_lx, s_m, s_y, s_yo, s_sd, s_xdd, s_sn = (st.sem(n) for n in
                                                             ("l", "ld1", "lx", "m", "y", "yo", "sd", "xdd", "sn"))
        s_g, s_sq, s_z, s_yn, s_yt, s_ye, s_ini = (st.sem(n) for n in ("g", "sq", "z", "yn", "yt", "ye", "ini"))
        s_cum2, s_pr, s_var, s_rstd = (st.sem(n) for n in ("cum2", "pr", "var", "rstd"))
        block = ctx.enter_context(nc.Block())

        @block.sync
        def _(sp):
            sp.dma_start(rows[0:24, :], t["state_conv"][0].rearrange("b j c -> (b j) c")).then_inc(s_ld, 16)
            sp.dma_start(rows[24:28, :], t["conv_w"][0]).then_inc(s_ld, 16)
            sp.dma_start(rows[28:29, :], t["conv_b"]).then_inc(s_ld, 16)
            sp.dma_start(dtb, t["dt_bias"][0].partition_broadcast(128)).then_inc(s_ld, 16)
            sp.dma_start(aneg, t["a_log"][0].partition_broadcast(128)).then_inc(s_ld, 16)
            sp.dma_start(dsk, t["d_skip"][0].partition_broadcast(128)).then_inc(s_ld, 16)
            sp.dma_start(gn, t["ssm_norm_g"][0].partition_broadcast(128)).then_inc(s_ld, 16)
            sp.dma_start(ngrow, t["ssm_norm_g"][0].rearrange("(m p) -> m p", p=128)).then_inc(s_ld, 16)
            sp.dma_start(o["conv_s"][0, :, 0:2, :], t["state_conv"][0, :, 1:3, :]).then_inc(s_out, 16)
            sp.wait_ge(s_cs, 1)
            sp.dma_start(o["conv_p"][0, 0], csb[0:3, :]).then_inc(s_out, 16)
            sp.dma_start(o["conv_s"][0, :, 2, :], csb[3:11, :]).then_inc(s_out, 16)
            sp.wait_ge(s_out, 48)

        @block.tensor
        def _(pe):
            pe.wait_ge(s_ld, 16 * 8)
            for i in range(AM):
                last = pe.transpose(m.bank[:, 0, i * 29:(i + 1) * 29], rows[:, i * 128:(i + 1) * 128], m.ident[0:29, 0:29])
            last = pe.transpose(m.bank[:, 0, 400:408], ngrow, m.ident[0:8, 0:8])
            last.then_inc(s_tp, 1)
            pe.wait_ge(s_par, 1)
            for i in range(AM):
                last = pe.transpose(m.bank[0:11, 1 + i // 4, (i % 4) * 128:(i % 4 + 1) * 128], stag[:, i, :], m.ident[:])
            last.then_inc(s_tp, 1)
            pe.wait_ge(s_la, 1)
            pe.matmul(m.bank[:, 4, 0:64], m.tri[:], la, start=True, stop=True)
            pe.matmul(m.bank[:, 4, 64:128], m.ones[:], la, start=True, stop=True).then_inc(s_cum, 1)
            pe.wait_ge(s_silu, AM)
            for c in range(NC):
                for h in range(3):
                    n = 3 * c + h
                    b = 5 + n % 3
                    if n >= 3:
                        pe.wait_ge(s_xe, n - 2)
                    for j in range(4 if h < 2 else 2):
                        last = pe.transpose(m.bank[:, b, j * 128:(j + 1) * 128],
                                            xc[:, 4 * h + j, c * 128:(c + 1) * 128], m.ident[:])
                    last.then_inc(s_xt, 1)
            pe.wait_ge(s_cs, 1)
            for c in range(NC):
                for g in range(AG):
                    n = 2 * c + g
                    last = pe.matmul(m.bank[:, 2 + n // 4, (n % 4) * 128:(n % 4 + 1) * 128],
                                     xc[:, 8 + g, c * 128:(c + 1) * 128], xc[:, 10 + g, c * 128:(c + 1) * 128],
                                     start=True, stop=True)
            last.then_inc(s_sc, 1)
            pe.wait_ge(s_scm, 2)
            pe.wait_ge(s_xa, 12)
            for c in range(NC):
                for g in range(AG):
                    n = 2 * c + g
                    for q in range(2):
                        i = 2 * n + q
                        if i >= 2:
                            pe.wait_ge(s_ld1, i - 1)
                        for j in range(4):
                            h = 8 * g + 4 * q + j
                            last = pe.matmul(m.bank[:, i % 2, j * 128:(j + 1) * 128],
                                             la[:, c * AH + h:c * AH + h + 1].broadcast_to([128, 128]), m.tri[:],
                                             start=True, stop=True)
                        last.then_inc(s_l, 1)
                    if n >= 2:
                        pe.wait_ge(s_yn, n - 1)
                    if n >= 2:
                        pe.wait_ge(s_sn, n - 1)
                    pe.matmul(m.bank[:, 4 + n % 2, :], xc[:, 10 + g, c * 128:(c + 1) * 128], stT[:, g, :],
                              start=True, stop=True).then_inc(s_yo, 1)
                    for q in range(2):
                        i = 2 * n + q
                        pe.wait_ge(s_m, i + 1)
                        for j in range(4):
                            h = 4 * q + j
                            last = pe.matmul(m.bank[:, 2 + n % 2, h * 64:(h + 1) * 64], mt[:, 2 + i % 2, j * 128:(j + 1) * 128],
                                             xdt[:, c, (8 * g + h) * 64:(8 * g + h + 1) * 64], start=True, stop=True)
                    last.then_inc(s_y, 1)
                    pe.wait_ge(s_xdd, n + 1)
                    if n >= 1:
                        pe.wait_ge(s_sn, n)
                    pe.matmul(m.bank[:, 6, :], btok[:, c, g, :], xdd[:, g, :], start=True, stop=True).then_inc(s_sd, 1)
                pe.wait_ge(s_yn, 2 * c + 2)
                for h in range(2):
                    if 2 * c + h >= 1:
                        pe.wait_ge(s_ye, 2 * c + h)
                    for j in range(4):
                        last = pe.transpose(m.bank[:, 7, j * 128:(j + 1) * 128], y[:, h, j * 128:(j + 1) * 128], m.ident[:])
                    last.then_inc(s_yt, 1)

        @block.vector
        def _(dve):
            link = linker(dve, s_v)
            dve.wait_ge(s_ld, 16 * 8)
            link(dve.memset(raw[:, :, 0:3], 0.0))
            link(dve.memset(stT, 0.0))
            dve.wait_ge(s_tp, 1)
            link(dve.tensor_copy(par, m.bank[:, 0, 0:AM * 29].rearrange("p (m j) -> p m j", m=AM)))
            link(dve.tensor_copy(ngT, m.bank[:, 0, 400:408]))
            link(dve.tensor_copy(stag[:, :, 0:3], raw[:, :, 512:515]))
            dve.tensor_copy(stag[:, :, 3:11], raws).then_inc(s_par, 1)
            for i in range(AM):
                link(dve.tensor_scalar(xc[:, i, :], raw[:, i, 0:512], par[:, i, 24:25], par[:, i, 28:29], ALU.mult, ALU.add))
                for j in range(1, 4):
                    ins = dve.scalar_tensor_tensor(xc[:, i, :], raw[:, i, j:j + 512], par[:, i, 24 + j:25 + j], xc[:, i, :],
                                                   ALU.mult, ALU.add)
                    if j < 3:
                        link(ins)
                ins.then_inc(s_conv, 1)
            link(dve.tensor_tensor(dt.rearrange("p (c h) -> p c h", c=NC), dtr, bmid(dtb, NC), ALU.add))
            link(dve.scalar_tensor_tensor(tmp64, dt, -1.0, dt, ALU.mult, ALU.max))
            dve.tensor_scalar(dt, dt, 0.0, None, ALU.max).then_inc(s_dt1, 1)
            dve.wait_ge(s_dt2, 1)
            link(dve.tensor_tensor(dt, dt, tmp64, ALU.add))
            dve.scalar_tensor_tensor(la.rearrange("p (c h) -> p c h", c=NC), dt.rearrange("p (c h) -> p c h", c=NC), -1.0,
                                     bmid(aneg, NC), ALU.mult, ALU.mult).then_inc(s_la, 1)
            dve.wait_ge(s_cum, 1)
            link(dve.tensor_scalar(nacum, m.bank[:, 4, 0:64], -1.0, None, ALU.mult))
            link(dve.tensor_tensor(dec, m.bank[:, 4, 64:128], nacum, ALU.add))
            dve.tensor_scalar(etot, m.bank[:, 4, 64:128], 1.0, None, ALU.mult).then_inc(s_cum2, 1)
            dve.wait_ge(s_tp, 2)
            dve.tensor_copy(csb, m.bank[0:11, 1:4, :]).then_inc(s_cs, 1)
            for n in range(12):
                c, h = divmod(n, 3)
                dve.wait_ge(s_xt, n + 1)
                src = m.bank[:, 5 + n % 3, :]
                if h < 2:
                    dve.tensor_copy(xtok[:, c, h * 512:(h + 1) * 512], src).then_inc(s_xe, 1)
                else:
                    dve.tensor_copy(btok[:, c, :, :], src[:, 0:256].rearrange("p (g n) -> p g n", g=AG)).then_inc(s_xe, 1)
            dve.wait_ge(s_xe, 12)
            dve.wait_ge(s_out, 48)
            for c in range(NC):
                dve.tensor_tensor(xdt[:, c, :].rearrange("p (h q) -> p h q", h=AH), xtok[:, c, :].rearrange("p (h q) -> p h q", h=AH),
                                  bc(dt[:, c * AH:(c + 1) * AH], AP_), ALU.mult).then_inc(s_xa, 3)
            dve.wait_ge(s_sc, 1)
            for h in range(2):
                dve.tensor_tensor(sc[:, 4 * h:4 * h + 4, :], m.bank[:, 2 + h, :].rearrange("p (i q) -> p i q", i=4),
                                  bmid(m.tri[:], 4), ALU.mult).then_inc(s_scm, 1)
            dve.wait_ge(s_scm, 2)
            dve.wait_ge(s_xa, 12)
            dve.wait_ge(s_pr, 1)
            for c in range(NC):
                for g in range(AG):
                    n = 2 * c + g
                    for q in range(2):
                        i = 2 * n + q
                        hs = c * AH + 8 * g + 4 * q
                        lt, mm = mt[:, i % 2, :].rearrange("p (j q) -> p j q", j=4), mt[:, 2 + i % 2, :].rearrange("p (j q) -> p j q", j=4)
                        dve.wait_ge(s_l, i + 1)
                        link(dve.tensor_tensor(lt, m.bank[:, i % 2, :].rearrange("p (j q) -> p j q", j=4),
                                               bc(nacum[:, hs:hs + 4], 128), ALU.add))
                        dve.tensor_scalar(lt, lt, 0.0, None, ALU.min).then_inc(s_ld1, 1)
                        dve.wait_ge(s_lx, i + 1)
                        if i >= 2:
                            dve.wait_ge(s_y, (i - 2) // 2 + 1)
                        dve.tensor_tensor(mm, lt, bmid(sc[:, n, :], 4), ALU.mult).then_inc(s_m, 1)
                    if n >= 2:
                        dve.wait_ge(s_sd, n - 1)
                    dve.tensor_tensor(xdd[:, g, :].rearrange("p (h q) -> p h q", h=8),
                                      xdt[:, c, g * 512:(g + 1) * 512].rearrange("p (h q) -> p h q", h=8),
                                      bc(dec[:, c * AH + 8 * g:c * AH + 8 * g + 8], AP_), ALU.mult).then_inc(s_xdd, 1)
                    yv = y[:, g, :].rearrange("p (h q) -> p h q", h=8)
                    if n >= 2:
                        dve.wait_ge(s_yt, 2 * c)
                    dve.wait_ge(s_yo, n + 1)
                    link(dve.tensor_tensor(yv, m.bank[:, 4 + n % 2, :].rearrange("p (h q) -> p h q", h=8),
                                           bc(eac[:, c * AH + 8 * g:c * AH + 8 * g + 8], AP_), ALU.mult))
                    dve.wait_ge(s_y, n + 1)
                    link(dve.tensor_tensor(y[:, g, :], y[:, g, :], m.bank[:, 2 + n % 2, :], ALU.add))
                    jk = junk[:, g * 512:(g + 1) * 512]
                    link(dve.tensor_tensor(jk.rearrange("p (h q) -> p h q", h=8),
                                           xtok[:, c, g * 512:(g + 1) * 512].rearrange("p (h q) -> p h q", h=8),
                                           bc(dsk[:, 8 * g:8 * g + 8], AP_), ALU.mult))
                    link(dve.tensor_tensor(y[:, g, :], y[:, g, :], jk, ALU.add))
                    dve.wait_ge(s_z, c + 1)
                    link(dve.tensor_tensor(y[:, g, :], y[:, g, :], z[:, c, g * 512:(g + 1) * 512], ALU.mult))
                    link(dve.tensor_tensor(jk, y[:, g, :], y[:, g, :], ALU.mult))
                    link(dve.tensor_reduce(rs[:, g:g + 1], jk, AX.X, ALU.add))
                    dve.tensor_scalar(rs[:, g:g + 1], rs[:, g:g + 1], 1.0 / 512, EPS, ALU.mult, ALU.add).then_inc(s_var, 1)
                    dve.wait_ge(s_rstd, n + 1)
                    last = dve.scalar_tensor_tensor(y[:, g, :], y[:, g, :], rs[:, g:g + 1], gn[:, g * 512:(g + 1) * 512],
                                                    ALU.mult, ALU.mult)
                    last.then_inc(s_yn, 1)
                    dve.wait_ge(s_yn, n + 1)
                    dve.wait_ge(s_sd, n + 1)
                    sv = stT[:, g, :].rearrange("p (h q) -> p h q", h=8)
                    link(dve.tensor_tensor(sv, sv, bc(etot[:, c * AH + 8 * g:c * AH + 8 * g + 8], AP_), ALU.mult))
                    dve.tensor_tensor(stT[:, g, :], stT[:, g, :], m.bank[:, 6, :], ALU.add).then_inc(s_sn, 1)
                    dve.wait_ge(s_sn, n + 1)

        @block.scalar
        def _(act):
            link = linker(act, s_a)
            for i in range(AM):
                act.wait_ge(s_conv, i + 1)
                act.activation(xc[:, i, :], xc[:, i, :], ACT.Silu).then_inc(s_silu, 1)
            for c in range(NC):
                act.activation(z[:, c, :], z[:, c, :], ACT.Silu).then_inc(s_z, 1)
            act.wait_ge(s_dt1, 1)
            link(act.activation(tmp64, tmp64, ACT.Exp, scale=-1.0))
            link(act.activation(tmp64, tmp64, ACT.Ln, bias=1.0))
            act.wait_ge(s_ld, 16 * 8)
            act.activation(aneg, aneg, ACT.Exp).then_inc(s_dt2, 1)
            act.wait_ge(s_cum2, 1)
            link(act.activation(eac, nacum, ACT.Exp, scale=-1.0))
            link(act.activation(dec, dec, ACT.Exp))
            act.activation(etot, etot, ACT.Exp).then_inc(s_pr, 1)
            for i in range(4 * NC):
                act.wait_ge(s_ld1, i + 1)
                act.activation(mt[:, i % 2, :], mt[:, i % 2, :], ACT.Exp).then_inc(s_lx, 1)
                if i % 2 == 1:
                    act.wait_ge(s_var, i // 2 + 1)
                    r = rs[:, i // 2 % 2:i // 2 % 2 + 1]
                    link(act.activation(r, r, ACT.Ln))
                    act.activation(r, r, ACT.Exp, scale=-0.5).then_inc(s_rstd, 1)
                if i % 4 == 3:
                    c = i // 4
                    for h in range(2):
                        act.wait_ge(s_yt, 2 * c + h + 1)
                        act.copy(m.yaT[:, 4 * h:4 * h + 4, c * 128:(c + 1) * 128],
                                 m.bank[:, 7, :].rearrange("p (j q) -> p j q", j=4)).then_inc(s_ye, 1)

    with ExitStack() as ctx:
        st = Stage(nc, ctx, "as")
        S = m.arena[:, 6 * SLOT:8 * SLOT].rearrange("p (b m n) -> p b m n", b=TS, m=8)
        Sm = m.arena[:, 6 * SLOT:8 * SLOT].rearrange("p (b m n) -> p (b m) n", b=TS, m=8)
        tmp = m.slot(5)
        bcs = m.ybT[:].rearrange("p k q -> p (k q)")[:, 0:4096].rearrange("p (i b n) -> p i b n", i=4, b=TS)
        exps = m.slot(2)[0:AH, 0:1024]
        so = m.slot(2)[:, 1024:2048]
        g64 = m.slot(2)[:, 2048:2112].rearrange("p (m b) -> p m b", m=8)
        gr = m.slot(2)[:, 2112:2128].rearrange("p (g b) -> p g b", g=AG)
        s_ld, s_st, s_v, s_a, s_c, s_xs, s_e, s_dd, s_ex, s_exe, s_dg, s_bb, s_be, s_sn, s_sq, s_sr, s_tr, s_so, s_out, s_d2, s_sp = (
            st.sem(n) for n in ("ld", "st", "v", "a", "c", "xs", "e", "dd", "ex", "exe", "dg", "bb", "be", "sn", "sq", "sr",
                                "tr", "so", "out", "d2", "sp"))
        s_var, s_rstd = st.sem("var"), st.sem("rstd")
        block = ctx.enter_context(nc.Block())

        @block.sync
        def _(sp):
            sp.dma_start(exps, t["c_headexp"]).then_inc(s_ld, 16)
            for i, n in enumerate(("dt_bias", "a_log", "d_skip")):
                c = (17, 18, 16)[i]
                sp.dma_start(dsm[:, c:c + 1], t[n][0].rearrange("(h i) -> h i", i=1)).then_inc(s_ld, 16)
            for b in range(TS):
                sp.dma_start(S[:, b], t["state_ssm"][0, b].rearrange("(m h) q n -> (h q) m n", h=2)).then_inc(s_st, 16)
            sp.wait_ge(s_so, 1)
            sp.dma_start(o["ssm_p"][0, 0].rearrange("(m h) q n -> (h q) m n", h=2), so.rearrange("p (m n) -> p m n", m=8))\
                .then_inc(s_out, 16)
            for b in range(TS):
                sp.wait_ge(s_sn, b // 4 + 1)
                sp.dma_start(o["ssm_s"][0, b].rearrange("(m h) q n -> (h q) m n", h=2), S[:, b]).then_inc(s_out, 16)
            sp.wait_ge(s_out, 16 * 9)

        @block.tensor
        def _(pe):
            for i in range(8):
                last = pe.transpose(m.bank[:, i // 4, (i % 4) * 128:(i % 4 + 1) * 128],
                                    stT[:, i // 4, (i % 4) * 128:(i % 4 + 1) * 128], m.ident[:])
            last.then_inc(s_tr, 1)
            pe.wait_ge(s_dd, 1)
            for i in range(8):
                last = pe.matmul(m.bank[:, 2, 17 * i:17 * i + 17], exps[:, i * 128:(i + 1) * 128], dsm[:, 0:17], start=True, stop=True)
            last.then_inc(s_ex, 1)
            pe.wait_ge(s_dg, 4)
            pe.wait_ge(s_so, 1)
            pe.wait_ge(s_exe, 1)
            for i in range(8):
                last = pe.matmul(m.bank[:, i, :], m.ones[:], tmp[:, i * 512:(i + 1) * 512], start=True, stop=True)
            last.then_inc(s_bb, 1)
            pe.wait_ge(s_sq, 1)
            pe.matmul(m.bank[:, 0, 0:64], m.ones[:], g64.rearrange("p m b -> p (m b)"), start=True, stop=True).then_inc(s_sr, 1)

        @block.vector
        def _(dve):
            link = linker(dve, s_v)
            dve.wait_ge(s_tr, 1)
            dve.tensor_copy(so.rearrange("p (b q) -> p b q", b=2), m.bank[:, 0:2, :]).then_inc(s_so, 1)
            dve.wait_ge(s_ld, 64)
            link(dve.tensor_tensor(xcs, raws, bc(par[:, :, 27], TS), ALU.mult))
            link(dve.tensor_tensor(xcs, xcs, bc(par[:, :, 28], TS), ALU.add))
            for j in range(3):
                link(dve.tensor_tensor(tmps, par[:, :, j:24:3], bc(par[:, :, 24 + j], TS), ALU.mult))
                link(dve.tensor_tensor(xcs, xcs, tmps, ALU.add))
            dve.tensor_scalar(dsm[:, 0:8], dts_raw, dsm[:, 17:18], None, ALU.add).then_inc(s_c, 1)
            dve.wait_ge(s_c, 1)
            link(dve.scalar_tensor_tensor(dsm[:, 24:32], dsm[:, 0:8], -1.0, dsm[:, 0:8], ALU.mult, ALU.max))
            dve.tensor_scalar(dsm[:, 0:8], dsm[:, 0:8], 0.0, None, ALU.max).then_inc(s_c, 1)
            dve.wait_ge(s_e, 1)
            link(dve.tensor_tensor(dsm[:, 0:8], dsm[:, 0:8], dsm[:, 24:32], ALU.add))
            dve.tensor_scalar(dsm[:, 8:16], dsm[:, 0:8], dsm[:, 18:19], -1.0, ALU.mult, ALU.mult).then_inc(s_d2, 1)
            dve.wait_ge(s_xs, 1)
            for i in range(4):
                dve.tensor_tensor(tmp[:, i * 1024:(i + 1) * 1024].rearrange("p (b n) -> p b n", b=TS), bmid(m.ident[:], TS),
                                  bc(xcs[:, 8 + i, :], 128), ALU.mult).then_inc(s_dg, 1)
            dve.wait_ge(s_ex, 1)
            dve.tensor_copy(ex, m.bank[:, 2, 0:136].rearrange("p (m q) -> p m q", m=8)).then_inc(s_exe, 1)
            dve.wait_ge(s_exe, 1)
            link(dve.tensor_tensor(us, xcs[:, 0:8, :], ex[:, :, 0:8], ALU.mult))
            dve.wait_ge(s_bb, 1)
            for i in range(4):
                dve.tensor_copy(bcs[:, i].rearrange("p (a b) n -> p a (b n)", a=2), m.bank[:, 2 * i:2 * i + 2, :]).then_inc(s_be, 1)
            dve.wait_ge(s_be, 4)
            dve.wait_ge(s_st, 16 * TS)
            for hb in range(2):
                bs = slice(4 * hb, 4 * hb + 4)
                tv = tmp.rearrange("p (b m n) -> p b m n", b=4, m=8)
                link(dve.tensor_tensor(S[:, bs], S[:, bs], bc(ex[:, :, 8 + 4 * hb:12 + 4 * hb].rearrange("p m b -> p b m"), 128), ALU.mult))
                for b in range(4):
                    for g in range(AG):
                        gm = slice(4 * g, 4 * g + 4)
                        dve.tensor_tensor(tv[:, b, gm, :], bc(us[:, gm, 4 * hb + b], 128), bmid(bcs[:, g, 4 * hb + b, :], 4), ALU.mult)\
                            .then_inc(s_sp, 1)
                dve.wait_ge(s_sp, 16 * hb + 8)
                last = dve.tensor_tensor(S[:, bs], S[:, bs], tv, ALU.add)
                last.then_inc(s_sn, 1)
                dve.wait_ge(s_sn, hb + 1)
                for b in range(4):
                    for g in range(AG):
                        gm = slice(4 * g, 4 * g + 4)
                        dve.tensor_tensor(tv[:, b, gm, :], S[:, 4 * hb + b, gm, :], bmid(bcs[:, 2 + g, 4 * hb + b, :], 4), ALU.mult)\
                            .then_inc(s_sp, 1)
                dve.wait_ge(s_sp, 16 * hb + 16)
                link(dve.tensor_reduce(ys[:, :, bs].rearrange("p m b -> p b m"), tv, AX.X, ALU.add))
            link(dve.tensor_tensor(us, xcs[:, 0:8, :], bc(ex[:, :, 16], TS), ALU.mult))
            link(dve.tensor_tensor(ys, ys, us, ALU.add))
            link(dve.tensor_tensor(ys, ys, zs, ALU.mult))
            dve.tensor_tensor(g64, ys, ys, ALU.mult).then_inc(s_sq, 1)
            dve.wait_ge(s_sr, 1)
            link(dve.tensor_reduce(gr, m.bank[:, 0, 0:64].rearrange("p (g m b) -> p g b m", g=AG, m=4), AX.X, ALU.add))
            dve.tensor_scalar(gr, gr, 1.0 / 512, EPS, ALU.mult, ALU.add).then_inc(s_var, 1)
            dve.wait_ge(s_rstd, 1)
            for g in range(AG):
                gm = slice(4 * g, 4 * g + 4)
                link(dve.tensor_tensor(ys[:, gm, :], ys[:, gm, :], bmid(gr[:, g, :], 4), ALU.mult))
            link(dve.tensor_tensor(m.yaT[:, :, TP:T], ys, bc(ngT, TS), ALU.mult))

        @block.scalar
        def _(act):
            link = linker(act, s_a)
            act.wait_ge(s_c, 1)
            link(act.activation(zs, zs, ACT.Silu))
            act.activation(xcs, xcs, ACT.Silu).then_inc(s_xs, 1)
            act.wait_ge(s_c, 2)
            link(act.activation(dsm[:, 24:32], dsm[:, 24:32], ACT.Exp, scale=-1.0))
            link(act.activation(dsm[:, 24:32], dsm[:, 24:32], ACT.Ln, bias=1.0))
            act.activation(dsm[:, 18:19], dsm[:, 18:19], ACT.Exp).then_inc(s_e, 1)
            act.wait_ge(s_d2, 1)
            act.activation(dsm[:, 8:16], dsm[:, 8:16], ACT.Exp).then_inc(s_dd, 1)
            act.wait_ge(s_var, 1)
            link(act.activation(gr, gr, ACT.Ln))
            act.activation(gr, gr, ACT.Exp, scale=-0.5).then_inc(s_rstd, 1)


def mixer_b(nc, m, t, o):
    q, v, g = m.slot(0), m.slot(2).rearrange("p (c d) -> p c d", c=NC), m.slot(3).rearrange("p (c d) -> p c d", c=NC)
    f = m.slot(1)
    qs = m.work[:, 0:64].rearrange("p (h b) -> p h b", h=BH)
    fs = m.work[:, 64:128].rearrange("p (h b) -> p h b", h=BH)
    gs = m.work[:, 128:192].rearrange("p (h b) -> p h b", h=BH)
    vs = m.work[0:TS, 192:1216]
    lb = m.work[:, 1216:1224]
    oml = m.work[:, 1224:1232]
    ng = m.work[:, 1232:1233]
    chunks = [(c0 + 512 * i, 512) for c0 in (BQ0, BF0, BI0, BG0) for i in range(2)]
    units = []
    for w, (dp, ds) in enumerate(((q, qs), (f, fs))):
        for i in range(2):
            for j in range(4):
                h = 4 * i + j
                units += chan_units(2 * w + i, 128 * j, dp[:, h * 512:(h + 1) * 512], ds[:, h, :])
    for i in range(2):
        units += tok_units(4 + i, 0, 512, lambda k, i=i: v[:, k, 512 * i:512 * i + 512])
        units.append((4 + i, "tok", 0, 512, TP, T, [(vs[:, 512 * i:512 * i + 512], TS, 0, 512)]))
    for i in range(2):
        units += tok_units(6 + i, 0, 512, lambda k, i=i: g[:, k, 512 * i:512 * i + 512])
        for j in range(4):
            units.append((6 + i, "chan", 128 * j, 128, TP, T, [(gs[:, 4 * i + j, :], 128, 0, TS)]))
    project(nc, m, t, "pb", chunks, units, [m.slot(i) for i in (4, 5, 6, 7)])

    KSC = BK ** -0.5
    with ExitStack() as ctx:
        st = Stage(nc, ctx, "b")
        W, b, k, kW, qW = m.slot(1), m.slot(4), m.slot(5), m.slot(6), m.slot(7)
        att = m.slot(8).rearrange("p (i q) -> p i q", i=BH * NC)
        gnr = m.slot(6)[:, 0:128]
        reset = m.slot(8)[:, 0:512]
        lbr = m.slot(8)[0:8, 512:640]
        masks = m.ycT[:].rearrange("p k q -> p (k q)")[:, 0:896].bitcast(U32).rearrange("p (l q) -> p l q", l=len(LEVELS))
        kdt = m.slot(0).rearrange("p (i q) -> p i q", i=BH * NC)
        S = m.slot(1)[:, 0:1024]
        sq = m.slot(1)[:, 1024:2048].rearrange("p (i q) -> p i q", i=2)
        y = m.slot(1)[:, 2048:3072].rearrange("p (i q) -> p i q", i=2)
        ebl = m.work[:, 1240:1272]
        rs = m.work[:, 1272:1280].rearrange("p (i h) -> p i h", i=2)
        e8 = m.work[:, 1280:1288]
        (s_ld, s_mk, s_lt, s_v, s_a, s_p, s_lb, s_le, s_sig, s_F, s_ln, s_k, s_z, s_g, s_sub, s_exp, s_mul, s_at, s_pr, s_b0) = (
            st.sem(n) for n in ("ld", "mk", "lt", "v", "a", "p", "lb", "le", "sig", "F", "ln", "k", "z", "g", "sub", "exp",
                                "mul", "at", "pr", "b0"))
        (s_e2, s_q2, s_kt, s_ke, s_o, s_S, s_Sd, s_sq, s_var, s_rstd, s_y, s_yt, s_ye, s_oe) = (
            st.sem(n) for n in ("e2", "q2", "kt", "ke", "o", "S", "Sd", "sq", "var", "rstd", "y", "yt", "ye", "oe"))
        nl = len(LEVELS)
        steps = [(hg, lv) for hg in range(2) for lv in range(nl)]
        block = ctx.enter_context(nc.Block())

        def transposes(pe, n):
            pe.wait_ge(s_y, n + 1)
            if n >= 2:
                pe.wait_ge(s_ye, n - 1)
            for j in range(4):
                last = pe.transpose(m.bank[:, 4 + n % 2, j * 128:(j + 1) * 128], y[:, n % 2, j * 128:(j + 1) * 128], m.ident[:])
            last.then_inc(s_yt, 1)

        def store_y(act, n):
            c, hg = divmod(n, 2)
            act.wait_ge(s_yt, n + 1)
            act.copy(m.ybT[:, 4 * hg:4 * hg + 4, c * 128:(c + 1) * 128],
                     m.bank[:, 4 + n % 2, :].rearrange("p (j q) -> p j q", j=4)).then_inc(s_ye, 1)

        def halves(x, z):
            v3 = x.rearrange("p (n z) -> p n z", z=z)
            return v3[:, :, 0:z // 2], v3[:, :, z // 2:z]

        @block.sync
        def _(sp):
            sp.dma_start(masks, t["c_masks"]).then_inc(s_mk, 16)
            sp.dma_start(reset, t["c_reset"][0].partition_broadcast(128)).then_inc(s_ld, 16)
            sp.dma_start(lbr, t["hgrn_lb"][0].rearrange("(h p) -> h p", p=128)).then_inc(s_ld, 16)
            sp.dma_start(gnr, t["hgrn_norm_g"][0].partition_broadcast(128)).then_inc(s_ld, 16)
            sp.dma_start(ng, t["hgrn_norm_g"][0].rearrange("(p i) -> p i", i=1)).then_inc(s_ld, 16)

        @block.gpsimd
        def _(pool):
            pool.wait_ge(s_g, 1)
            pool.wait_ge(s_ld, 64)
            pool.tensor_tensor(m.slot(3).rearrange("p (i q) -> p i q", q=128), m.slot(3).rearrange("p (i q) -> p i q", q=128),
                               bmid(gnr, 32), ALU.mult).then_inc(s_p, 1)
            pool.wait_ge(s_p, 1)
            pool.memset(kW, 0.0).then_inc(s_z, 1)
            pool.memset(qW, 0.0).then_inc(s_z, 1)

        @block.tensor
        def _(pe):
            pe.wait_ge(s_ld, 64)
            pe.transpose(m.bank[:, 7, 0:8], lbr, m.ident[0:8, 0:8]).then_inc(s_lt, 1)
            pe.wait_ge(s_k, 1)
            for hg in range(2):
                for i in range(16):
                    c0 = hg * 2048 + i * 128
                    last = pe.matmul(m.bank[:, 4 * hg + i // 4, (i % 4) * 128:(i % 4 + 1) * 128], k[:, c0:c0 + 128], q[:, c0:c0 + 128],
                                     start=True, stop=True)
                last.then_inc(s_at, 1)
            for n, (hg, lv) in enumerate(steps):
                pe.wait_ge(s_mul, n + 1)
                pe.wait_ge(s_pr, n + 1)
                for i in range(16):
                    c0 = (n % 2) * 2048 + i * 128
                    last = pe.matmul(m.bank[:, 4 * (n % 2) + i // 4, (i % 4) * 128:(i % 4 + 1) * 128], kW[:, c0:c0 + 128],
                                     qW[:, c0:c0 + 128], start=True, stop=True)
                last.then_inc(s_at, 1)
            pe.wait_ge(s_q2, 2)
            pe.wait_ge(s_pr, 2 * nl + 2)
            for n in range(8):
                for j in range(4):
                    i = 4 * n + j
                    last = pe.transpose(m.bank[:, n, j * 128:(j + 1) * 128], kW[:, i * 128:(i + 1) * 128], m.ident[:])
                last.then_inc(s_kt, 1)
            pe.wait_ge(s_ke, 8)
            for c in range(NC):
                for hg in range(2):
                    n = 2 * c + hg
                    if n >= 2:
                        pe.wait_ge(s_y, n - 1)
                    if c > 0:
                        pe.wait_ge(s_Sd, n - 1)
                    for j in range(4):
                        h = 4 * hg + j
                        i = h * NC + c
                        out = m.bank[:, n % 2, j * 128:(j + 1) * 128]
                        vv = v[:, c, h * 128:(h + 1) * 128]
                        last = pe.matmul(out, att[:, i, :], vv, start=True, stop=(c == 0))
                        if c > 0:
                            last = pe.matmul(out, qW[:, i * 128:(i + 1) * 128], S[:, h * 128:(h + 1) * 128], start=False, stop=True)
                    last.then_inc(s_o, 1)
                    for j in range(4):
                        h = 4 * hg + j
                        last = pe.matmul(m.bank[:, 2 + n % 2, j * 128:(j + 1) * 128], kdt[:, h * NC + c, :], v[:, c, h * 128:(h + 1) * 128],
                                         start=True, stop=True)
                    last.then_inc(s_S, 1)
                    if n >= 1:
                        transposes(pe, n - 1)
            transposes(pe, 2 * NC - 1)

        @block.vector
        def _(dve):
            link = linker(dve, s_v)
            dve.wait_ge(s_lt, 1)
            link(dve.tensor_copy(lb, m.bank[:, 7, 0:8]))
            dve.tensor_tensor(e8, lb, lb, ALU.subtract).then_inc(s_lb, 1)
            dve.wait_ge(s_le, 1)
            link(dve.reciprocal(oml, e8))
            link(dve.tensor_tensor(e8, e8, oml, ALU.mult))
            link(dve.tensor_tensor(lb, e8, e8, ALU.subtract))
            link(dve.tensor_scalar(oml, lb, -1.0, 1.0, ALU.mult, ALU.add))
            dve.wait_ge(s_sig, 1)
            for h in range(BH):
                c = slice(h * 512, (h + 1) * 512)
                link(dve.tensor_scalar(f[:, c], f[:, c], oml[:, h:h + 1], lb[:, h:h + 1], ALU.mult, ALU.add))
            dve.tensor_scalar(f, f, 1e-30, None, ALU.max).then_inc(s_F, 1)
            dve.wait_ge(s_sig, 2)
            for h in range(BH):
                c = slice(h * 512, (h + 1) * 512)
                ins = dve.tensor_scalar(k[:, c], k[:, c], oml[:, h:h + 1], None, ALU.mult)
            ins.then_inc(s_k, 1)
            dve.wait_ge(s_k, 1)
            dve.wait_ge(s_ln, 1)
            dve.wait_ge(s_ld, 64)
            for h in range(BH):
                c = slice(h * 512, (h + 1) * 512)
                ins = dve.tensor_tensor_scan(b[:, c], reset, f[:, c], 0.0, ALU.mult, ALU.add)
            ins.then_inc(s_b0, 1)
            dve.wait_ge(s_b0, 1)

            def sub(n):
                hg, lv = steps[n]
                z = LEVELS[lv]
                bl, br = halves(b[:, hg * 2048:(hg + 1) * 2048], z)
                wl, wr = halves(W[:, (n % 2) * 2048:(n % 2 + 1) * 2048], z)
                r = bl[:, :, z // 2 - 1:z // 2].broadcast_to([128, 2048 // z, z // 2])
                dve.tensor_tensor(wl, r, bl, ALU.subtract)
                dve.tensor_tensor(wr, br, r, ALU.subtract).then_inc(s_sub, 1)

            sub(0)
            for hg in range(2):
                dve.wait_ge(s_at, hg + 1)
                dve.scalar_tensor_tensor(att[:, hg * 16:(hg + 1) * 16, :],
                                         m.bank[:, 4 * hg:4 * hg + 4, :].rearrange("p i (j q) -> p (i j) q", j=4), KSC,
                                         bmid(m.ident[:], 16), ALU.mult, ALU.mult).then_inc(s_pr, 1)
            dve.wait_ge(s_mk, 16)
            dve.wait_ge(s_z, 2)

            def choose(n):
                hg, lv = steps[n]
                dve.wait_ge(s_at, n + 3)
                dve.wait_ge(s_pr, n + 2)
                for j in range(4):
                    ins = dve.copy_predicated(att[:, hg * 16 + 4 * j:hg * 16 + 4 * j + 4, :], bmid(masks[:, lv, :], 4),
                                              m.bank[:, 4 * (n % 2) + j, :].rearrange("p (j q) -> p j q", j=4))
                ins.then_inc(s_pr, 1)

            for n, (hg, lv) in enumerate(steps):
                if n + 1 < len(steps):
                    sub(n + 1)
                dve.wait_ge(s_exp, n + 1)
                z = LEVELS[lv]
                cs, cw = slice(hg * 2048, (hg + 1) * 2048), slice((n % 2) * 2048, (n % 2 + 1) * 2048)
                wl, wr = halves(W[:, cw], z)
                dve.tensor_tensor(halves(kW[:, cw], z)[0], halves(k[:, cs], z)[0], wl, ALU.mult)
                dve.scalar_tensor_tensor(halves(qW[:, cw], z)[1], halves(q[:, cs], z)[1], KSC, wr, ALU.mult, ALU.mult)\
                    .then_inc(s_mul, 1)
                dve.wait_ge(s_mul, n + 1)
                if n >= 1:
                    choose(n - 1)
            choose(len(steps) - 1)
            b3 = b.rearrange("p (i q) -> p i q", q=128)
            bend = b3[:, :, 127:128].broadcast_to([128, 32, 128])
            dve.wait_ge(s_e2, 1)
            dve.scalar_tensor_tensor(qW, q, KSC, W, ALU.mult, ALU.mult).then_inc(s_q2, 1)
            dve.wait_ge(s_q2, 1)
            dve.tensor_tensor(W.rearrange("p (i q) -> p i q", q=128), bend, b3, ALU.subtract).then_inc(s_sub, 1)
            dve.wait_ge(s_e2, 2)
            dve.tensor_tensor(kW, k, W, ALU.mult).then_inc(s_q2, 1)
            dve.wait_ge(s_q2, 2)
            link(dve.memset(S, 0.0))
            for n in range(8):
                dve.wait_ge(s_kt, n + 1)
                dve.tensor_copy(kdt[:, 4 * n:4 * n + 4, :], m.bank[:, n, :].rearrange("p (j q) -> p j q", j=4)).then_inc(s_ke, 1)
            dve.wait_ge(s_e2, 3)
            for n in range(2 * NC):
                c, hg = divmod(n, 2)
                dve.wait_ge(s_S, n + 1)
                for j in range(4):
                    h = 4 * hg + j
                    Sh = S[:, h * 128:(h + 1) * 128]
                    ins = dve.scalar_tensor_tensor(Sh, Sh, ebl[:, h * NC + c:h * NC + c + 1], m.bank[:, 2 + n % 2, j * 128:(j + 1) * 128],
                                                   ALU.mult, ALU.add)
                ins.then_inc(s_Sd, 1)
                dve.wait_ge(s_Sd, n + 1)
                dve.wait_ge(s_sq, n + 1)
                link(dve.tensor_reduce(rs[:, n % 2, :], sq[:, n % 2, :].rearrange("p (j q) -> p j q", j=4), AX.X, ALU.add))
                dve.tensor_scalar(rs[:, n % 2, :], rs[:, n % 2, :], 1.0 / 128, EPS, ALU.mult, ALU.add).then_inc(s_var, 1)
                dve.wait_ge(s_rstd, n + 1)
                if n >= 2:
                    dve.wait_ge(s_yt, n - 1)
                link(dve.tensor_tensor(y[:, n % 2, :].rearrange("p (j q) -> p j q", j=4),
                                       m.bank[:, n % 2, :].rearrange("p (j q) -> p j q", j=4), bc(rs[:, n % 2, :], 128), ALU.mult))
                if n == 0:
                    dve.wait_ge(s_p, 1)
                dve.tensor_tensor(y[:, n % 2, :], y[:, n % 2, :], g[:, c, hg * 512:(hg + 1) * 512], ALU.mult).then_inc(s_y, 1)

        @block.scalar
        def _(act):
            link = linker(act, s_a)
            act.activation(m.slot(3), m.slot(3), ACT.Silu).then_inc(s_g, 1)
            link(act.activation(q, q, ACT.Silu))
            link(act.activation(k, f, ACT.Sigmoid, scale=-1.0))
            act.activation(f, f, ACT.Sigmoid).then_inc(s_sig, 2)
            act.wait_ge(s_lb, 1)
            act.activation(e8, e8, ACT.Exp).then_inc(s_le, 1)
            act.wait_ge(s_F, 1)
            link(act.activation(f, f, ACT.Sqrt))
            act.activation(f, f, ACT.Ln).then_inc(s_ln, 1)
            for n in range(len(steps)):
                act.wait_ge(s_sub, n + 1)
                cw = slice((n % 2) * 2048, (n % 2 + 1) * 2048)
                act.activation(W[:, cw], W[:, cw], ACT.Exp, scale=2.0).then_inc(s_exp, 1)
            act.wait_ge(s_mul, len(steps))
            act.activation(W, b, ACT.Exp, scale=2.0).then_inc(s_e2, 1)
            act.wait_ge(s_sub, len(steps) + 1)
            act.activation(W, W, ACT.Exp, scale=2.0).then_inc(s_e2, 1)
            act.activation(ebl, b.rearrange("p (i q) -> p i q", q=128)[:, :, 127], ACT.Exp, scale=2.0).then_inc(s_e2, 1)
            act.wait_ge(s_q2, 2)
            for n in range(2 * NC):
                c, hg = divmod(n, 2)
                act.wait_ge(s_o, n + 1)
                act.activation(sq[:, n % 2, :], m.bank[:, n % 2, :], ACT.Square).then_inc(s_sq, 1)
                act.wait_ge(s_var, n + 1)
                link(act.activation(rs[:, n % 2, :], rs[:, n % 2, :], ACT.Ln))
                act.activation(rs[:, n % 2, :], rs[:, n % 2, :], ACT.Exp, scale=-0.5).then_inc(s_rstd, 1)
                if n >= 1:
                    store_y(act, n - 1)
            store_y(act, 2 * NC - 1)

    with ExitStack() as ctx:
        st = Stage(nc, ctx, "bs")
        Ss = m.arena[:, 6 * SLOT:8 * SLOT].rearrange("p (b h v) -> p b h v", b=TS, h=BH)
        tmp = m.slot(5).rearrange("p (i h v) -> p i h v", i=8, h=4)
        ks = m.work[:, 1300:1364].rearrange("p (h b) -> p h b", h=BH)
        sqs = m.work[:, 1364:1428]
        r64 = m.work[:, 1428:1492]
        y64 = m.work[:, 1492:1556]
        (s_st, s_out, s_v, s_a, s_f, s_g, s_vb, s_t, s_o, s_sq, s_sr, s_var, s_rstd, s_up) = (
            st.sem(n) for n in ("st", "out", "v", "a", "f", "g", "vb", "t", "o", "sq", "sr", "var", "rstd", "up"))
        block = ctx.enter_context(nc.Block())

        @block.sync
        def _(sp):
            for bb in range(TS):
                sp.dma_start(Ss[:, bb], t["state_hgrn"][0, bb].rearrange("h k v -> k h v")).then_inc(s_st, 16)
            sp.dma_start(o["hgrn_p"][0, 0].rearrange("h k v -> k h v"), S.rearrange("p (h v) -> p h v", h=BH)).then_inc(s_out, 16)
            for bb in range(TS):
                sp.wait_ge(s_up, 2 * bb + 2)
                sp.dma_start(o["hgrn_s"][0, bb].rearrange("h k v -> k h v"), Ss[:, bb]).then_inc(s_out, 16)
            sp.wait_ge(s_out, 16 * (TS + 1))

        @block.tensor
        def _(pe):
            for n in range(2 * TS):
                bb, hg = divmod(n, 2)
                if n >= 8:
                    pe.wait_ge(s_t, n - 7)
                pe.matmul(m.bank[:, n % 8, :], m.ident[0:TS, bb:bb + 1].broadcast_to([TS, 128]), vs[:, hg * 512:(hg + 1) * 512],
                          start=True, stop=True).then_inc(s_vb, 1)
            pe.wait_ge(s_t, 2 * TS)
            for bb in range(TS):
                pe.wait_ge(s_up, 2 * bb + 2)
                for h in range(BH):
                    last = pe.matmul(m.bank[:, 0, h * TS + bb:h * TS + bb + 1], Ss[:, bb, h, :], qs[:, h, bb:bb + 1], start=True, stop=True)
            last.then_inc(s_o, 1)
            pe.wait_ge(s_sq, 1)
            pe.matmul(m.bank[:, 1, 0:64], m.ones[:], sqs, start=True, stop=True).then_inc(s_sr, 1)

        @block.vector
        def _(dve):
            link = linker(dve, s_v)
            dve.wait_ge(s_f, 1)
            link(dve.tensor_tensor(fs, fs, bc(oml, TS), ALU.mult))
            link(dve.tensor_tensor(fs, fs, bc(lb, TS), ALU.add))
            link(dve.tensor_scalar(fs, fs, 1e-30, None, ALU.max))
            link(dve.tensor_tensor(ks, ks, bc(oml, TS), ALU.mult))
            link(dve.tensor_scalar(qs, qs, KSC, None, ALU.mult))
            for bb in range(TS):
                dve.wait_ge(s_st, 16 * TS)
                link(dve.tensor_tensor(Ss[:, bb], Ss[:, bb], bc(fs[:, :, bb], 128), ALU.mult))
                for hg in range(2):
                    n = 2 * bb + hg
                    dve.wait_ge(s_vb, n + 1)
                    dve.tensor_tensor(tmp[:, n % 8], m.bank[:, n % 8, :].rearrange("p (h v) -> p h v", h=4),
                                      bc(ks[:, 4 * hg:4 * hg + 4, bb], 128), ALU.mult).then_inc(s_t, 1)
                dve.wait_ge(s_t, 2 * bb + 2)
                for hg in range(2):
                    n = 2 * bb + hg
                    h4 = slice(4 * hg, 4 * hg + 4)
                    dve.tensor_tensor(Ss[:, bb, h4], Ss[:, bb, h4], tmp[:, n % 8], ALU.add).then_inc(s_up, 1)
                dve.wait_ge(s_up, 2 * bb + 2)
            dve.wait_ge(s_sr, 1)
            dve.tensor_scalar(r64, m.bank[:, 1, 0:64], 1.0 / 128, EPS, ALU.mult, ALU.add).then_inc(s_var, 1)
            dve.wait_ge(s_rstd, 1)
            link(dve.tensor_tensor(y64, m.bank[:, 0, 0:64], r64, ALU.mult))
            link(dve.tensor_scalar(y64, y64, ng, None, ALU.mult))
            link(dve.tensor_tensor(m.ybT[:, :, TP:T], y64.rearrange("p (h b) -> p h b", h=BH), gs, ALU.mult))

        @block.scalar
        def _(act):
            link = linker(act, s_a)
            link(act.activation(gs, gs, ACT.Silu))
            link(act.activation(qs, qs, ACT.Silu))
            link(act.activation(ks, fs, ACT.Sigmoid, scale=-1.0))
            act.activation(fs, fs, ACT.Sigmoid).then_inc(s_f, 1)
            act.wait_ge(s_o, 1)
            act.activation(sqs, m.bank[:, 0, 0:64], ACT.Square).then_inc(s_sq, 1)
            act.wait_ge(s_var, 1)
            link(act.activation(r64, r64, ACT.Ln))
            act.activation(r64, r64, ACT.Exp, scale=-0.5).then_inc(s_rstd, 1)


def mixer_c(nc, m, t, o):
    rel = nc.dram_tensor("rel_rows", [CH, CG, 384], F32).ap()
    og = [nc.dram_tensor(f"group{g}_out", [TP, 260], F32).ap() for g in (1, 2)]
    qT = m.slot(0)[:, 0:6 * TP].rearrange("p (i q) -> p i q", i=6)
    kt = m.slot(1)[:, 0:NC * CW].rearrange("p (c d) -> p c d", c=NC)
    vt = m.slot(2)[:, 0:NC * CW].rearrange("p (c d) -> p c d", c=NC)
    news = m.slot(3)[0:TS, 0:3 * CW]
    DIL = (1, 4, 16)

    def by_class(dst, g):
        return dst if g == 0 else dst.rearrange("p (r i) -> p i r", r=DIL[g])

    chunks = [(c0, n) for b0 in (CQ0, CK0, CV0) for c0, n in ((b0, 512), (b0 + 512, 256))]
    units = []
    for w, (c0, n) in enumerate(chunks[0:2]):
        for j in range(n // 128):
            i = 4 * w + j
            units.append((w, "chan", 128 * j, 128, 0, TP, [(by_class(qT[:, i, :], i // 2), 128, 0, TP)]))
        units.append((w, "tok", 0, n, TP, T, [(news[:, 512 * w:512 * w + n], TS, 0, n)]))
    for w in range(2, 6):
        n, a = chunks[w][1], 512 * (w % 2)
        dst, s0 = ((kt, CW), (vt, 2 * CW))[w // 2 - 1]
        units += tok_units(w, 0, n, lambda c, dst=dst, a=a, n=n: dst[:, c, a:a + n])
        units.append((w, "tok", 0, n, TP, T, [(news[:, s0 + a:s0 + a + n], TS, 0, n)]))
    project(nc, m, t, "pc", chunks, units, [m.slot(i) for i in (4, 5, 6, 7)])

    SCALE = CD ** -0.5
    with ExitStack() as ctx:
        st = Stage(nc, ctx, "c")
        kT = m.slot(4)[:, 0:6 * TP].rearrange("p (i q) -> p i q", i=6)
        v1 = m.slot(5)[:, 0:1024].rearrange("p (r d) -> p r d", r=4)
        v2 = m.slot(5)[:, 1024:2048].rearrange("p (r d) -> p r d", r=4)
        rvs = m.slot(5)[0:CH, 2048:2048 + 3 * 384].rearrange("p (g d) -> p g d", g=CG)
        relb = m.slot(3)[0:32, 2304:2304 + CH]
        relm = m.slot(3)[0:CH, 2320:2704]
        hot = m.slot(3)[0:32, 2704:2704 + 3 * 384].rearrange("p (g d) -> p g d", g=CG)
        bf = m.slot(8)[:, 0:2048]
        bf2 = bf[:, 1536:2048].rearrange("p (h j) -> p h j", h=4)
        flip = m.slot(3)[:, 3900:4028]
        b0 = m.slot(6)[:, 0:1024].rearrange("p (h j) -> p h j", h=4)
        b1 = m.slot(6)[:, 1024:1536].rearrange("p (h j) -> p h j", h=4)
        b2 = m.slot(6)[:, 1536:2048].rearrange("p (h j) -> p h j", h=4)
        mx = m.slot(6)[:, 2048:2056].rearrange("p (i h) -> p i h", i=2)
        den = m.slot(6)[:, 2056:2064].rearrange("p (i h) -> p i h", i=2)
        rden = m.slot(6)[:, 2064:2068]
        lmax = m.slot(6)[:, 2100:2116].rearrange("p (c h) -> p c h", c=NC)
        le = m.slot(6)[:, 2116:2164].rearrange("p (g c h) -> p g c h", g=CG, c=NC)
        lsum = m.slot(6)[:, 2164:2180].rearrange("p (c h) -> p c h", c=NC)
        yc = m.slot(6)[:, 2200:3224].rearrange("p (c d) -> p c d", c=NC)
        os_ = [m.slot(7)[:, 1040 * g:1040 * g + 1040].rearrange("p (c d) -> p c d", c=NC) for g in range(3)]
        back = [None] + [m.slot(4)[:, 1040 * g:1040 * g + 1040].rearrange("p (c d) -> p c d", c=NC) for g in range(2)]
        back[0] = os_[0]
        tmp = m.slot(5)[:, 0:1024].rearrange("p (c d) -> p c d", c=NC)
        P = [m.slot(8)[:, 1024 * i:1024 * i + 1024] for i in range(2)]
        pT = [m.slot(8)[:, 2048 + 1024 * i:3072 + 1024 * i].rearrange("p (i q) -> p i q", i=8) for i in range(2)]
        todo = [(g, n) for g in range(CG) for n in range(NC)]
        width = [256 if g == 0 and n > 0 else 128 for g, n in todo]
        nu = len(todo)
        (s_ld, s_kv, s_vl, s_bm, s_rv, s_rvs, s_rvd, s_bl, s_kt, s_ke, s_ka, s_sc, s_rd, s_sub, s_exp, s_tr, s_pe_, s_pv, s_nm,
         s_v, s_a, s_ln, s_og, s_bk, s_lx, s_le, s_yc, s_yt, s_ye, s_den, s_fl, s_fe) = (st.sem(n) for n in (
             "ld", "kv", "vl", "bm", "rv", "rvs", "rvd", "bl", "kt", "ke", "ka", "sc", "rd", "sub", "exp", "tr", "pe", "pv",
             "nm", "v", "a", "ln", "og", "bk", "lx", "le", "yc", "yt", "ye", "den", "fl", "fe"))
        block = ctx.enter_context(nc.Block())

        @block.sync
        def _(sp):
            sp.dma_start(relb, t["rel_bias"]).then_inc(s_ld, 16)
            sp.dma_start(relm, t["c_relmask"][0].partition_broadcast(CH)).then_inc(s_ld, 16)
            sp.dma_start(hot, t["c_buckets"]).then_inc(s_ld, 16)
            sp.dma_start(flip, t["c_flip"]).then_inc(s_ld, 16)
            for g, name in enumerate(("kv128", "kv512", "kv2048")):
                d = slice(256 * g, 256 * g + 256)
                for i, src in enumerate((kt, vt)):
                    if g == 0:
                        sp.dma_start(o[name + "_p"][0, 0, :, i].rearrange("q h d -> q (h d)"), src[:, 3, d]).then_inc(s_kv, 16)
                    else:
                        sp.dma_start(o[name + "_p"][0, 0, :, i].rearrange("(c q) h d -> q c (h d)", c=NC), src[:, :, d])\
                            .then_inc(s_kv, 16)
                    sp.dma_start(o[name + "_s"][0, :, 0, i].rearrange("b h d -> b (h d)"),
                                 news[:, CW * (i + 1) + 256 * g:CW * (i + 1) + 256 * g + 256]).then_inc(s_kv, 16)
            sp.wait_ge(s_rvs, CG)
            sp.dma_start(rel, rvs).then_inc(s_rvd, 16)
            sp.wait_ge(s_rvd, 16)
            sp.wait_ge(s_bm, 1)

            def toeplitz(h, g, first, rows, cols):
                return bass.AP(rel.tensor, rel[h, g, first:first + 1].offset, [[1, rows], [CG * 384, 4], [1, cols]])
            sp.dma_start(bf[:, 0:1024].rearrange("p (h j) -> p h j", h=4), toeplitz(0, 0, 0, 128, 256)).then_inc(s_bl, 16)
            sp.dma_start(bf[:, 1024:1536].rearrange("p (h j) -> p h j", h=4), toeplitz(4, 1, 128, 128, 128)).then_inc(s_bl, 16)
            for r in range(4):
                sp.dma_start(bf2[32 * r:32 * r + 32, :, 96 - 32 * r:128 - 32 * r], toeplitz(8, 2, 224, 32, 32)).then_inc(s_bl, 16)
            sp.wait_ge(s_kv, 16 * 12)
            sp.dma_start(v1, o["kv512_p"][0, 0, :, 1].rearrange("(i r) h d -> i r (h d)", r=4)).then_inc(s_vl, 16)
            vd = o["kv2048_p"][0, 0, :, 1].rearrange("(i j r) h d -> r i j (h d)", r=4, j=4)
            for r in range(4):
                sp.dma_start(v2[32 * r:32 * r + 32], vd[r]).then_inc(s_vl, 16)
            sp.wait_ge(s_nm, 2 * NC)
            sp.wait_ge(s_ln, 2 * NC)
            sp.dma_start(og[0].rearrange("(i r) d -> i r d", r=4), os_[1]).then_inc(s_og, 16)
            sp.wait_ge(s_nm, 3 * NC)
            sp.wait_ge(s_ln, 3 * NC)
            od = og[1].rearrange("(i j r) d -> r i j d", r=4, j=4)
            for r in range(4):
                sp.dma_start(od[r], os_[2][32 * r:32 * r + 32]).then_inc(s_og, 16)
            sp.wait_ge(s_og, 80)
            for g in range(2):
                sp.dma_start(back[1 + g], og[g].rearrange("(c q) d -> q c d", c=NC)).then_inc(s_bk, 16)
            sp.wait_ge(s_bk, 32)

        @block.gpsimd
        def _(pool):
            pool.memset(bf[:, 1536:2048], NEG).then_inc(s_bm, 1)

        @block.tensor
        def _(pe):
            pe.wait_ge(s_ld, 64)
            for g in range(CG):
                pe.matmul(m.bank[0:CH, 5 + g, 0:384], relb, hot[:, g, :], start=True, stop=True).then_inc(s_rv, 1)
            for i in range(6):
                b = i % 4
                if i >= 4:
                    pe.wait_ge(s_ke, i - 3)
                for c in range(NC):
                    last = pe.transpose(m.bank[:, b, c * 128:(c + 1) * 128], kt[:, c, 128 * i:128 * i + 128], m.ident[:])
                last.then_inc(s_kt, 1)
            pe.wait_ge(s_ke, 6)
            pe.wait_ge(s_rvs, CG)
            pe.wait_ge(s_bl, 16 * 6)
            for i in range(4):
                last = pe.matmul(m.bank[:, 4 + i, :], flip, bf[:, i * 512:(i + 1) * 512], start=True, stop=True)
            last.then_inc(s_fl, 1)
            pe.wait_ge(s_fe, 1)

            def scores(u):
                g, n = todo[u]
                L = width[u]
                if u >= 2:
                    pe.wait_ge(s_rd, u - 1)
                first = (n - 1) * 128 if L == 256 else n * 128
                for h in range(4):
                    i, p0 = 2 * g + h // 2, 64 * (h % 2)
                    out = m.bank[:, 2 * (u % 2) + h % 2, h // 2 * L:h // 2 * L + L]
                    last = pe.matmul(out, qT[p0:p0 + 64, i, n * 128:(n + 1) * 128], kT[p0:p0 + 64, i, first:first + L],
                                     start=True, stop=True)
                last.then_inc(s_sc, 1)

            scores(0)
            for u, (g, n) in enumerate(todo):
                if u + 1 < nu:
                    scores(u + 1)
                nb = width[u] // 128
                pe.wait_ge(s_exp, u + 1)
                for h in range(4):
                    for b in range(nb):
                        i = h * nb + b
                        last = pe.transpose(m.bank[:, 4 + i // 4, (i % 4) * 128:(i % 4 + 1) * 128],
                                            P[u % 2][:, i * 128:(i + 1) * 128], m.ident[:])
                last.then_inc(s_tr, 1)
                pe.wait_ge(s_pe_, u + 1)
                if u >= 2:
                    pe.wait_ge(s_nm, u - 1)
                if u == NC:
                    pe.wait_ge(s_vl, 16 * 5)
                for h in range(4):
                    for b in range(nb):
                        vv = (vt[:, n - nb + 1 + b, :], v1[:, n, :], v2[:, n, :])[g]
                        last = pe.matmul(m.bank[:, 6 + u % 2, h * 64:(h + 1) * 64], pT[u % 2][:, h * nb + b, :],
                                         vv[:, h * 64:(h + 1) * 64], start=(b == 0), stop=(b == nb - 1))
                last.then_inc(s_pv, 1)
            pe.wait_ge(s_yc, 1)
            for c in range(NC):
                for j in range(2):
                    last = pe.transpose(m.bank[:, j, c * 128:(c + 1) * 128], yc[:, c, j * 128:(j + 1) * 128], m.ident[:])
            last.then_inc(s_yt, 1)

        @block.vector
        def _(dve):
            link = linker(dve, s_v)
            dve.wait_ge(s_ld, 64)
            for g in range(CG):
                dve.wait_ge(s_rv, g + 1)
                dve.tensor_tensor(rvs[:, g, :], m.bank[0:CH, 5 + g, 0:384], relm, ALU.add).then_inc(s_rvs, 1)
            for i in range(6):
                dve.wait_ge(s_kt, i + 1)
                src = m.bank[:, i % 4, :]
                if i // 2:
                    src = src.rearrange("p (i r) -> p i r", r=DIL[i // 2])
                dve.tensor_copy(by_class(kT[:, i, :], i // 2), src).then_inc(s_ke, 1)
            dve.wait_ge(s_fl, 1)
            dve.tensor_copy(m.slot(6)[:, 0:2048].rearrange("p (i q) -> p i q", i=4), m.bank[:, 4:8, :]).then_inc(s_fe, 1)
            dve.wait_ge(s_fe, 1)

            def shifted(u):
                g, n = todo[u]
                L = width[u]
                bias = ((b0 if L == 256 else b0[:, :, 128:256]), b1, b2)[g]
                p3 = P[u % 2][:, 0:4 * L].rearrange("p (h j) -> p h j", h=4)
                dve.wait_ge(s_sc, u + 1)
                for b in range(2):
                    ins = dve.scalar_tensor_tensor(p3[:, b::2, :], m.bank[:, 2 * (u % 2) + b, 0:2 * L].rearrange("p (h j) -> p h j", j=L),
                                                   SCALE, bias[:, b::2, :], ALU.mult, ALU.add)
                ins.then_inc(s_rd, 1)
                dve.wait_ge(s_rd, u + 1)
                if u >= 2:
                    dve.wait_ge(s_ln, u - 1)
                link(dve.tensor_reduce(mx[:, u % 2, :], p3, AX.X, ALU.max))
                dve.tensor_tensor(p3, p3, bc(mx[:, u % 2, :], L), ALU.subtract).then_inc(s_sub, 1)
                dve.wait_ge(s_sub, u + 1)

            shifted(0)
            for u, (g, n) in enumerate(todo):
                if u + 1 < nu:
                    shifted(u + 1)
                L = width[u]
                p3 = P[u % 2][:, 0:4 * L].rearrange("p (h j) -> p h j", h=4)
                dve.wait_ge(s_exp, u + 1)
                dve.tensor_reduce(den[:, u % 2, :], p3, AX.X, ALU.add).then_inc(s_den, 1)
                dve.wait_ge(s_den, u + 1)
                link(dve.reciprocal(rden, den[:, u % 2, :]))
                dve.wait_ge(s_pv, u + 1)
                dve.tensor_tensor(os_[g][:, n, 0:256].rearrange("p (h d) -> p h d", h=4),
                                  m.bank[:, 6 + u % 2, 0:256].rearrange("p (h d) -> p h d", h=4), bc(rden, CD), ALU.mult)\
                    .then_inc(s_nm, 1)
                dve.wait_ge(s_nm, u + 1)
                dve.wait_ge(s_lx, u + 1)
                link(dve.tensor_tensor(os_[g][:, n, 256:260], den[:, u % 2, :], mx[:, u % 2, :], ALU.add))
                dve.tensor_copy(rden[:, 0:1], mx[:, u % 2, 0:1]).then_inc(s_ln, 1)
            dve.wait_ge(s_bk, 32)
            ls = [back[g][:, :, 256:260] for g in range(3)]
            link(dve.tensor_tensor(lmax, ls[0], ls[1], ALU.max))
            link(dve.tensor_tensor(lmax, lmax, ls[2], ALU.max))
            for g in range(3):
                ins = dve.tensor_tensor(le[:, g], ls[g], lmax, ALU.subtract)
            ins.then_inc(s_le, 1)
            dve.wait_ge(s_le, 2)
            link(dve.tensor_tensor(lsum, le[:, 0], le[:, 1], ALU.add))
            link(dve.tensor_tensor(lsum, lsum, le[:, 2], ALU.add))
            link(dve.reciprocal(lsum, lsum))
            for g in range(3):
                link(dve.tensor_tensor(le[:, g], le[:, g], lsum, ALU.mult))
                for c in range(NC):
                    ov = back[g][:, c, 0:256].rearrange("p (h d) -> p h d", h=4)
                    dst = (yc if g == 0 else tmp)[:, c, :].rearrange("p (h d) -> p h d", h=4)
                    link(dve.tensor_tensor(dst, ov, bc(le[:, g, c, :], CD), ALU.mult))
                if g:
                    link(dve.tensor_tensor(yc, yc, tmp, ALU.add))
            dve.tensor_copy(rden[:, 0:1], lsum[:, 0, 0:1]).then_inc(s_yc, 1)
            dve.wait_ge(s_yt, 1)
            for j in range(2):
                link(dve.tensor_copy(m.ycT[:, j, 0:TP], m.bank[:, j, :]))

        @block.scalar
        def _(act):
            for u in range(nu):
                L = width[u]
                act.wait_ge(s_sub, u + 1)
                act.activation(P[u % 2][:, 0:4 * L], P[u % 2][:, 0:4 * L], ACT.Exp).then_inc(s_exp, 1)
                act.wait_ge(s_tr, u + 1)
                nb = L // 128
                act.copy(pT[u % 2][:, 0:4 * nb, :], m.bank[:, 4:4 + nb, :].rearrange("p b (i q) -> p (b i) q", q=128)).then_inc(s_pe_, 1)
                act.wait_ge(s_nm, u + 1)
                act.activation(den[:, u % 2, :], den[:, u % 2, :], ACT.Ln).then_inc(s_lx, 1)
            act.wait_ge(s_le, 1)
            act.activation(le, le, ACT.Exp).then_inc(s_le, 1)

    with ExitStack() as ctx:
        st = Stage(nc, ctx, "cs")
        kv = [m.slot(s).rearrange("p (b d) -> p b d", b=TS) for s in (4, 5, 6)]
        prod = [m.slot(7)[:, 0:2048], m.slot(7)[:, 2048:4096], m.slot(8)[:, 0:2048]]
        sT = m.slot(8)[:, 2048:2144].rearrange("p (g b h) -> p g b h", g=CG, b=TS)
        pTs = m.slot(8)[:, 2144:2240].rearrange("p (i b) -> p i b", i=CH)
        sm = m.slot(0)[0:TS, 0:CH * 129].rearrange("p (i j) -> p i j", i=CH)
        bias = m.slot(0)[0:TS, 1600:1600 + CH * 129].rearrange("p (i j) -> p i j", i=CH)
        new = m.slot(1)[0:TS, 0:768]
        sc12 = m.slot(1)[0:TS, 768:780]
        mx12 = m.slot(1)[0:TS, 780:792]
        den12 = m.slot(1)[0:TS, 792:804]
        lse12 = m.slot(1)[0:TS, 804:816]
        m4, d4 = m.slot(1)[0:TS, 816:820], m.slot(1)[0:TS, 820:824]
        rd12 = m.slot(1)[0:TS, 824:836]
        tn = m.slot(1)[0:TS, 836:1092]
        half = m.slot(1)[:, 1100:1116]
        (s_kv, s_b, s_q, s_pr, s_s, s_t, s_sm, s_e, s_p, s_pt, s_pe_, s_w, s_o, s_v, s_a, s_l, s_l2) = (st.sem(n) for n in (
            "kv", "b", "q", "pr", "s", "t", "sm", "e", "p", "pt", "pe", "w", "o", "v", "a", "l", "l2"))
        block = ctx.enter_context(nc.Block())

        @block.sync
        def _(sp):
            for g, name in enumerate(("cache_kv_w128", "cache_kv_w512", "cache_kv_w2048")):
                src = t[name][0].rearrange("b (j r) s h d -> j r b (s h d)", r=DIL[g])[:, 0]
                sp.dma_start(kv[g], src).then_inc(s_kv, 16)
                sp.dma_start(bias[:, 4 * g:4 * g + 4, :], rel[4 * g:4 * g + 4, g, 127:256].partition_broadcast(TS)).then_inc(s_b, 16)

        @block.tensor
        def _(pe):
            for g in range(CG):
                if g >= 2:
                    pe.wait_ge(s_pr, g - 1)
                for b in range(TS):
                    last = pe.matmul(m.bank[:, 4 * (g % 2) + b // 2, (b % 2) * 256:(b % 2 + 1) * 256],
                                     m.ident[0:TS, b:b + 1].broadcast_to([TS, 128]), news[:, 256 * g:256 * g + 256], start=True, stop=True)
                last.then_inc(s_q, 1)
            pe.wait_ge(s_s, CG)
            for i in range(CH):
                g, h = divmod(i, 4)
                last = pe.transpose(m.bank[0:TS, 4 + i // 4, (i % 4) * 128:(i % 4 + 1) * 128], sT[:, g, :, h], m.ident[:])
            last.then_inc(s_t, 1)
            pe.wait_ge(s_p, 1)
            for i in range(CH):
                last = pe.transpose(m.bank[:, 0, 8 * i:8 * i + 8], sm[:, i, 0:128], m.ident[0:TS, 0:TS])
            last.then_inc(s_pt, 1)
            pe.wait_ge(s_w, CG + 1)
            for j in range(2):
                for b in range(TS):
                    for g in range(CG):
                        pe.matmul(m.bank[:, 1, 8 * j + b:8 * j + b + 1], prod[g][:, 256 * b + 128 * j:256 * b + 128 * j + 128],
                                  m.ones[:, 0:1], start=(g == 0), stop=(g == CG - 1))
                last = pe.matmul(m.bank[:, 2, 8 * j:8 * j + 8], tn[:, 128 * j:128 * j + 128], m.ident[0:TS, 0:TS], start=True, stop=True)
            last.then_inc(s_o, 1)

        @block.vector
        def _(dve):
            link = linker(dve, s_v)
            dve.wait_ge(s_kv, 48)
            for g in range(CG):
                dve.wait_ge(s_q, g + 1)
                for a in range(4):
                    ins = dve.tensor_tensor(prod[g][:, a * 512:(a + 1) * 512].rearrange("p (b d) -> p b d", b=2),
                                            kv[g][:, 2 * a:2 * a + 2, 0:256],
                                            m.bank[:, 4 * (g % 2) + a, :].rearrange("p (b d) -> p b d", b=2), ALU.mult)
                ins.then_inc(s_pr, 1)
                dve.wait_ge(s_pr, g + 1)
                dve.tensor_reduce(sT[:, g].rearrange("p b h -> p (b h)"), prod[g].rearrange("p (i d) -> p i d", d=CD), AX.X, ALU.add)\
                    .then_inc(s_s, 1)
            link(dve.tensor_tensor(new, news[:, 0:CW], news[:, CW:2 * CW], ALU.mult))
            link(dve.tensor_reduce(sc12, new.rearrange("p (i d) -> p i d", d=CD), AX.X, ALU.add))
            dve.wait_ge(s_b, 48)
            link(dve.scalar_tensor_tensor(sm[:, :, 128], sc12, SCALE, bias[:, :, 128], ALU.mult, ALU.add))
            dve.wait_ge(s_t, 1)
            for g in range(CG):
                link(dve.scalar_tensor_tensor(sm[:, 4 * g:4 * g + 4, 0:128], m.bank[0:TS, 4 + g, :].rearrange("p (i j) -> p i j", i=4),
                                              SCALE, bias[:, 4 * g:4 * g + 4, 0:128], ALU.mult, ALU.add))
            link(dve.tensor_reduce(mx12, sm, AX.X, ALU.max))
            dve.tensor_tensor(sm, sm, bc(mx12, 129), ALU.subtract).then_inc(s_sm, 1)
            dve.wait_ge(s_e, 1)
            dve.tensor_reduce(den12, sm, AX.X, ALU.add).then_inc(s_l, 1)
            dve.wait_ge(s_l2, 1)
            link(dve.tensor_tensor(lse12, lse12, mx12, ALU.add))
            link(dve.tensor_reduce(m4, lse12.rearrange("p (g h) -> p h g", g=CG), AX.X, ALU.max))
            dve.tensor_tensor(lse12.rearrange("p (g h) -> p g h", g=CG), lse12.rearrange("p (g h) -> p g h", g=CG),
                              bmid(m4, CG), ALU.subtract).then_inc(s_l, 1)
            dve.wait_ge(s_l2, 2)
            link(dve.tensor_reduce(d4, lse12.rearrange("p (g h) -> p h g", g=CG), AX.X, ALU.add))
            link(dve.reciprocal(d4, d4))
            link(dve.reciprocal(rd12, den12))
            link(dve.tensor_tensor(rd12, rd12, lse12, ALU.mult))
            link(dve.tensor_tensor(rd12.rearrange("p (g h) -> p g h", g=CG), rd12.rearrange("p (g h) -> p g h", g=CG), bmid(d4, CG), ALU.mult))
            dve.tensor_tensor(sm, sm, bc(rd12, 129), ALU.mult).then_inc(s_p, 1)
            dve.wait_ge(s_p, 1)
            link(dve.tensor_tensor(new.rearrange("p (i d) -> p i d", d=CD), news[:, 2 * CW:3 * CW].rearrange("p (i d) -> p i d", d=CD),
                                   bc(sm[:, :, 128], CD), ALU.mult))
            link(dve.tensor_tensor(tn, new[:, 0:256], new[:, 256:512], ALU.add))
            dve.tensor_tensor(tn, tn, new[:, 512:768], ALU.add).then_inc(s_w, 1)
            dve.wait_ge(s_pt, 1)
            link(dve.tensor_copy(pTs, m.bank[:, 0, 0:96].rearrange("p (i b) -> p i b", i=CH)))
            for g in range(CG):
                for b in range(TS):
                    ins = dve.tensor_tensor(prod[g][:, 256 * b:256 * b + 256].rearrange("p (h d) -> p h d", h=4),
                                            kv[g][:, b, 256:512].rearrange("p (h d) -> p h d", h=4), bc(pTs[:, 4 * g:4 * g + 4, b], CD), ALU.mult)
                ins.then_inc(s_w, 1)
            dve.wait_ge(s_o, 1)
            link(dve.tensor_copy(half, m.bank[:, 2, 0:16]))
            link(dve.tensor_tensor(m.ycT[:, :, TP:T], m.bank[:, 1, 0:16].rearrange("p (j b) -> p j b", j=2),
                                   half.rearrange("p (j b) -> p j b", j=2), ALU.add))

        @block.scalar
        def _(act):
            act.wait_ge(s_sm, 1)
            act.activation(sm, sm, ACT.Exp).then_inc(s_e, 1)
            act.wait_ge(s_l, 1)
            act.activation(lse12, den12, ACT.Ln).then_inc(s_l2, 1)
            act.wait_ge(s_l, 2)
            act.activation(lse12, lse12, ACT.Exp).then_inc(s_l2, 1)


TILES = [(c * 128, 128) for c in range(NC)] + [(TP, TS)]
NT = len(TILES)
SLOTS_E = 128
PASSES = -(-T // SLOTS_E)
ITEMS = PASSES * NE


def merge(nc, m, t):
    x1d = nc.dram_tensor("x1_rows", [T, D], F32).ap()
    merged = m.arena[:, 0:NT * D].rearrange("p (c d) -> p c d", c=NT)
    wo = [m.slot(6 + i).rearrange("p (k n) -> p k n", k=KT) for i in range(2)]
    with ExitStack() as ctx:
        st = Stage(nc, ctx, "mg")
        sg = [m.arena[:, 5120 + 512 * i:5632 + 512 * i] for i in range(2)]
        tm = [m.arena[:, 6144 + 512 * i:6656 + 512 * i] for i in range(2)]
        jobs = [(br, hf) for br in range(3) for hf in range(2)]
        kts = (KT, KT, 2)
        src = (m.yaT, m.ybT, m.ycT)
        wn = ("w_branch_a", "w_branch_b", "w_branch_c")
        s_w = [st.sem(f"w{i}") for i in range(2)]
        s_wo, s_pe, s_sig, s_prod, s_add = (st.sem(n) for n in ("wo", "pe", "sig", "prod", "add"))
        gate_w = [m.slot(2 + i).rearrange("p (k n) -> p k n", k=KT) for i in range(2)]
        br_w = [m.slot(4 + i).rearrange("p (k n) -> p k n", k=KT) for i in range(2)]
        block = ctx.enter_context(nc.Block())

        @block.sync
        def _(sp):
            for j, (br, hf) in enumerate(jobs):
                if j >= 2:
                    sp.wait_ge(s_pe, NT * (j - 1))
                c0 = GT0 + br * D + hf * 512
                sp.dma_start(gate_w[j % 2], t["w_in"][0, :, c0:c0 + 512].rearrange("(k p) n -> p k n", p=128)).then_inc(s_w[j % 2], 16)
                sp.dma_start(br_w[j % 2][:, 0:kts[br], :],
                             t[wn[br]][0, :, hf * 512:(hf + 1) * 512].rearrange("(k p) n -> p k n", p=128)).then_inc(s_w[j % 2], 16)
            for i in range(2):
                sp.dma_start(wo[i], t["w_out"][0, :, i * 512:(i + 1) * 512].rearrange("(k p) n -> p k n", p=128)).then_inc(s_wo, 16)
            sp.wait_ge(s_wo, 32)

        @block.tensor
        def _(pe):
            for j, (br, hf) in enumerate(jobs):
                pe.wait_ge(s_w[j % 2], 32 * (j // 2 + 1))
                for c, (a, R) in enumerate(TILES):
                    n = NT * j + c
                    if n >= 4:
                        pe.wait_ge(s_prod, n - 3)
                    for k in range(KT):
                        pe.matmul(m.bank[0:R, 2 * (n % 4), :], m.xT[:, k, a:a + R], gate_w[j % 2][:, k, :], start=(k == 0), stop=(k == KT - 1))
                    for k in range(kts[br]):
                        last = pe.matmul(m.bank[0:R, 2 * (n % 4) + 1, :], src[br][:, k, a:a + R], br_w[j % 2][:, k, :],
                                         start=(k == 0), stop=(k == kts[br] - 1))
                    last.then_inc(s_pe, 1)

        @block.scalar
        def _(act):
            for n in range(NT * len(jobs)):
                R = TILES[n % NT][1]
                act.wait_ge(s_pe, n + 1)
                if n >= 2:
                    act.wait_ge(s_prod, n - 1)
                act.activation(sg[n % 2][0:R], m.bank[0:R, 2 * (n % 4), :], ACT.Sigmoid).then_inc(s_sig, 1)

        @block.vector
        def _(dve):
            for n in range(NT * len(jobs)):
                j, c = divmod(n, NT)
                br, hf = jobs[j]
                R = TILES[c][1]
                dst = merged[0:R, c, hf * 512:(hf + 1) * 512]
                out = dst if br == 0 else tm[n % 2][0:R]
                dve.wait_ge(s_sig, n + 1)
                dve.tensor_tensor(out, sg[n % 2][0:R], m.bank[0:R, 2 * (n % 4) + 1, :], ALU.mult).then_inc(s_prod, 1)
                dve.wait_ge(s_prod, n + 1)
                if br:
                    dve.tensor_tensor(dst, dst, out, ALU.add).then_inc(s_add, 1)
                    dve.wait_ge(s_add, n + 1 - 2 * NT)

    with ExitStack() as ctx:
        st = Stage(nc, ctx, "o")
        xr = m.arena[:, 2 * SLOT:2 * SLOT + NT * D].rearrange("p (c d) -> p c d", c=NT)
        lng, lnb = m.slot(4)[:, 0:D], m.slot(4)[:, D:2 * D]
        bn = m.slot(4)[:, 2 * D:2 * D + 64]
        s_ld, s_tr, s_te, s_mm, s_x, s_v, s_var, s_rstd, s_out, s_n, s_t2, s_e2 = (st.sem(n) for n in (
            "ld", "tr", "te", "mm", "x", "v", "var", "rstd", "out", "n", "t2", "e2"))
        block = ctx.enter_context(nc.Block())

        def x1_transposes(pe, c):
            R = TILES[c][1]
            pe.wait_ge(s_n, c + 1)
            if c >= 1:
                pe.wait_ge(s_e2, c)
            for k in range(KT):
                last = pe.transpose(m.bank[:, 6 + k // 4, (k % 4) * 128:(k % 4) * 128 + R], xr[0:R, c, k * 128:(k + 1) * 128], m.ident[0:R, 0:R])
            last.then_inc(s_t2, 1)

        def rest(act, c):
            a, R = TILES[c]
            act.wait_ge(s_var, c + 1)
            act.activation(bn[0:R, 14:15], bn[0:R, 14:15], ACT.Sqrt).then_inc(s_rstd, 1)
            act.wait_ge(s_t2, c + 1)
            act.copy(m.xT[:, :, a:a + R], m.bank[:, 6:8, :].rearrange("p b (j q) -> p (b j) q", j=4)[:, :, 0:R]).then_inc(s_e2, 1)

        @block.sync
        def _(sp):
            sp.dma_start(xr[:, 0:NC, :], t["x_prompt"][0].rearrange("(c p) d -> p c d", p=128)).then_inc(s_ld, 16)
            sp.dma_start(xr[0:TS, NC, :], t["x_sample"][:, 0, :]).then_inc(s_ld, 16)
            sp.dma_start(lng, t["ln1_g"][0].partition_broadcast(128)).then_inc(s_ld, 16)
            sp.dma_start(lnb, t["ln1_b"][0].partition_broadcast(128)).then_inc(s_ld, 16)
            for c, (a, R) in enumerate(TILES):
                sp.wait_ge(s_n, c + 1)
                sp.dma_start(x1d[a:a + R], xr[0:R, c, :]).then_inc(s_out, 16)
            sp.wait_ge(s_out, 16 * NT)

        @block.tensor
        def _(pe):
            for c, (a, R) in enumerate(TILES):
                for h in range(2):
                    n = 2 * c + h
                    if n >= 2:
                        pe.wait_ge(s_te, n - 1)
                    for j in range(4):
                        k = 4 * h + j
                        last = pe.transpose(m.bank[:, n % 2, j * 128:j * 128 + R], merged[0:R, c, k * 128:(k + 1) * 128], m.ident[0:R, 0:R])
                    last.then_inc(s_tr, 1)
                pe.wait_ge(s_te, 2 * c + 2)
                if c >= 2:
                    pe.wait_ge(s_x, 2 * (c - 1))
                for h in range(2):
                    for k in range(KT):
                        last = pe.matmul(m.bank[0:R, 2 + 2 * (c % 2) + h, :], m.yaT[:, k, a:a + R], wo[h][:, k, :], start=(k == 0), stop=(k == KT - 1))
                    last.then_inc(s_mm, 1)
                if c >= 1:
                    x1_transposes(pe, c - 1)
            x1_transposes(pe, NT - 1)

        @block.vector
        def _(dve):
            link = linker(dve, s_v)
            dve.wait_ge(s_ld, 64)
            for c, (a, R) in enumerate(TILES):
                x = xr[0:R, c, :]
                for h in range(2):
                    dve.wait_ge(s_mm, 2 * c + h + 1)
                    xh = x[:, h * 512:(h + 1) * 512]
                    dve.scalar_tensor_tensor(xh, xh, ALPHA, m.bank[0:R, 2 + 2 * (c % 2) + h, :], ALU.mult, ALU.add).then_inc(s_x, 1)
                dve.wait_ge(s_x, 2 * c + 2)
                layer_norm(dve, link, x, bn[0:R], lng[0:R], lnb[0:R], s_var, s_rstd, s_n, c)

        @block.scalar
        def _(act):
            for c, (a, R) in enumerate(TILES):
                for h in range(2):
                    n = 2 * c + h
                    act.wait_ge(s_tr, n + 1)
                    act.copy(m.yaT[:, 4 * h:4 * h + 4, a:a + R],
                             m.bank[:, n % 2, :].rearrange("p (j q) -> p j q", j=4)[:, :, 0:R]).then_inc(s_te, 1)
                if c >= 1:
                    rest(act, c - 1)
            rest(act, NT - 1)

    return x1d


def layer_norm(dve, link, x, bn, gain, shift, s_var, s_rstd, s_done, c):
    for h in range(2):
        link(dve.bn_stats(bn[:, 6 * h:6 * h + 6], x[:, h * 512:(h + 1) * 512]))
    link(dve.bn_aggr(bn[:, 12:14], bn[:, 0:12]))
    dve.tensor_scalar(bn[:, 14:15], bn[:, 13:14], EPS, None, ALU.add).then_inc(s_var, 1)
    dve.wait_ge(s_rstd, c + 1)
    link(dve.reciprocal(bn[:, 15:16], bn[:, 14:15]))
    link(dve.tensor_scalar(x, x, bn[:, 12:13], bn[:, 15:16], ALU.subtract, ALU.mult))
    link(dve.tensor_tensor(x, x, gain, ALU.mult))
    dve.tensor_tensor(x, x, shift, ALU.add).then_inc(s_done, 1)
    dve.wait_ge(s_done, c + 1)


def route(nc, m, t):
    table = nc.dram_tensor("slot_table", [(ITEMS + 1) * SLOTS_E, 2], U32).ap()
    w = m.work
    gates = w[:, 0:20].rearrange("p (c k) -> p c k", c=NT)
    dest = w[:, 20:40].bitcast(U32).rearrange("p (c k) -> p c k", c=NT)
    counts = w[:, 40:42].bitcast(mybir.dt.int32)
    GT = m.ybT[0:NE].rearrange("p k q -> p (k q)")[:, 0:T]
    with ExitStack() as ctx:
        st = Stage(nc, ctx, "r")
        s = m.slot(0)
        rw = s[:, 0:256].rearrange("p (k n) -> p k n", k=KT)
        rb, iota = s[:, 256:288], s[:, 288:320]
        tok = s[:, 320:360].bitcast(U32).rearrange("p (c k i) -> p c k i", c=NT, k=TOPK)
        stri = s[:, 500:628]
        lg = s[:, 640:800].rearrange("p (c e) -> p c e", c=NT)
        v8 = s[:, 800:840].rearrange("p (c e) -> p c e", c=NT)
        i8 = s[:, 840:880].bitcast(U32).rearrange("p (c e) -> p c e", c=NT)
        if8 = s[:, 880:920].rearrange("p (c e) -> p c e", c=NT)
        mask = s[:, 1000:1160].rearrange("p (c e) -> p c e", c=NT)
        G = s[:, 1160:1320].rearrange("p (c e) -> p c e", c=NT)
        oh = s[:, 1320:1960].rearrange("p (c k e) -> p c k e", c=NT, k=TOPK)
        pr = s[:, 1960:2088].rearrange("p (k e) -> p k e", k=TOPK)
        rank = s[:, 2090:2094]
        df = s[:, 2094:2098]
        gs = s[:, 2100:2101]
        cm = s[:, 2101:2104]
        ge = s[:, 2104:2108]
        s_ld, s_lg, s_v, s_e, s_ee, s_m, s_rk, s_g, s_gt, s_d, s_sc = (st.sem(n) for n in (
            "ld", "lg", "v", "e", "ee", "m", "rk", "g", "gt", "d", "sc"))
        block = ctx.enter_context(nc.Block())

        @block.sync
        def _(sp):
            sp.dma_start(rw, t["router_w"][0].rearrange("(k p) n -> p k n", p=128)).then_inc(s_ld, 16)
            sp.dma_start(rb, t["router_b"][0].partition_broadcast(128)).then_inc(s_ld, 16)
            sp.dma_start(iota, t["c_iota"][0].partition_broadcast(128)).then_inc(s_ld, 16)
            sp.dma_start(s[:, 320:360].bitcast(U32), t["c_token"]).then_inc(s_ld, 16)

        @block.gpsimd
        def _(pool):
            pool.dma_start(table, t["c_empty"]).then_inc(s_sc, 16)
            pool.wait_ge(s_sc, 16)
            pool.wait_ge(s_ld, 64)
            n = 1
            for c, (a, R) in enumerate(TILES):
                pool.wait_ge(s_d, c + 1)
                for k in range(TOPK):
                    pool.indirect_dma_start(out=table, out_offset=bass.IndirectOffsetOnAxis(ap=dest[0:R, c, k:k + 1], axis=0),
                                            in_=tok[0:R, c, k, :], in_offset=None).then_inc(s_sc, 16)
                    n += 1
            pool.wait_ge(s_sc, 16 * n)

        @block.tensor
        def _(pe):
            pe.wait_ge(s_ld, 64)
            for c, (a, R) in enumerate(TILES):
                for k in range(KT):
                    last = pe.matmul(m.bank[0:R, 3 + c, 0:32], m.xT[:, k, a:a + R], rw[:, k, :], start=(k == 0), stop=(k == KT - 1))
                last.then_inc(s_lg, 1)
            pe.wait_ge(s_m, NT + 1)
            for c, (a, R) in enumerate(TILES):
                for b in range(c):
                    pe.matmul(m.bank[0:R, 1, 32 * c:32 * c + 32], m.ones[:, 0:R], mask[:, b, :], start=(b == 0), stop=False)
                pe.matmul(m.bank[0:R, 1, 32 * c:32 * c + 32], stri[0:R, 0:R], mask[0:R, c, :], start=(c == 0), stop=True)
            for c, (a, R) in enumerate(TILES):
                last = pe.matmul(m.bank[:, 2, 0:32], m.ones[0:R, :], mask[0:R, c, :], start=(c == 0), stop=(c == NT - 1))
            last.then_inc(s_rk, 1)
            pe.wait_ge(s_g, NT)
            for c, (a, R) in enumerate(TILES):
                last = pe.transpose(m.bank[0:NE, 3 + c // 4, (c % 4) * 128:(c % 4) * 128 + R], G[0:R, c, :], m.ident[0:R, 0:R])
            last.then_inc(s_gt, 1)

        @block.vector
        def _(dve):
            link = linker(dve, s_v)
            dve.wait_ge(s_ld, 64)
            dve.tensor_tensor(stri, m.tri[:], m.ident[:], ALU.subtract).then_inc(s_m, 1)
            for c, (a, R) in enumerate(TILES):
                dve.wait_ge(s_lg, c + 1)
                link(dve.tensor_tensor(lg[0:R, c], m.bank[0:R, 3 + c, 0:32], rb[0:R], ALU.add))
                link(dve.max(v8[0:R, c], lg[0:R, c]))
                link(dve.max_index(i8[0:R, c], v8[0:R, c], lg[0:R, c]))
                link(dve.tensor_copy(if8[0:R, c], i8[0:R, c]))
                for k in range(TOPK):
                    link(dve.tensor_scalar(oh[0:R, c, k], iota[0:R], if8[0:R, c, k:k + 1], None, ALU.is_equal))
                dve.tensor_reduce(mask[0:R, c], oh[0:R, c].rearrange("p k e -> p e k"), AX.X, ALU.add).then_inc(s_m, 1)
                dve.tensor_scalar(gates[0:R, c], v8[0:R, c, 0:TOPK], v8[0:R, c, 0:1], None, ALU.subtract).then_inc(s_e, 1)
            dve.wait_ge(s_m, NT + 1)
            for c, (a, R) in enumerate(TILES):
                dve.wait_ge(s_ee, c + 1)
                link(dve.tensor_reduce(gs[0:R], gates[0:R, c], AX.X, ALU.add))
                link(dve.reciprocal(gs[0:R], gs[0:R]))
                link(dve.tensor_scalar(gates[0:R, c], gates[0:R, c], gs[0:R], None, ALU.mult))
                link(dve.tensor_scalar(G[0:R, c], oh[0:R, c, 0], gates[0:R, c, 0:1], None, ALU.mult))
                for k in range(1, TOPK):
                    ins = dve.scalar_tensor_tensor(G[0:R, c], oh[0:R, c, k], gates[0:R, c, k:k + 1], G[0:R, c], ALU.mult, ALU.add)
                    if k < TOPK - 1:
                        link(ins)
                ins.then_inc(s_g, 1)
            dve.wait_ge(s_rk, 1)
            for c, (a, R) in enumerate(TILES):
                link(dve.tensor_tensor(pr[0:R], oh[0:R, c], bmid(m.bank[0:R, 1, 32 * c:32 * c + 32], TOPK), ALU.mult))
                link(dve.tensor_reduce(rank[0:R], pr[0:R], AX.X, ALU.add))
                link(dve.scalar_tensor_tensor(df[0:R], if8[0:R, c, 0:TOPK], float(SLOTS_E), rank[0:R], ALU.mult, ALU.add))
                for p in range(1, PASSES):
                    link(dve.tensor_scalar(ge[0:R], rank[0:R], float(p * SLOTS_E), float((NE - 1) * SLOTS_E), ALU.is_ge, ALU.mult))
                    link(dve.tensor_tensor(df[0:R], df[0:R], ge[0:R], ALU.add))
                dve.tensor_copy(dest[0:R, c], df[0:R]).then_inc(s_d, 1)
            link(dve.tensor_reduce(cm[:, 0:1], m.bank[:, 2, 0:32], AX.X, ALU.max))
            link(dve.memset(cm[:, 1:2], 1.0))
            for p in range(1, PASSES):
                link(dve.tensor_scalar(cm[:, 2:3], cm[:, 0:1], float(p * SLOTS_E), None, ALU.is_gt))
                link(dve.tensor_tensor(cm[:, 1:2], cm[:, 1:2], cm[:, 2:3], ALU.add))
            link(dve.tensor_scalar(cm[:, 0:1], cm[:, 1:2], float(NE), None, ALU.mult))
            link(dve.tensor_copy(counts, cm[:, 0:2]))
            dve.wait_ge(s_gt, 1)
            link(dve.tensor_copy(GT[:, 0:512], m.bank[0:NE, 3, :]))
            link(dve.tensor_copy(GT[:, 512:T], m.bank[0:NE, 4, 0:TS]))

        @block.scalar
        def _(act):
            for c, (a, R) in enumerate(TILES):
                act.wait_ge(s_e, c + 1)
                act.activation(gates[0:R, c], gates[0:R, c], ACT.Exp).then_inc(s_ee, 1)
    return table, gates, counts, GT


def experts(nc, m, t, x1d, table, counts):
    ybuf = nc.dram_tensor("choice_out", [TOPK * T + SLOTS_E, D], F32).ap()
    w1 = [m.slot(q).rearrange("p (k n) -> p k n", k=KT) for q in range(4)]
    w2 = [m.slot(4 + q).rearrange("p (k n) -> p k n", k=KT) for q in range(2)]
    xg = m.slot(6)[:, 0:1024]
    xgT = m.slot(6)[:, 1024:2048].rearrange("p (k q) -> p k q", k=KT)
    actT = m.slot(6)[:, 2048:3072].rearrange("p (k q) -> p k q", k=KT)
    ysb = m.slot(6)[:, 3072:4096]
    b1T = m.slot(7)[:, 0:512].rearrange("p (i e) -> p i e", e=NE)
    tb = [m.slot(7)[:, 512 + 512 * i:1024 + 512 * i].rearrange("p (g f q) -> p g f q", g=2, f=2) for i in range(2)]
    sg = [m.slot(7)[:, 1536 + 256 * i:1792 + 256 * i].rearrange("p (f q) -> p f q", f=2) for i in range(2)]
    bcur = m.slot(7)[:, 2048:2064].rearrange("p (g f) -> p g f", g=2)
    itok = m.slot(7)[:, 2100:2101].bitcast(U32)
    irow = m.slot(7)[:, 2101:2102].bitcast(U32)
    b1r = m.slot(8)[0:NE, 0:2 * FF]
    with ExitStack() as ctx:
        st = Stage(nc, ctx, "e")
        s_w = [st.sem(f"w{q}") for q in range(6)]
        s_done = [st.sem(f"done{q}") for q in range(6)]
        (s_b1, s_bt, s_bc, s_ix, s_go, s_yfree, s_ir, s_g, s_tr, s_xe, s_pre, s_sig, s_act, s_ye, s_st, s_v, s_bq) = (st.sem(n) for n in (
            "b1", "bt", "bc", "ix", "go", "yfree", "ir", "g", "tr", "xe", "pre", "sig", "act", "ye", "st", "v", "bq"))
        block = ctx.enter_context(nc.Block())

        @block.sync
        def _(sp):
            sp.dma_start(b1r, t["moe_b1"][0]).then_inc(s_b1, 16)
            for q in range(6):
                sp.sem_inc(s_done[q], 1)
            passes = sp.value_load(counts[0:1, 1:2], min_val=1, max_val=PASSES)
            with sp.Fori(0, passes) as p:
                with sp.Fori(0, NE) as e:
                    i = p * NE + e
                    for q in range(6):
                        sp.wait_ge(s_done[q], i + 1)
                        if q < 4:
                            sp.dma_start(w1[q], t["moe_w1"][0, e, :, q * 512:(q + 1) * 512].rearrange("(k p) n -> p k n", p=128))\
                                .then_inc(s_w[q], 16)
                        else:
                            sp.dma_start(w2[q - 4], t["moe_w2"][0, e, :, (q - 4) * 512:(q - 3) * 512].rearrange("(k p) n -> p k n", p=128))\
                                .then_inc(s_w[q], 16)

        @block.gpsimd
        def _(pool):
            items = pool.value_load(counts[0:1, 0:1], min_val=NE, max_val=ITEMS)

            def gather(i, number):
                pool.dma_start(itok, table[bass.ds(i * SLOTS_E, SLOTS_E), 0:1], allow_slow_non_contiguous=True).then_inc(s_ix, 16)
                pool.wait_ge(s_ix, number * 16)
                pool.sem_inc(s_go, 1)
                pool.indirect_dma_start(out=xg, out_offset=None, in_=x1d,
                                        in_offset=bass.IndirectOffsetOnAxis(ap=itok, axis=0)).then_inc(s_g, 16)
            gather(0, 1)
            with pool.Fori(0, items) as i:
                pool.wait_ge(s_g, (i + 1) * 16)
                pool.wait_ge(s_tr, i + 1)
                gather(i + 1, i + 2)
                pool.dma_start(irow, table[bass.ds(i * SLOTS_E, SLOTS_E), 1:2], allow_slow_non_contiguous=True).then_inc(s_ir, 16)
                pool.wait_ge(s_ir, (i + 1) * 16)
                pool.wait_ge(s_ye, i * 2 + 3)
                pool.sem_inc(s_go, 1)
                pool.indirect_dma_start(out=ybuf, out_offset=bass.IndirectOffsetOnAxis(ap=irow, axis=0), in_=ysb, in_offset=None)\
                    .then_inc(s_st, 16)
                pool.wait_ge(s_st, (i + 1) * 16)
                pool.sem_inc(s_yfree, 1)
            pool.wait_ge(s_g, items * 16 + 16)

        @block.tensor
        def _(pe):
            items = pe.value_load(counts[0:1, 0:1], min_val=NE, max_val=ITEMS)
            pe.wait_ge(s_b1, 16)
            for g in range(2):
                for f in range(8):
                    last = pe.transpose(m.bank[:, 0, (8 * g + f) * 32:(8 * g + f + 1) * 32],
                                        b1r[:, 256 * f + g:256 * f + 256:2], m.ident[0:NE, 0:NE])
            last.then_inc(s_bt, 1)

            def transposes(number):
                pe.wait_ge(s_g, number * 16)
                for k in range(KT):
                    last = pe.transpose(m.bank[:, 6 + k // 4, (k % 4) * 128:(k % 4 + 1) * 128], xg[:, k * 128:(k + 1) * 128], m.ident[:])
                last.then_inc(s_tr, 1)
            transposes(1)
            pe.wait_ge(s_bc, 1)
            with pe.Fori(0, items) as i:
                pe.wait_ge(s_xe, i + 1)
                for q in range(4):
                    pe.wait_ge(s_w[q], (i + 1) * 16)
                    for g in range(2):
                        for f in range(2):
                            for k in range(KT):
                                last = pe.matmul(m.bank[:, q, (2 * g + f) * 128:(2 * g + f + 1) * 128],
                                                 w1[q][:, k, 256 * f + g:256 * f + 256:2], xgT[:, k, :], start=(k == 0), stop=(k == KT - 1))
                    last.then_inc(s_done[q], 1)
                transposes(i + 2)
                pe.wait_ge(s_act, (i + 1) * 4)
                pe.wait_ge(s_ye, i * 2 + 1)
                for n in range(2):
                    pe.wait_ge(s_w[4 + n], (i + 1) * 16)
                    for f in range(8):
                        last = pe.matmul(m.bank[:, 4 + n, :], actT[:, f, :], w2[n][:, f, :], start=(f == 0), stop=(f == 7))
                    last.then_inc(s_done[4 + n], 1)

        @block.vector
        def _(dve):
            link = linker(dve, s_v)
            dve.wait_ge(s_bt, 1)
            dve.tensor_copy(b1T, m.bank[:, 0, :].rearrange("p (i e) -> p i e", e=NE)).then_inc(s_bc, 1)
            dve.wait_ge(s_bc, 1)
            passes = dve.value_load(counts[0:1, 1:2], min_val=1, max_val=PASSES)
            with dve.Fori(0, passes) as p:
                with dve.Fori(0, NE) as e:
                    i = p * NE + e
                    dve.tensor_copy(bcur.rearrange("p g f -> p (g f)"), b1T[:, :, e]).then_inc(s_bq, 1)
                    dve.wait_ge(s_bq, i + 1)
                    for q in range(5):
                        if q < 4:
                            tt = tb[q % 2]
                            dve.wait_ge(s_done[q], i + 2)
                            dve.tensor_tensor(tt, m.bank[:, q, :].rearrange("p (g f q) -> p g f q", g=2, f=2),
                                              bc(bcur[:, :, 2 * q:2 * q + 2], 128), ALU.add).then_inc(s_v, 1)
                            dve.wait_ge(s_v, i * 12 + 3 * q + 1)
                            dve.tensor_scalar(tt[:, 0], tt[:, 0], 7.0, None, ALU.min).then_inc(s_pre, 1)
                            dve.tensor_scalar(tt[:, 1], tt[:, 1], 7.0, -7.0, ALU.min, ALU.max).then_inc(s_v, 1)
                            dve.wait_ge(s_pre, i * 4 + q + 1)
                            dve.wait_ge(s_v, i * 12 + 3 * q + 2)
                            dve.scalar_tensor_tensor(tt[:, 1], tt[:, 1], 1.0, tt[:, 0], ALU.add, ALU.mult).then_inc(s_v, 1)
                            dve.wait_ge(s_v, i * 12 + 3 * q + 3)
                        if q > 0:
                            dve.wait_ge(s_sig, i * 4 + q)
                            dve.tensor_tensor(actT[:, 2 * q - 2:2 * q, :], tb[(q - 1) % 2][:, 1], sg[(q - 1) % 2], ALU.mult)\
                                .then_inc(s_act, 1)
                            dve.wait_ge(s_act, i * 4 + q)

        @block.scalar
        def _(act):
            items = act.value_load(counts[0:1, 0:1], min_val=NE, max_val=ITEMS)

            def rows_T(number):
                act.wait_ge(s_tr, number)
                act.copy(xgT, m.bank[:, 6:8, :].rearrange("p b (j q) -> p (b j) q", j=4)).then_inc(s_xe, 1)
            act.sem_inc(s_ye, 1)
            act.sem_inc(s_yfree, 1)
            rows_T(1)
            with act.Fori(0, items) as i:
                for q in range(4):
                    act.wait_ge(s_pre, i * 4 + q + 1)
                    act.activation(sg[q % 2], tb[q % 2][:, 0], ACT.Sigmoid, scale=1.702).then_inc(s_sig, 1)
                rows_T(i + 2)
                act.wait_ge(s_yfree, i + 1)
                for n in range(2):
                    act.wait_ge(s_done[4 + n], i + 2)
                    act.copy(ysb[:, n * 512:(n + 1) * 512], m.bank[:, 4 + n, :]).then_inc(s_ye, 1)
    return ybuf


def combine(nc, m, t, o, x1d, ybuf, gates, GT):
    with ExitStack() as ctx:
        st = Stage(nc, ctx, "f")
        rows = [m.slot(i).rearrange("p (k d) -> p k d", k=TOPK) for i in range(2)]
        x1 = m.arena[:, 2 * SLOT:2 * SLOT + NT * D].rearrange("p (c d) -> p c d", c=NT)
        lng, lnb = m.slot(4)[:, 0:D], m.slot(4)[:, D:2 * D]
        bn = m.slot(4)[:, 2 * D:2 * D + 64]
        b2 = m.slot(5)[0:NE, 0:D]
        s_ld, s_g, s_mm, s_v, s_var, s_rstd, s_n, s_out, s_r = (st.sem(n) for n in ("ld", "g", "mm", "v", "var", "rstd", "n", "out", "r"))
        s_rows = [st.sem(f"rows{i}") for i in range(2)]
        block = ctx.enter_context(nc.Block())

        def load_rows(sp, c):
            a, R = TILES[c]
            sp.dma_start(rows[c % 2][0:R], ybuf[TOPK * a:TOPK * (a + R)].rearrange("(q k) d -> q k d", k=TOPK)).then_inc(s_rows[c % 2], 16)

        @block.sync
        def _(sp):
            sp.dma_start(x1[:, 0:NC, :], x1d[0:TP].rearrange("(c p) d -> p c d", p=128)).then_inc(s_ld, 16)
            sp.dma_start(x1[0:TS, NC, :], x1d[TP:T]).then_inc(s_ld, 16)
            sp.dma_start(b2, t["moe_b2"][0]).then_inc(s_ld, 16)
            sp.dma_start(lng, t["ln2_g"][0].partition_broadcast(128)).then_inc(s_ld, 16)
            sp.dma_start(lnb, t["ln2_b"][0].partition_broadcast(128)).then_inc(s_ld, 16)
            for c in range(2):
                load_rows(sp, c)
            for c, (a, R) in enumerate(TILES):
                if c + 2 < NT:
                    sp.wait_ge(s_r, c + 1)
                    load_rows(sp, c + 2)
                sp.wait_ge(s_n, c + 1)
                dst = o["y_p"][0, a:a + R] if c < NC else o["y_s"][:, 0, :]
                sp.dma_start(dst, x1[0:R, c, :]).then_inc(s_out, 16)
            sp.wait_ge(s_out, 16 * NT)

        @block.tensor
        def _(pe):
            pe.wait_ge(s_ld, 80)
            for c, (a, R) in enumerate(TILES):
                if c >= 4:
                    pe.wait_ge(s_r, c - 3)
                for h in range(2):
                    last = pe.matmul(m.bank[0:R, 2 * (c % 4) + h, :], GT[:, a:a + R], b2[:, h * 512:(h + 1) * 512], start=True, stop=True)
                last.then_inc(s_mm, 1)

        @block.vector
        def _(dve):
            link = linker(dve, s_v)
            dve.wait_ge(s_ld, 80)
            for c, (a, R) in enumerate(TILES):
                x = x1[0:R, c, :]
                dve.wait_ge(s_mm, c + 1)
                link(dve.scalar_tensor_tensor(x.rearrange("p (h n) -> p h n", h=2), x.rearrange("p (h n) -> p h n", h=2), ALPHA,
                                              m.bank[0:R, 2 * (c % 4):2 * (c % 4) + 2, :], ALU.mult, ALU.add))
                dve.wait_ge(s_rows[c % 2], 16 * (c // 2 + 1))
                for k in range(TOPK):
                    ins = dve.scalar_tensor_tensor(x, rows[c % 2][0:R, k, :], gates[0:R, c, k:k + 1], x, ALU.mult, ALU.add)
                    if k < TOPK - 1:
                        link(ins)
                ins.then_inc(s_r, 1)
                dve.wait_ge(s_r, c + 1)
                layer_norm(dve, link, x, bn[0:R], lng[0:R], lnb[0:R], s_var, s_rstd, s_n, c)

        @block.scalar
        def _(act):
            for c, (a, R) in enumerate(TILES):
                act.wait_ge(s_var, c + 1)
                act.activation(bn[0:R, 14:15], bn[0:R, 14:15], ACT.Sqrt).then_inc(s_rstd, 1)


def moe(nc, m, t, o, x1d):
    table, gates, counts, GT = route(nc, m, t)
    ybuf = experts(nc, m, t, x1d, table, counts)
    combine(nc, m, t, o, x1d, ybuf, gates, GT)


def decoder_layer(nc, t, o):
    with ExitStack() as ctx:
        m = Mem(nc, ctx)
        load_x(nc, m, t)
        mixer_a(nc, m, t, o)
        mixer_b(nc, m, t, o)
        mixer_c(nc, m, t, o)
        x1d = merge(nc, m, t)
        moe(nc, m, t, o, x1d)


def constants():
    import numpy as np
    i = np.arange(128)
    c = {"c_ident": np.eye(128, dtype=np.float32), "c_tri": (i[:, None] <= i[None, :]).astype(np.float32),
         "c_ones": np.ones((128, 128), np.float32), "c_headexp": np.repeat(np.eye(AH, dtype=np.float32), AP_, axis=1),
         "c_flip": np.ascontiguousarray(np.eye(128, dtype=np.float32)[::-1]), "c_reset": (np.arange(TP) % 128 != 0).astype(np.float32)[None],
         "c_iota": np.arange(NE, dtype=np.float32)[None]}
    masks = np.zeros((128, len(LEVELS), 128), np.uint32)
    for n, z in enumerate(LEVELS):
        masks[:, n, :] = (i[:, None] // z == i[None, :] // z) & (i[:, None] % z < z // 2) & (i[None, :] % z >= z // 2)
    c["c_masks"] = masks
    rel = 255 - np.arange(384)
    valid = (rel >= 0) & (rel <= 128)
    hot = np.zeros((32, CG, 384), np.float32)
    for g, dil in enumerate((1, 4, 16)):
        d = np.maximum(rel, 0) * dil
        large = 16 + (np.log(np.maximum(d, 1).astype(np.float32) / 16) / np.float32(np.log(128)) * 16).astype(np.int32)
        bucket = np.where(d < 16, d, np.clip(large, 0, 31))
        hot[bucket[valid], g, np.arange(384)[valid]] = 1
    c["c_buckets"] = hot
    c["c_relmask"] = np.where(valid, 0, NEG).astype(np.float32)[None]
    token = np.zeros((128, NT, TOPK, 2), np.uint32)
    for n, (a, R) in enumerate(TILES):
        token[:R, n, :, 0] = a + np.arange(R)[:, None]
        token[:R, n, :, 1] = TOPK * (a + np.arange(R)[:, None]) + np.arange(TOPK)
    c["c_token"] = token.reshape(128, -1)
    empty = np.zeros(((ITEMS + 1) * SLOTS_E, 2), np.uint32)
    empty[:, 1] = TOPK * T + np.arange(len(empty)) % SLOTS_E
    c["c_empty"] = empty
    return c


INPUTS = ["x_prompt", "x_sample", "state_conv", "state_ssm", "state_hgrn", "cache_kv_w128", "cache_kv_w512", "cache_kv_w2048",
          "w_in", "conv_w", "conv_b", "dt_bias", "a_log", "d_skip", "ssm_norm_g", "hgrn_lb", "hgrn_norm_g", "rel_bias",
          "w_branch_a", "w_branch_b", "w_branch_c", "w_out", "ln1_g", "ln1_b", "router_w", "router_b",
          "moe_w1", "moe_b1", "moe_w2", "moe_b2", "ln2_g", "ln2_b"]
OUTPUTS = [("y_p", (1, TP, D)), ("y_s", (TS, 1, D)), ("conv_p", (1, 1, 3, ACH)), ("conv_s", (1, TS, 3, ACH)),
           ("ssm_p", (1, 1, AH, AP_, AN)), ("ssm_s", (1, TS, AH, AP_, AN)), ("hgrn_p", (1, 1, BH, BK, 128)),
           ("hgrn_s", (1, TS, BH, BK, 128)), ("kv128_p", (1, 1, 128, 2, 4, CD)), ("kv128_s", (1, TS, 1, 2, 4, CD)),
           ("kv512_p", (1, 1, TP, 2, 4, CD)), ("kv512_s", (1, TS, 1, 2, 4, CD)), ("kv2048_p", (1, 1, TP, 2, 4, CD)),
           ("kv2048_s", (1, TS, 1, 2, 4, CD))]


def kernel(**inputs):
    import numpy as np
    import concourse.bacc as bacc
    from concourse.bass_utils import run_bass_kernel_spmd

    nc = bacc.Bacc("TRN2", target_bir_lowering=False, num_devices=1)
    data = {n: np.ascontiguousarray(inputs[n]) for n in INPUTS} | constants()
    t = {n: nc.dram_tensor(f"in_{n}", a.shape, mybir.dt.from_np(a.dtype), kind="ExternalInput").ap() for n, a in data.items()}
    o = {n: nc.dram_tensor(f"out_{n}", shape, F32, kind="ExternalOutput").ap() for n, shape in OUTPUTS}
    decoder_layer(nc, t, o)
    r = run_bass_kernel_spmd(nc, [{f"in_{n}": a for n, a in data.items()}], core_ids=[0])
    return tuple(r.results[0][f"out_{n}"] for n, _ in OUTPUTS)
```

```python
from contextlib import ExitStack

import concourse.bass as bass
from concourse import mybir

F32 = mybir.dt.float32
R32 = mybir.dt.float32r
U32 = mybir.dt.uint32
ALU = mybir.AluOpType
ACT = mybir.ActivationFunctionType
AX = mybir.AxisListType

D = 1024
KT = D // 128
TP = 512
TS = 8
T = TP + TS
NC = TP // 128
HALF = T // 2
AH, AP_, AN, AG = 16, 64, 128, 2
ACH = D + 2 * AG * AN
AM = ACH // 128
BH, BK = 8, 128
CH, CD, CG, CHG = 12, 64, 3, 4
CW = CH * CD
NE, TOPK, FF = 32, 4, 1024
EPS = 1e-5
ALPHA = 2.0 ** 0.25
NEG = -1e30
Z0 = 0
XBC0 = Z0 + D
DT0 = XBC0 + ACH
BQ0 = DT0 + AH
BF0 = BQ0 + D
BI0 = BF0 + D
BG0 = BI0 + D
CQ0 = BG0 + D
CK0 = CQ0 + CW
CV0 = CK0 + CW
GT0 = CV0 + CW

SLOT = 4096
SLOTS = 9
LOW = 4
LEVELS = (128, 64, 32, 16, 8, 4, 2)


class Stage:

    def __init__(self, nc, ctx, name):
        self.nc, self.name, self.sems = nc, name, []
        ctx.callback(self.release)

    def sem(self, name):
        self.sems.append(self.nc.alloc_semaphore(f"{self.name}_{name}"))
        return self.sems[-1]

    def release(self):
        self.nc.clear_and_free_semaphores(self.sems)
        self.nc.all_engine_barrier()


def linker(eng, sem):
    count = [0]

    def link(ins):
        count[0] += 1
        ins.then_inc(sem, 1)
        eng.wait_ge(sem, count[0])
    return link


def bc(ap, n):
    return ap.unsqueeze(len(ap.shape)).broadcast_to(list(ap.shape) + [n])


def bmid(ap, n):
    return ap.unsqueeze(1).broadcast_to([ap.shape[0], n, ap.shape[1]])


class Mem:

    def __init__(self, nc, ctx):
        self.nc = nc
        self.low = None
        self.ident = self.sb(ctx, "ident", [128, 128])
        self.work = self.sb(ctx, "work", [128, 1600])
        self.GT = self.sb(ctx, "GT", [NE, T])
        self.xT = self.sb(ctx, "xT", [128, KT, T])
        self.tri, self.ones = (self.sb(ctx, name, [128, 128]) for name in ("tri", "ones"))
        self.bank = ctx.enter_context(nc.psum_tensor("bank", [128, 8, 512], F32))

    def sb(self, ctx, name, shape, dt=F32):
        return ctx.enter_context(self.nc.sbuf_tensor(name, shape, dt))

    def branch_memory(self, ctx):
        self.yaT, self.ybT = (self.sb(ctx, name, [128, KT, T]) for name in ("yaT", "ybT"))
        self.ycT = self.sb(ctx, "ycT", [128, 2, T])

    def low_memory(self, ctx):
        self.low = self.sb(ctx, "low", [128, LOW * SLOT])

    def project_memory(self, ctx, name):
        self.x_hi, self.x_lo = (self.sb(ctx, f"{name}_{n}", [128, KT, T], R32) for n in ("x_hi", "x_lo"))
        self.w_hi, self.w_lo = (self.sb(ctx, f"{name}_{n}", [128, 2, KT, 256], R32) for n in ("w_hi", "w_lo"))
        self.w_raw = self.sb(ctx, f"{name}_w_raw", [128, 2, KT, 256])

    def mixer_memory(self, ctx, name):
        self.arena = self.sb(ctx, name + "_arena", [128, (SLOTS - LOW) * SLOT])

    def merge_memory(self, ctx):
        self.x_hi, self.x_lo, self.y_hi, self.y_lo = (self.sb(ctx, n, [128, KT, T], R32) for n in ("x_hi", "x_lo", "y_hi", "y_lo"))
        self.yc_hi, self.yc_lo = (self.sb(ctx, n, [128, 2, T], R32) for n in ("yc_hi", "yc_lo"))
        self.w_hi, self.w_lo = (self.sb(ctx, n, [128, 2, 2, KT, 128], R32) for n in ("w_hi", "w_lo"))
        self.low = None
        self.arena = self.sb(ctx, "merge_arena", [128, 4 * 2048 + 3 * HALF])

    def norm_memory(self, ctx):
        self.norm = self.sb(ctx, "norm", [128, (T // 128 + 1) * D + 2 * D + 64])
        self.wo_hi, self.wo_lo = (self.sb(ctx, n, [128, 2, KT, 512], R32) for n in ("wo_hi", "wo_lo"))
        self.mg_hi, self.mg_lo = (self.sb(ctx, n, [128, KT, T], R32) for n in ("mg_hi", "mg_lo"))

    def moe_memory(self, ctx):
        self.arena = self.sb(ctx, "moe_arena", [128, 6 * SLOT])
        self.small = self.sb(ctx, "moe_small", [128, 1048])
        self.route = self.sb(ctx, "route", [128, 2108])
        self.w2_hi, self.w2_lo = (self.sb(ctx, name, [128, 8, 1024], R32) for name in ("w2_hi", "w2_lo"))
        self.act_hi, self.act_lo = (self.sb(ctx, name, [128, 8, 128], R32) for name in ("act_hi", "act_lo"))

    def slot(self, i, n=SLOT):
        if self.low is not None:
            if i < LOW:
                return self.low[:, i * SLOT:i * SLOT + n]
            i -= LOW
        return self.arena[:, i * SLOT:i * SLOT + n]


def load_x(nc, m, t):
    with ExitStack() as ctx:
        st = Stage(nc, ctx, "x")
        s_const, s_x, s_tr, s_ev, s_ea = (st.sem(n) for n in ("const", "x", "tr", "ev", "ea"))
        xp = m.slot(0).rearrange("p (c d) -> p c d", c=NC)
        xs = m.slot(1)[0:TS, 0:D]
        block = ctx.enter_context(nc.Block())

        @block.sync
        def _(sp):
            for dst, name in ((m.ident, "c_ident"), (m.tri, "c_tri"), (m.ones, "c_ones")):
                sp.dma_start(dst[:], t[name]).then_inc(s_const, 16)
            for c in range(NC):
                sp.dma_start(xp[:, c, :], t["x_prompt"][0, c * 128:(c + 1) * 128, :]).then_inc(s_x, 16)
            sp.dma_start(xs, t["x_sample"][:, 0, :]).then_inc(s_x, 16)

        @block.tensor
        def _(pe):
            pe.wait_ge(s_const, 48)
            pe.wait_ge(s_x, 16 * (NC + 1))
            for c in range(NC):
                for h in range(2):
                    n = 2 * c + h
                    for j in range(4):
                        k = 4 * h + j
                        last = pe.transpose(m.bank[:, n, j * 128:(j + 1) * 128], xp[:, c, k * 128:(k + 1) * 128], m.ident[:])
                    last.then_inc(s_tr, 1)
            pe.wait_ge(s_ev, 1)
            for k in range(KT):
                last = pe.transpose(m.bank[:, 0, k * TS:(k + 1) * TS], xs[:, k * 128:(k + 1) * 128], m.ident[0:TS, 0:TS])
            last.then_inc(s_tr, 1)

        @block.vector
        def _(dve):
            for n in range(0, 8, 2):
                dve.wait_ge(s_tr, n + 1)
                dve.tensor_copy(m.xT[:, 0:4, n // 2 * 128:(n // 2 + 1) * 128],
                                m.bank[:, n, :].rearrange("p (j q) -> p j q", j=4)).then_inc(s_ev, 1)
            dve.wait_ge(s_tr, 9)
            dve.tensor_copy(m.xT[:, :, TP:T], m.bank[:, 0, 0:KT * TS].rearrange("p (k q) -> p k q", k=KT)).then_inc(s_ev, 1)

        @block.scalar
        def _(act):
            for n in range(1, 8, 2):
                act.wait_ge(s_tr, n + 1)
                act.copy(m.xT[:, 4:8, n // 2 * 128:(n // 2 + 1) * 128],
                         m.bank[:, n, :].rearrange("p (j q) -> p j q", j=4)).then_inc(s_ea, 1)


def project(nc, m, t, name, first, last, units):
    with ExitStack() as ctx:
        m.project_memory(ctx, name)
        st = Stage(nc, ctx, name)
        s_w = [st.sem(f"w{i}") for i in range(2)]
        s_u, s_ev, s_ea, s_hi, s_lo = (st.sem(n) for n in ("u", "ev", "ea", "hi", "lo"))
        chunks = [(c0, min(256, last - c0)) for c0 in range(first, last, 256)]
        chunk_of = [(u[1] - first) // 256 for u in units]
        last_unit = [max(i for i, c in enumerate(chunk_of) if c == k) for k in range(len(chunks))]

        order = [("x", 0), ("w", 0), ("x", 1)] + [("w", c) for c in range(1, len(chunks))]
        done = {q: i + 1 for i, q in enumerate(order)}

        def operands(kind, i):
            if kind == "x":
                return tuple(a[:, :, i * HALF:(i + 1) * HALF] for a in (m.xT, m.x_hi, m.x_lo))
            return tuple(a[:, i % 2, :, 0:chunks[i][1]] for a in (m.w_raw, m.w_hi, m.w_lo))
        block = ctx.enter_context(nc.Block())

        @block.sync
        def _(sp):
            for c, (c0, n) in enumerate(chunks):
                if c >= 2:
                    sp.wait_ge(s_lo, done[("w", c - 2)])
                sp.dma_start(m.w_raw[:, c % 2, :, 0:n], t["w_in"][0, :, c0:c0 + n].rearrange("(k p) n -> p k n", p=128))\
                    .then_inc(s_w[c % 2], 16)

        @block.tensor
        def _(pe):
            for i, (form, c0, n, a, b, _) in enumerate(units):
                c = chunk_of[i]
                off = c0 - chunks[c][0]
                pe.wait_ge(s_lo, max(done[("w", c)], done[("x", 0 if b <= HALF else 1)]))
                if i >= 8:
                    pe.wait_ge(s_ea if i % 2 else s_ev, (i - 8) // 2 + 1)
                for k in range(KT):
                    for j, (wp, xp) in enumerate(((m.w_hi, m.x_hi), (m.w_hi, m.x_lo), (m.w_lo, m.x_hi))):
                        w, x = wp[:, c % 2, k, off:off + n], xp[:, k, a:b]
                        flags = dict(start=(k == 0 and j == 0), stop=(k == KT - 1 and j == 2))
                        if form == "chan":
                            ins = pe.matmul(m.bank[0:n, i % 8, 0:b - a], w, x, **flags)
                        else:
                            ins = pe.matmul(m.bank[0:b - a, i % 8, 0:n], x, w, **flags)
                ins.then_inc(s_u, 1)

        def evacuate(eng, copy, odd, s_done, split):
            for q in order[0:3]:
                split(*q)
            for i, u in enumerate(units):
                c = chunk_of[i]
                if (i == 0 or chunk_of[i - 1] != c) and c + 1 < len(chunks):
                    if c >= 1:
                        eng.wait_ge(s_u, last_unit[c - 1] + 1)
                    split("w", c + 1)
                if i % 2 != odd:
                    continue
                eng.wait_ge(s_u, i + 1)
                for dst, rows, a, b in u[5]:
                    src = m.bank[0:rows, i % 8, a:b]
                    if len(dst.shape) == 3:
                        src = src.rearrange("p (i r) -> p i r", r=dst.shape[2])
                    ins = copy(dst, src)
                ins.then_inc(s_done, 1)

        @block.vector
        def _(dve):
            def split(kind, i):
                src, hi, lo = operands(kind, i)
                dve.wait_ge(s_hi, done[(kind, i)])
                dve.tensor_tensor(lo, src, hi.bitcast(F32), ALU.subtract).then_inc(s_lo, 1)
            evacuate(dve, dve.tensor_copy, 0, s_ev, split)

        @block.scalar
        def _(act):
            def split(kind, i):
                src, hi, lo = operands(kind, i)
                if kind == "w":
                    act.wait_ge(s_w[i % 2], 16 * (i // 2 + 1))
                act.copy(hi, src).then_inc(s_hi, 1)
            evacuate(act, act.copy, 1, s_ea, split)


def chan_units(col, dst_p, dst_s):
    return [("chan", col, 128, 0, HALF, [(dst_p[:, 0:HALF], 128, 0, HALF)]),
            ("chan", col, 128, HALF, T, [(dst_p[:, HALF:TP], 128, 0, TP - HALF), (dst_s, 128, TP - HALF, HALF)])]


def tok_units(col, n, dst):
    return [("tok", col, n, c * 128, (c + 1) * 128, [(dst(c), 128, 0, n)]) for c in range(NC)]


def mixer_a(nc, m, t, o):
    raw = m.low[:, 0:AM * 515].rearrange("p (m q) -> p m q", m=AM)
    raws = m.low[:, AM * 515:AM * 515 + AM * TS].rearrange("p (m q) -> p m q", m=AM)
    zs = m.low[:, AM * 523:AM * 523 + 64].rearrange("p (m q) -> p m q", m=KT)
    dtr = m.low[:, AM * 523 + 64:AM * 523 + 128].rearrange("p (c h) -> p c h", c=NC)
    dts_raw = m.low[0:AH, AM * 523 + 128:AM * 523 + 136]
    z = m.slot(2).rearrange("p (c d) -> p c d", c=NC)
    units = []
    for c in range(0, D, 256):
        units += tok_units(Z0 + c, 256, lambda k, c=c: z[:, k, c:c + 256])
        for j in range(2):
            units.append(("chan", Z0 + c + 128 * j, 128, TP, T, [(zs[:, c // 128 + j, :], 128, 0, TS)]))
    for i in range(AM):
        units += chan_units(XBC0 + 128 * i, raw[:, i, 3:515], raws[:, i, :])
    units += tok_units(DT0, AH, lambda k: dtr[:, k, :])
    units.append(("chan", DT0, AH, TP, T, [(dts_raw, AH, 0, TS)]))
    project(nc, m, t, "pa", Z0, BQ0, units)
    with ExitStack() as ctx:
        m.mixer_memory(ctx, "a")
        mixer_a_steps(nc, m, t, o, raw, raws, zs, dtr, dts_raw, z)


def mixer_a_steps(nc, m, t, o, raw, raws, zs, dtr, dts_raw, z):
    with ExitStack() as ctx:
        st = Stage(nc, ctx, "a")
        xc = m.arena[:, 0:AM * 512].rearrange("p (m q) -> p m q", m=AM)
        o0 = AM * 512
        par = m.arena[:, o0:o0 + AM * 29].rearrange("p (m j) -> p m j", m=AM)
        o0 += AM * 29
        xcs = m.arena[:, o0:o0 + AM * TS].rearrange("p (m q) -> p m q", m=AM)
        o0 += AM * TS
        tmps = m.arena[:, o0:o0 + AM * TS].rearrange("p (m q) -> p m q", m=AM)
        o0 += AM * TS
        stag = m.arena[:, o0:o0 + AM * 11].rearrange("p (m q) -> p m q", m=AM)
        o0 += AM * 11
        ex = m.arena[:, o0:o0 + 8 * 17].rearrange("p (m q) -> p m q", m=8)
        o0 += 8 * 17
        us = m.arena[:, o0:o0 + 64].rearrange("p (m b) -> p m b", m=8)
        o0 += 64
        ys = m.arena[:, o0:o0 + 64].rearrange("p (m b) -> p m b", m=8)
        o0 += 64
        gs = m.arena[:, o0:o0 + 64].rearrange("p (m b) -> p m b", m=8)
        o0 += 64
        ngT = m.arena[:, o0:o0 + 8]
        o0 += 8
        dsm = m.arena[0:AH, o0:o0 + 40]
        o0 += 40
        assert o0 <= 2 * SLOT
        xtok = m.slot(3).rearrange("p (c d) -> p c d", c=NC)
        xdt = m.slot(6).rearrange("p (c d) -> p c d", c=NC)
        s8 = m.slot(8)
        sc = s8[:, 0:1024].rearrange("p (i q) -> p i q", i=2 * NC)
        btok = s8[:, 1024:2048].rearrange("p (c g n) -> p c g n", c=NC, g=AG)
        stT = s8[:, 2048:3072].rearrange("p (g q) -> p g q", g=AG)
        xdd = s8[:, 3072:4096].rearrange("p (g q) -> p g q", g=AG)
        y = m.work[:, 0:1024].rearrange("p (g q) -> p g q", g=AG)
        mt = m.slot(7)[:, 0:2048].rearrange("p (i q) -> p i q", i=4)
        gn = m.slot(7)[:, 2048:3072]
        junk = m.slot(7)[:, 3072:4096]
        w0 = 1024
        dt = m.work[:, w0:w0 + 64]
        la = m.work[:, w0 + 64:w0 + 128]
        acum = m.work[:, w0 + 128:w0 + 192]
        eac = m.work[:, w0 + 192:w0 + 256]
        dec = m.work[:, w0 + 256:w0 + 320]
        etot = m.work[:, w0 + 320:w0 + 384]
        dtb = m.work[:, w0 + 384:w0 + 400]
        aneg = m.work[:, w0 + 400:w0 + 416]
        dsk = m.work[:, w0 + 416:w0 + 432]
        rs = m.work[:, w0 + 432:w0 + 440]
        tmp64 = m.work[:, w0 + 440:w0 + 504]
        dx = m.ybT[:].rearrange("p k q -> p (k q)")[:, 0:4096].rearrange("p (c d) -> p c d", c=NC)
        S0 = m.slot(0).rearrange("p (b m n) -> p b m n", b=4, m=8)
        rows = m.slot(3)[0:29, 0:ACH]
        csb = m.slot(6)[0:11, 0:ACH]
        ngrow = m.slot(6)[0:8, ACH:ACH + 128]

        s_ld, s_par, s_tp, s_tq, s_cs, s_out = (st.sem(n) for n in ("ld", "par", "tp", "tq", "cs", "out"))
        s_v, s_a = st.sem("v"), st.sem("a")
        s_conv, s_silu, s_dt1, s_dt2, s_la, s_cum = (st.sem(n) for n in ("conv", "silu", "dt1", "dt2", "la", "cum"))
        s_xt, s_xe, s_xa, s_sc, s_scm = (st.sem(n) for n in ("xt", "xe", "xa", "sc", "scm"))
        s_l, s_ld1, s_lx, s_m, s_y, s_yo, s_sd, s_xdd, s_sn = (st.sem(n) for n in
                                                             ("l", "ld1", "lx", "m", "y", "yo", "sd", "xdd", "sn"))
        s_g, s_sq, s_z, s_yn, s_yt, s_ye, s_ini = (st.sem(n) for n in ("g", "sq", "z", "yn", "yt", "ye", "ini"))
        s_cum2, s_pr, s_var, s_rstd, s_pad, s_tap, s_dx, s_s0 = (st.sem(n) for n in ("cum2", "pr", "var", "rstd", "pad", "tap", "dx", "s0"))
        block = ctx.enter_context(nc.Block())

        @block.gpsimd
        def _(pool):
            pool.wait_ge(s_ld, 16 * 8)
            pool.wait_ge(s_xa, 12)
            pool.wait_ge(s_pr, 1)
            for c in range(NC):
                for g in range(AG):
                    n = 2 * c + g
                    if n >= 2:
                        pool.wait_ge(s_sd, n - 1)
                    pool.tensor_tensor(xdd[:, g, :].rearrange("p (h q) -> p h q", h=8),
                                       xdt[:, c, g * 512:(g + 1) * 512].rearrange("p (h q) -> p h q", h=8),
                                       bc(dec[:, c * AH + 8 * g:c * AH + 8 * g + 8], AP_), ALU.mult).then_inc(s_xdd, 1)
                    if g == 0:
                        pool.tensor_tensor(dx[:, c, :].rearrange("p (h q) -> p h q", h=AH), xtok[:, c, :].rearrange("p (h q) -> p h q", h=AH),
                                           bc(dsk, AP_), ALU.mult).then_inc(s_dx, 1)

        @block.sync
        def _(sp):
            sp.dma_start(rows[0:24, :], t["state_conv"][0].rearrange("b j c -> (b j) c")).then_inc(s_ld, 16)
            sp.dma_start(rows[24:28, :], t["conv_w"][0]).then_inc(s_ld, 16)
            sp.dma_start(rows[28:29, :], t["conv_b"]).then_inc(s_ld, 16)
            sp.dma_start(dtb, t["dt_bias"][0].partition_broadcast(128)).then_inc(s_ld, 16)
            sp.dma_start(aneg, t["a_log"][0].partition_broadcast(128)).then_inc(s_ld, 16)
            sp.dma_start(dsk, t["d_skip"][0].partition_broadcast(128)).then_inc(s_ld, 16)
            sp.dma_start(gn, t["ssm_norm_g"][0].partition_broadcast(128)).then_inc(s_ld, 16)
            sp.dma_start(ngrow, t["ssm_norm_g"][0].rearrange("(m p) -> m p", p=128)).then_inc(s_ld, 16)
            sp.dma_start(o["conv_s"][0, :, 0:2, :], t["state_conv"][0, :, 1:3, :]).then_inc(s_out, 16)
            sp.wait_ge(s_cs, 1)
            sp.dma_start(o["conv_p"][0, 0], csb[0:3, :]).then_inc(s_out, 16)
            sp.dma_start(o["conv_s"][0, :, 2, :], csb[3:11, :]).then_inc(s_out, 16)
            sp.wait_ge(s_out, 48)
            sp.wait_ge(s_conv, AM)
            sp.wait_ge(s_cs, 1)
            for b in range(4):
                sp.dma_start(S0[:, b], t["state_ssm"][0, b].rearrange("(m h) q n -> (h q) m n", h=2)).then_inc(s_s0, 16)
            sp.wait_ge(s_s0, 64)

        @block.tensor
        def _(pe):
            pe.wait_ge(s_ld, 16 * 8)
            for i in range(AM):
                last = pe.transpose(m.bank[:, 0, i * 29:(i + 1) * 29], rows[:, i * 128:(i + 1) * 128], m.ident[0:29, 0:29])
            last = pe.transpose(m.bank[:, 0, 400:408], ngrow, m.ident[0:8, 0:8])
            last.then_inc(s_tp, 1)
            pe.wait_ge(s_par, 1)
            for i in range(AM):
                last = pe.transpose(m.bank[0:11, 1 + i // 4, (i % 4) * 128:(i % 4 + 1) * 128], stag[:, i, :], m.ident[:])
            last.then_inc(s_tp, 1)
            pe.wait_ge(s_la, 1)
            pe.matmul(m.bank[:, 4, 0:64], m.tri[:], la, start=True, stop=True)
            pe.matmul(m.bank[:, 4, 64:128], m.ones[:], la, start=True, stop=True).then_inc(s_cum, 1)
            pe.wait_ge(s_silu, AM)
            for c in range(NC):
                for h in range(3):
                    n = 3 * c + h
                    b = 5 + n % 3
                    if n >= 3:
                        pe.wait_ge(s_xe, n - 2)
                    for j in range(4 if h < 2 else 2):
                        last = pe.transpose(m.bank[:, b, j * 128:(j + 1) * 128],
                                            xc[:, 4 * h + j, c * 128:(c + 1) * 128], m.ident[:])
                    last.then_inc(s_xt, 1)
            pe.wait_ge(s_cs, 1)
            for c in range(NC):
                for g in range(AG):
                    n = 2 * c + g
                    last = pe.matmul(m.bank[:, 2 + n // 4, (n % 4) * 128:(n % 4 + 1) * 128],
                                     xc[:, 8 + g, c * 128:(c + 1) * 128], xc[:, 10 + g, c * 128:(c + 1) * 128],
                                     start=True, stop=True)
            last.then_inc(s_sc, 1)
            pe.wait_ge(s_scm, 2)
            pe.wait_ge(s_xa, 12)
            for c in range(NC):
                for g in range(AG):
                    n = 2 * c + g
                    for q in range(2):
                        i = 2 * n + q
                        if i >= 2:
                            pe.wait_ge(s_ld1, i - 1)
                        for j in range(4):
                            h = 8 * g + 4 * q + j
                            last = pe.matmul(m.bank[:, i % 2, j * 128:(j + 1) * 128],
                                             la[:, c * AH + h:c * AH + h + 1].broadcast_to([128, 128]), m.tri[:],
                                             start=True, stop=True)
                        last.then_inc(s_l, 1)
                    if n >= 2:
                        pe.wait_ge(s_yn, n - 1)
                    if n >= 2:
                        pe.wait_ge(s_sn, n - 1)
                    pe.matmul(m.bank[:, 4 + n % 2, :], xc[:, 10 + g, c * 128:(c + 1) * 128], stT[:, g, :],
                              start=True, stop=True).then_inc(s_yo, 1)
                    for q in range(2):
                        i = 2 * n + q
                        pe.wait_ge(s_m, i + 1)
                        for j in range(4):
                            h = 4 * q + j
                            last = pe.matmul(m.bank[:, 2 + n % 2, h * 64:(h + 1) * 64], mt[:, 2 + i % 2, j * 128:(j + 1) * 128],
                                             xdt[:, c, (8 * g + h) * 64:(8 * g + h + 1) * 64], start=True, stop=True)
                    last.then_inc(s_y, 1)
                    pe.wait_ge(s_xdd, n + 1)
                    if n >= 1:
                        pe.wait_ge(s_sn, n)
                    pe.matmul(m.bank[:, 6, :], btok[:, c, g, :], xdd[:, g, :], start=True, stop=True).then_inc(s_sd, 1)
                pe.wait_ge(s_yn, 2 * c + 2)
                for h in range(2):
                    if 2 * c + h >= 1:
                        pe.wait_ge(s_ye, 2 * c + h)
                    for j in range(4):
                        last = pe.transpose(m.bank[:, 7, j * 128:(j + 1) * 128], y[:, h, j * 128:(j + 1) * 128], m.ident[:])
                    last.then_inc(s_yt, 1)

        @block.vector
        def _(dve):
            link = linker(dve, s_v)
            dve.wait_ge(s_ld, 16 * 8)
            dve.memset(raw[:, :, 0:3], 0.0).then_inc(s_pad, 1)
            link(dve.memset(stT, 0.0))
            dve.wait_ge(s_tp, 1)
            dve.tensor_copy(par, m.bank[:, 0, 0:AM * 29].rearrange("p (m j) -> p m j", m=AM)).then_inc(s_pad, 1)
            dve.wait_ge(s_pad, 2)
            link(dve.tensor_copy(ngT, m.bank[:, 0, 400:408]))
            link(dve.tensor_copy(stag[:, :, 0:3], raw[:, :, 512:515]))
            dve.tensor_copy(stag[:, :, 3:11], raws).then_inc(s_par, 1)
            for i in range(AM):
                dve.wait_ge(s_tap, i + 1)
                for j in range(1, 4):
                    ins = dve.scalar_tensor_tensor(xc[:, i, :], raw[:, i, j:j + 512], par[:, i, 24 + j:25 + j], xc[:, i, :],
                                                   ALU.mult, ALU.add)
                    if j < 3:
                        link(ins)
                ins.then_inc(s_conv, 1)
            link(dve.tensor_tensor(dt.rearrange("p (c h) -> p c h", c=NC), dtr, bmid(dtb, NC), ALU.add))
            link(dve.scalar_tensor_tensor(tmp64, dt, -1.0, dt, ALU.mult, ALU.max))
            dve.tensor_scalar(dt, dt, 0.0, None, ALU.max).then_inc(s_dt1, 1)
            dve.wait_ge(s_dt2, 1)
            link(dve.tensor_tensor(dt, dt, tmp64, ALU.add))
            dve.scalar_tensor_tensor(la.rearrange("p (c h) -> p c h", c=NC), dt.rearrange("p (c h) -> p c h", c=NC), -1.0,
                                     bmid(aneg, NC), ALU.mult, ALU.mult).then_inc(s_la, 1)
            dve.wait_ge(s_cum, 1)
            link(dve.tensor_copy(acum, m.bank[:, 4, 0:64]))
            link(dve.tensor_tensor(dec, m.bank[:, 4, 64:128], acum, ALU.subtract))
            dve.tensor_scalar(etot, m.bank[:, 4, 64:128], 1.0, None, ALU.mult).then_inc(s_cum2, 1)
            dve.wait_ge(s_tp, 2)
            dve.tensor_copy(csb, m.bank[0:11, 1:4, :]).then_inc(s_cs, 1)
            for n in range(12):
                c, h = divmod(n, 3)
                dve.wait_ge(s_xt, n + 1)
                src = m.bank[:, 5 + n % 3, :]
                if h < 2:
                    dve.tensor_copy(xtok[:, c, h * 512:(h + 1) * 512], src).then_inc(s_xe, 1)
                else:
                    dve.tensor_copy(btok[:, c, :, :], src[:, 0:256].rearrange("p (g n) -> p g n", g=AG)).then_inc(s_xe, 1)
            dve.wait_ge(s_xe, 12)
            dve.wait_ge(s_out, 48)
            for c in range(NC):
                dve.tensor_tensor(xdt[:, c, :].rearrange("p (h q) -> p h q", h=AH), xtok[:, c, :].rearrange("p (h q) -> p h q", h=AH),
                                  bc(dt[:, c * AH:(c + 1) * AH], AP_), ALU.mult).then_inc(s_xa, 3)
            dve.wait_ge(s_sc, 1)
            for h in range(2):
                dve.tensor_tensor(sc[:, 4 * h:4 * h + 4, :], m.bank[:, 2 + h, :].rearrange("p (i q) -> p i q", i=4),
                                  bmid(m.tri[:], 4), ALU.mult).then_inc(s_scm, 1)
            dve.wait_ge(s_scm, 2)
            dve.wait_ge(s_xa, 12)
            dve.wait_ge(s_pr, 1)
            for c in range(NC):
                for g in range(AG):
                    n = 2 * c + g
                    for q in range(2):
                        i = 2 * n + q
                        lt, mm = mt[:, i % 2, :].rearrange("p (j q) -> p j q", j=4), mt[:, 2 + i % 2, :].rearrange("p (j q) -> p j q", j=4)
                        dve.wait_ge(s_lx, i + 1)
                        if i >= 2:
                            dve.wait_ge(s_y, (i - 2) // 2 + 1)
                        dve.tensor_tensor(mm, lt, bmid(sc[:, n, :], 4), ALU.mult).then_inc(s_m, 1)
                    yv = y[:, g, :].rearrange("p (h q) -> p h q", h=8)
                    if n >= 2:
                        dve.wait_ge(s_yt, 2 * c)
                    dve.wait_ge(s_yo, n + 1)
                    link(dve.tensor_tensor(yv, m.bank[:, 4 + n % 2, :].rearrange("p (h q) -> p h q", h=8),
                                           bc(eac[:, c * AH + 8 * g:c * AH + 8 * g + 8], AP_), ALU.mult))
                    dve.wait_ge(s_y, n + 1)
                    link(dve.tensor_tensor(y[:, g, :], y[:, g, :], m.bank[:, 2 + n % 2, :], ALU.add))
                    jk = junk[:, g * 512:(g + 1) * 512]
                    dve.wait_ge(s_dx, c + 1)
                    link(dve.tensor_tensor(y[:, g, :], y[:, g, :], dx[:, c, g * 512:(g + 1) * 512], ALU.add))
                    dve.wait_ge(s_z, c + 1)
                    link(dve.tensor_tensor(y[:, g, :], y[:, g, :], z[:, c, g * 512:(g + 1) * 512], ALU.mult))
                    link(dve.tensor_tensor(jk, y[:, g, :], y[:, g, :], ALU.mult))
                    link(dve.tensor_reduce(rs[:, g:g + 1], jk, AX.X, ALU.add))
                    dve.tensor_scalar(rs[:, g:g + 1], rs[:, g:g + 1], 1.0 / 512, EPS, ALU.mult, ALU.add).then_inc(s_var, 1)
                    dve.wait_ge(s_rstd, n + 1)
                    last = dve.scalar_tensor_tensor(y[:, g, :], y[:, g, :], rs[:, g:g + 1], gn[:, g * 512:(g + 1) * 512],
                                                    ALU.mult, ALU.mult)
                    last.then_inc(s_yn, 1)
                    dve.wait_ge(s_yn, n + 1)
                    dve.wait_ge(s_sd, n + 1)
                    sv = stT[:, g, :].rearrange("p (h q) -> p h q", h=8)
                    link(dve.tensor_tensor(sv, sv, bc(etot[:, c * AH + 8 * g:c * AH + 8 * g + 8], AP_), ALU.mult))
                    dve.tensor_tensor(stT[:, g, :], stT[:, g, :], m.bank[:, 6, :], ALU.add).then_inc(s_sn, 1)
                    dve.wait_ge(s_sn, n + 1)

        @block.scalar
        def _(act):
            link = linker(act, s_a)
            act.wait_ge(s_pad, 2)
            for i in range(AM):
                act.activation(xc[:, i, :], raw[:, i, 0:512], ACT.Identity, scale=par[:, i, 24:25], bias=par[:, i, 28:29])\
                    .then_inc(s_tap, 1)
            for i in range(AM):
                act.wait_ge(s_conv, i + 1)
                act.activation(xc[:, i, :], xc[:, i, :], ACT.Silu).then_inc(s_silu, 1)
            for c in range(NC):
                act.activation(z[:, c, :], z[:, c, :], ACT.Silu).then_inc(s_z, 1)
            act.wait_ge(s_dt1, 1)
            link(act.activation(tmp64, tmp64, ACT.Exp, scale=-1.0))
            link(act.activation(tmp64, tmp64, ACT.Ln, bias=1.0))
            act.wait_ge(s_ld, 16 * 8)
            act.activation(aneg, aneg, ACT.Exp).then_inc(s_dt2, 1)
            act.wait_ge(s_cum2, 1)
            link(act.activation(eac, acum, ACT.Exp))
            link(act.activation(dec, dec, ACT.Exp))
            act.activation(etot, etot, ACT.Exp).then_inc(s_pr, 1)
            for i in range(4 * NC):
                c, hs = i // 4, 4 * (i % 4)
                act.wait_ge(s_l, i + 1)
                if i >= 2:
                    act.wait_ge(s_m, i - 1)
                for j in range(4):
                    ins = act.activation(mt[:, i % 2, j * 128:(j + 1) * 128], m.bank[:, i % 2, j * 128:(j + 1) * 128], ACT.Relu,
                                         scale=-1.0, bias=acum[:, c * AH + hs + j:c * AH + hs + j + 1])
                ins.then_inc(s_ld1, 1)
                act.wait_ge(s_ld1, i + 1)
                act.activation(mt[:, i % 2, :], mt[:, i % 2, :], ACT.Exp, scale=-1.0).then_inc(s_lx, 1)
                if i % 2 == 1:
                    act.wait_ge(s_var, i // 2 + 1)
                    r = rs[:, i // 2 % 2:i // 2 % 2 + 1]
                    link(act.activation(r, r, ACT.Ln))
                    act.activation(r, r, ACT.Exp, scale=-0.5).then_inc(s_rstd, 1)
                if i % 4 == 3:
                    c = i // 4
                    for h in range(2):
                        act.wait_ge(s_yt, 2 * c + h + 1)
                        act.copy(m.yaT[:, 4 * h:4 * h + 4, c * 128:(c + 1) * 128],
                                 m.bank[:, 7, :].rearrange("p (j q) -> p j q", j=4)).then_inc(s_ye, 1)

    with ExitStack() as ctx:
        st = Stage(nc, ctx, "as")
        S = [m.slot(i).rearrange("p (b m n) -> p b m n", b=4, m=8) for i in (0, 6)]
        tmp = m.slot(3)
        bcs = m.ybT[:].rearrange("p k q -> p (k q)")[:, 0:4096].rearrange("p (i b n) -> p i b n", i=4, b=TS)
        exps = m.slot(2)[0:AH, 0:1024]
        so = m.slot(2)[:, 1024:2048]
        g64 = m.slot(2)[:, 2048:2112].rearrange("p (m b) -> p m b", m=8)
        gr = m.slot(2)[:, 2112:2128].rearrange("p (g b) -> p g b", g=AG)
        s_ld, s_st, s_v, s_a, s_c, s_xs, s_e, s_dd, s_ex, s_exe, s_bb, s_be, s_sn, s_sq, s_sr, s_tr, s_so, s_out, s_d2, s_sp = (
            st.sem(n) for n in ("ld", "st", "v", "a", "c", "xs", "e", "dd", "ex", "exe", "bb", "be", "sn", "sq", "sr",
                                "tr", "so", "out", "d2", "sp"))
        s_var, s_rstd, s_dec = st.sem("var"), st.sem("rstd"), st.sem("dec")
        block = ctx.enter_context(nc.Block())

        @block.gpsimd
        def _(pool):
            pool.wait_ge(s_exe, 1)
            for hb in range(2):
                if hb:
                    pool.wait_ge(s_st, 64)
                pool.tensor_tensor(S[hb], S[hb], bc(ex[:, :, 8 + 4 * hb:12 + 4 * hb].rearrange("p m b -> p b m"), 128), ALU.mult)\
                    .then_inc(s_dec, 1)

        @block.sync
        def _(sp):
            sp.dma_start(exps, t["c_headexp"]).then_inc(s_ld, 16)
            for i, n in enumerate(("dt_bias", "a_log", "d_skip")):
                c = (17, 18, 16)[i]
                sp.dma_start(dsm[:, c:c + 1], t[n][0].rearrange("(h i) -> h i", i=1)).then_inc(s_ld, 16)
            for b in range(4):
                sp.dma_start(S[1][:, b], t["state_ssm"][0, 4 + b].rearrange("(m h) q n -> (h q) m n", h=2)).then_inc(s_st, 16)
            sp.wait_ge(s_so, 1)
            sp.dma_start(o["ssm_p"][0, 0].rearrange("(m h) q n -> (h q) m n", h=2), so.rearrange("p (m n) -> p m n", m=8))\
                .then_inc(s_out, 16)
            for b in range(TS):
                sp.wait_ge(s_sn, b // 4 + 1)
                sp.dma_start(o["ssm_s"][0, b].rearrange("(m h) q n -> (h q) m n", h=2), S[b // 4][:, b % 4]).then_inc(s_out, 16)
            sp.wait_ge(s_out, 16 * 9)

        @block.tensor
        def _(pe):
            for i in range(8):
                last = pe.transpose(m.bank[:, i // 4, (i % 4) * 128:(i % 4 + 1) * 128],
                                    stT[:, i // 4, (i % 4) * 128:(i % 4 + 1) * 128], m.ident[:])
            last.then_inc(s_tr, 1)
            pe.wait_ge(s_dd, 1)
            for i in range(8):
                last = pe.matmul(m.bank[:, 2, 17 * i:17 * i + 17], exps[:, i * 128:(i + 1) * 128], dsm[:, 0:17], start=True, stop=True)
            last.then_inc(s_ex, 1)
            pe.wait_ge(s_xs, 1)
            pe.wait_ge(s_so, 1)
            pe.wait_ge(s_exe, 1)
            for i in range(4):
                for b in range(TS):
                    last = pe.matmul(m.bank[:, 2 * i + b // 4, b % 4 * 128:(b % 4 + 1) * 128], xcs[:, 8 + i, b:b + 1].broadcast_to([128, 128]),
                                     m.ident[:], start=True, stop=True)
                last.then_inc(s_bb, 1)
            pe.wait_ge(s_sq, 1)
            pe.wait_ge(s_be, 4)
            pe.matmul(m.bank[:, 0, 0:64], m.ones[:], g64.rearrange("p m b -> p (m b)"), start=True, stop=True).then_inc(s_sr, 1)

        @block.vector
        def _(dve):
            link = linker(dve, s_v)
            dve.wait_ge(s_tr, 1)
            dve.tensor_copy(so.rearrange("p (b q) -> p b q", b=2), m.bank[:, 0:2, :]).then_inc(s_so, 1)
            dve.wait_ge(s_ld, 64)
            link(dve.tensor_tensor(xcs, raws, bc(par[:, :, 27], TS), ALU.mult))
            link(dve.tensor_tensor(xcs, xcs, bc(par[:, :, 28], TS), ALU.add))
            for j in range(3):
                link(dve.tensor_tensor(tmps, par[:, :, j:24:3], bc(par[:, :, 24 + j], TS), ALU.mult))
                link(dve.tensor_tensor(xcs, xcs, tmps, ALU.add))
            dve.tensor_scalar(dsm[:, 0:8], dts_raw, dsm[:, 17:18], None, ALU.add).then_inc(s_c, 1)
            dve.wait_ge(s_c, 1)
            link(dve.scalar_tensor_tensor(dsm[:, 24:32], dsm[:, 0:8], -1.0, dsm[:, 0:8], ALU.mult, ALU.max))
            dve.tensor_scalar(dsm[:, 0:8], dsm[:, 0:8], 0.0, None, ALU.max).then_inc(s_c, 1)
            dve.wait_ge(s_e, 1)
            link(dve.tensor_tensor(dsm[:, 0:8], dsm[:, 0:8], dsm[:, 24:32], ALU.add))
            dve.tensor_scalar(dsm[:, 8:16], dsm[:, 0:8], dsm[:, 18:19], -1.0, ALU.mult, ALU.mult).then_inc(s_d2, 1)
            dve.wait_ge(s_xs, 1)
            dve.wait_ge(s_ex, 1)
            dve.tensor_copy(ex, m.bank[:, 2, 0:136].rearrange("p (m q) -> p m q", m=8)).then_inc(s_exe, 1)
            dve.wait_ge(s_exe, 1)
            link(dve.tensor_tensor(us, xcs[:, 0:8, :], ex[:, :, 0:8], ALU.mult))
            dve.wait_ge(s_be, 2)
            for hb in range(2):
                bs = slice(4 * hb, 4 * hb + 4)
                tv = tmp.rearrange("p (b m n) -> p b m n", b=4, m=8)
                for b in range(4):
                    for g in range(AG):
                        gm = slice(4 * g, 4 * g + 4)
                        dve.tensor_tensor(tv[:, b, gm, :], bc(us[:, gm, 4 * hb + b], 128), bmid(bcs[:, g, 4 * hb + b, :], 4), ALU.mult)\
                            .then_inc(s_sp, 1)
                dve.wait_ge(s_sp, 16 * hb + 8)
                dve.wait_ge(s_dec, hb + 1)
                dve.tensor_tensor(S[hb], S[hb], tv, ALU.add).then_inc(s_sn, 1)
                dve.wait_ge(s_sn, hb + 1)
                dve.wait_ge(s_be, 4)
                for b in range(4):
                    for g in range(AG):
                        gm = slice(4 * g, 4 * g + 4)
                        dve.tensor_tensor(tv[:, b, gm, :], S[hb][:, b, gm, :], bmid(bcs[:, 2 + g, 4 * hb + b, :], 4), ALU.mult)\
                            .then_inc(s_sp, 1)
                dve.wait_ge(s_sp, 16 * hb + 16)
                link(dve.tensor_reduce(ys[:, :, bs].rearrange("p m b -> p b m"), tv, AX.X, ALU.add))
            link(dve.tensor_tensor(us, xcs[:, 0:8, :], bc(ex[:, :, 16], TS), ALU.mult))
            link(dve.tensor_tensor(ys, ys, us, ALU.add))
            link(dve.tensor_tensor(ys, ys, zs, ALU.mult))
            dve.tensor_tensor(g64, ys, ys, ALU.mult).then_inc(s_sq, 1)
            dve.wait_ge(s_sr, 1)
            link(dve.tensor_reduce(gr, m.bank[:, 0, 0:64].rearrange("p (g m b) -> p g b m", g=AG, m=4), AX.X, ALU.add))
            dve.tensor_scalar(gr, gr, 1.0 / 512, EPS, ALU.mult, ALU.add).then_inc(s_var, 1)
            dve.wait_ge(s_rstd, 1)
            for g in range(AG):
                gm = slice(4 * g, 4 * g + 4)
                link(dve.tensor_tensor(ys[:, gm, :], ys[:, gm, :], bmid(gr[:, g, :], 4), ALU.mult))
            link(dve.tensor_tensor(m.yaT[:, :, TP:T], ys, bc(ngT, TS), ALU.mult))

        @block.scalar
        def _(act):
            link = linker(act, s_a)
            act.wait_ge(s_c, 1)
            link(act.activation(zs, zs, ACT.Silu))
            act.activation(xcs, xcs, ACT.Silu).then_inc(s_xs, 1)
            act.wait_ge(s_c, 2)
            link(act.activation(dsm[:, 24:32], dsm[:, 24:32], ACT.Exp, scale=-1.0))
            link(act.activation(dsm[:, 24:32], dsm[:, 24:32], ACT.Ln, bias=1.0))
            act.activation(dsm[:, 18:19], dsm[:, 18:19], ACT.Exp).then_inc(s_e, 1)
            act.wait_ge(s_d2, 1)
            act.activation(dsm[:, 8:16], dsm[:, 8:16], ACT.Exp).then_inc(s_dd, 1)
            for i in range(4):
                act.wait_ge(s_bb, i + 1)
                act.copy(bcs[:, i].rearrange("p (a b) n -> p a (b n)", a=2), m.bank[:, 2 * i:2 * i + 2, :]).then_inc(s_be, 1)
            act.wait_ge(s_var, 1)
            link(act.activation(gr, gr, ACT.Ln))
            act.activation(gr, gr, ACT.Exp, scale=-0.5).then_inc(s_rstd, 1)


def mixer_b(nc, m, t, o):
    q, v, g = m.slot(0), m.slot(2).rearrange("p (c d) -> p c d", c=NC), m.slot(3).rearrange("p (c d) -> p c d", c=NC)
    f = m.slot(1)
    qs = m.work[:, 0:64].rearrange("p (h b) -> p h b", h=BH)
    fs = m.work[:, 64:128].rearrange("p (h b) -> p h b", h=BH)
    gs = m.work[:, 128:192].rearrange("p (h b) -> p h b", h=BH)
    vs = m.work[0:TS, 192:1216]
    units = []
    for c0, dp, ds in ((BQ0, q, qs), (BF0, f, fs)):
        for h in range(BH):
            units += chan_units(c0 + 128 * h, dp[:, h * 512:(h + 1) * 512], ds[:, h, :])
    for c in range(0, D, 256):
        units += tok_units(BI0 + c, 256, lambda k, c=c: v[:, k, c:c + 256])
        units.append(("tok", BI0 + c, 256, TP, T, [(vs[:, c:c + 256], TS, 0, 256)]))
    for c in range(0, D, 256):
        units += tok_units(BG0 + c, 256, lambda k, c=c: g[:, k, c:c + 256])
        for j in range(2):
            units.append(("chan", BG0 + c + 128 * j, 128, TP, T, [(gs[:, c // 128 + j, :], 128, 0, TS)]))
    project(nc, m, t, "pb", BQ0, CQ0, units)
    with ExitStack() as ctx:
        m.mixer_memory(ctx, "b")
        mixer_b_steps(nc, m, t, o, q, f, v, g, qs, fs, gs, vs)


def mixer_b_steps(nc, m, t, o, q, f, v, g, qs, fs, gs, vs):
    lb = m.work[:, 1216:1224]
    oml = m.work[:, 1224:1232]
    ng = m.work[:, 1232:1233]
    KSC = BK ** -0.5
    with ExitStack() as ctx:
        st = Stage(nc, ctx, "b")
        W, b, k, kW, qW = m.slot(1), m.slot(4), m.slot(5), m.slot(6), m.slot(7)
        att = m.slot(8).rearrange("p (i q) -> p i q", i=BH * NC)
        Ss = m.arena[:, 0:2 * SLOT].rearrange("p (b h v) -> p b h v", b=TS, h=BH)
        gnr = m.slot(6)[:, 0:128]
        reset = m.slot(8)[:, 0:512]
        lbr = m.slot(8)[0:8, 512:640]
        masks = m.ycT[:].rearrange("p k q -> p (k q)")[:, 0:896].bitcast(U32).rearrange("p (l q) -> p l q", l=len(LEVELS))
        kdt = m.slot(0).rearrange("p (i q) -> p i q", i=BH * NC)
        S = m.slot(1)[:, 0:1024]
        sq = m.slot(1)[:, 1024:2048].rearrange("p (i q) -> p i q", i=2)
        y = m.slot(1)[:, 2048:3072].rearrange("p (i q) -> p i q", i=2)
        ebl = m.work[:, 1240:1272]
        rs = m.work[:, 1272:1280].rearrange("p (i h) -> p i h", i=2)
        e8 = m.work[:, 1280:1288]
        (s_ld, s_mk, s_lt, s_v, s_a, s_p, s_lb, s_le, s_sig, s_F, s_ln, s_k, s_z, s_g, s_sub, s_exp, s_mul, s_at, s_pr, s_b0) = (
            st.sem(n) for n in ("ld", "mk", "lt", "v", "a", "p", "lb", "le", "sig", "F", "ln", "k", "z", "g", "sub", "exp",
                                "mul", "at", "pr", "b0"))
        (s_e2, s_q2, s_kt, s_ke, s_o, s_S, s_Sd, s_sq, s_var, s_rstd, s_y, s_yt, s_ye, s_oe) = (
            st.sem(n) for n in ("e2", "q2", "kt", "ke", "o", "S", "Sd", "sq", "var", "rstd", "y", "yt", "ye", "oe"))
        s_ss = st.sem("ss")
        nl = len(LEVELS)
        steps = [(hg, lv) for hg in range(2) for lv in range(nl)]
        block = ctx.enter_context(nc.Block())

        def transposes(pe, n):
            pe.wait_ge(s_y, n + 1)
            if n >= 2:
                pe.wait_ge(s_ye, n - 1)
            for j in range(4):
                last = pe.transpose(m.bank[:, 4 + n % 2, j * 128:(j + 1) * 128], y[:, n % 2, j * 128:(j + 1) * 128], m.ident[:])
            last.then_inc(s_yt, 1)

        def store_y(act, n):
            c, hg = divmod(n, 2)
            act.wait_ge(s_yt, n + 1)
            act.copy(m.ybT[:, 4 * hg:4 * hg + 4, c * 128:(c + 1) * 128],
                     m.bank[:, 4 + n % 2, :].rearrange("p (j q) -> p j q", j=4)).then_inc(s_ye, 1)

        def halves(x, z):
            v3 = x.rearrange("p (n z) -> p n z", z=z)
            return v3[:, :, 0:z // 2], v3[:, :, z // 2:z]

        @block.sync
        def _(sp):
            sp.dma_start(masks, t["c_masks"]).then_inc(s_mk, 16)
            sp.dma_start(reset, t["c_reset"][0].partition_broadcast(128)).then_inc(s_ld, 16)
            sp.dma_start(lbr, t["hgrn_lb"][0].rearrange("(h p) -> h p", p=128)).then_inc(s_ld, 16)
            sp.dma_start(gnr, t["hgrn_norm_g"][0].partition_broadcast(128)).then_inc(s_ld, 16)
            sp.dma_start(ng, t["hgrn_norm_g"][0].rearrange("(p i) -> p i", i=1)).then_inc(s_ld, 16)
            sp.wait_ge(s_q2, 2)
            sp.wait_ge(s_e2, 3)
            for bb in range(TS):
                sp.dma_start(Ss[:, bb], t["state_hgrn"][0, bb].rearrange("h k v -> k h v")).then_inc(s_ss, 16)
            sp.wait_ge(s_ss, 16 * TS)

        @block.gpsimd
        def _(pool):
            pool.wait_ge(s_g, 1)
            pool.wait_ge(s_ld, 64)
            pool.tensor_tensor(m.slot(3).rearrange("p (i q) -> p i q", q=128), m.slot(3).rearrange("p (i q) -> p i q", q=128),
                               bmid(gnr, 32), ALU.mult).then_inc(s_p, 1)
            pool.wait_ge(s_p, 1)
            pool.memset(kW, 0.0).then_inc(s_z, 1)
            pool.memset(qW, 0.0).then_inc(s_z, 1)
            pool.wait_ge(s_b0, 1)
            for n, (hg, lv) in enumerate(steps):
                if n >= 2:
                    pool.wait_ge(s_mul, n - 1)
                z = LEVELS[lv]
                bl, br = halves(b[:, hg * 2048:(hg + 1) * 2048], z)
                wl, wr = halves(W[:, (n % 2) * 2048:(n % 2 + 1) * 2048], z)
                r = bl[:, :, z // 2 - 1:z // 2].broadcast_to([128, 2048 // z, z // 2])
                pool.tensor_tensor(wl, r, bl, ALU.subtract)
                pool.tensor_tensor(wr, br, r, ALU.subtract).then_inc(s_sub, 1)

        @block.tensor
        def _(pe):
            pe.wait_ge(s_ld, 64)
            pe.transpose(m.bank[:, 7, 0:8], lbr, m.ident[0:8, 0:8]).then_inc(s_lt, 1)
            pe.wait_ge(s_k, 1)
            for hg in range(2):
                for i in range(16):
                    c0 = hg * 2048 + i * 128
                    last = pe.matmul(m.bank[:, 4 * hg + i // 4, (i % 4) * 128:(i % 4 + 1) * 128], k[:, c0:c0 + 128], q[:, c0:c0 + 128],
                                     start=True, stop=True)
                last.then_inc(s_at, 1)
            for n, (hg, lv) in enumerate(steps):
                pe.wait_ge(s_mul, n + 1)
                pe.wait_ge(s_pr, n + 1)
                for i in range(16):
                    c0 = (n % 2) * 2048 + i * 128
                    last = pe.matmul(m.bank[:, 4 * (n % 2) + i // 4, (i % 4) * 128:(i % 4 + 1) * 128], kW[:, c0:c0 + 128],
                                     qW[:, c0:c0 + 128], start=True, stop=True)
                last.then_inc(s_at, 1)
            pe.wait_ge(s_q2, 2)
            pe.wait_ge(s_pr, 2 * nl + 2)
            for n in range(8):
                for j in range(4):
                    i = 4 * n + j
                    last = pe.transpose(m.bank[:, n, j * 128:(j + 1) * 128], kW[:, i * 128:(i + 1) * 128], m.ident[:])
                last.then_inc(s_kt, 1)
            pe.wait_ge(s_ke, 8)
            for c in range(NC):
                for hg in range(2):
                    n = 2 * c + hg
                    if n >= 2:
                        pe.wait_ge(s_y, n - 1)
                    if c > 0:
                        pe.wait_ge(s_Sd, n - 1)
                    for j in range(4):
                        h = 4 * hg + j
                        i = h * NC + c
                        out = m.bank[:, n % 2, j * 128:(j + 1) * 128]
                        vv = v[:, c, h * 128:(h + 1) * 128]
                        last = pe.matmul(out, att[:, i, :], vv, start=True, stop=(c == 0))
                        if c > 0:
                            last = pe.matmul(out, qW[:, i * 128:(i + 1) * 128], S[:, h * 128:(h + 1) * 128], start=False, stop=True)
                    last.then_inc(s_o, 1)
                    for j in range(4):
                        h = 4 * hg + j
                        last = pe.matmul(m.bank[:, 2 + n % 2, j * 128:(j + 1) * 128], kdt[:, h * NC + c, :], v[:, c, h * 128:(h + 1) * 128],
                                         start=True, stop=True)
                    last.then_inc(s_S, 1)
                    if n >= 1:
                        transposes(pe, n - 1)
            transposes(pe, 2 * NC - 1)

        @block.vector
        def _(dve):
            link = linker(dve, s_v)
            dve.wait_ge(s_lt, 1)
            link(dve.tensor_copy(lb, m.bank[:, 7, 0:8]))
            dve.tensor_tensor(e8, lb, lb, ALU.subtract).then_inc(s_lb, 1)
            dve.wait_ge(s_le, 1)
            link(dve.reciprocal(oml, e8))
            link(dve.tensor_tensor(e8, e8, oml, ALU.mult))
            link(dve.tensor_tensor(lb, e8, e8, ALU.subtract))
            link(dve.tensor_scalar(oml, lb, -1.0, 1.0, ALU.mult, ALU.add))
            dve.wait_ge(s_sig, 1)
            for h in range(BH):
                c = slice(h * 512, (h + 1) * 512)
                link(dve.tensor_scalar(f[:, c], f[:, c], oml[:, h:h + 1], lb[:, h:h + 1], ALU.mult, ALU.add))
            dve.tensor_scalar(f, f, 1e-30, None, ALU.max).then_inc(s_F, 1)
            dve.wait_ge(s_sig, 2)
            for h in range(BH):
                c = slice(h * 512, (h + 1) * 512)
                ins = dve.tensor_scalar(k[:, c], k[:, c], oml[:, h:h + 1], None, ALU.mult)
            ins.then_inc(s_k, 1)
            dve.wait_ge(s_k, 1)
            dve.wait_ge(s_ln, 1)
            dve.wait_ge(s_ld, 64)
            for h in range(BH):
                c = slice(h * 512, (h + 1) * 512)
                ins = dve.tensor_tensor_scan(b[:, c], reset, f[:, c], 0.0, ALU.mult, ALU.add)
            ins.then_inc(s_b0, 1)
            dve.wait_ge(s_b0, 1)

            for hg in range(2):
                dve.wait_ge(s_at, hg + 1)
                dve.scalar_tensor_tensor(att[:, hg * 16:(hg + 1) * 16, :],
                                         m.bank[:, 4 * hg:4 * hg + 4, :].rearrange("p i (j q) -> p (i j) q", j=4), KSC,
                                         bmid(m.ident[:], 16), ALU.mult, ALU.mult).then_inc(s_pr, 1)
            dve.wait_ge(s_mk, 16)
            dve.wait_ge(s_z, 2)

            def choose(n):
                hg, lv = steps[n]
                dve.wait_ge(s_at, n + 3)
                dve.wait_ge(s_pr, n + 2)
                for j in range(4):
                    ins = dve.copy_predicated(att[:, hg * 16 + 4 * j:hg * 16 + 4 * j + 4, :], bmid(masks[:, lv, :], 4),
                                              m.bank[:, 4 * (n % 2) + j, :].rearrange("p (j q) -> p j q", j=4))
                ins.then_inc(s_pr, 1)

            for n, (hg, lv) in enumerate(steps):
                dve.wait_ge(s_exp, n + 1)
                z = LEVELS[lv]
                cs, cw = slice(hg * 2048, (hg + 1) * 2048), slice((n % 2) * 2048, (n % 2 + 1) * 2048)
                wl, wr = halves(W[:, cw], z)
                dve.tensor_tensor(halves(kW[:, cw], z)[0], halves(k[:, cs], z)[0], wl, ALU.mult)
                dve.scalar_tensor_tensor(halves(qW[:, cw], z)[1], halves(q[:, cs], z)[1], KSC, wr, ALU.mult, ALU.mult)\
                    .then_inc(s_mul, 1)
                dve.wait_ge(s_mul, n + 1)
                if n >= 1:
                    choose(n - 1)
            choose(len(steps) - 1)
            b3 = b.rearrange("p (i q) -> p i q", q=128)
            bend = b3[:, :, 127:128].broadcast_to([128, 32, 128])
            dve.wait_ge(s_e2, 1)
            dve.scalar_tensor_tensor(qW, q, KSC, W, ALU.mult, ALU.mult).then_inc(s_q2, 1)
            dve.wait_ge(s_q2, 1)
            dve.tensor_tensor(W.rearrange("p (i q) -> p i q", q=128), bend, b3, ALU.subtract).then_inc(s_sub, 1)
            dve.wait_ge(s_e2, 2)
            dve.tensor_tensor(kW, k, W, ALU.mult).then_inc(s_q2, 1)
            dve.wait_ge(s_q2, 2)
            link(dve.memset(S, 0.0))
            for n in range(8):
                dve.wait_ge(s_kt, n + 1)
                dve.tensor_copy(kdt[:, 4 * n:4 * n + 4, :], m.bank[:, n, :].rearrange("p (j q) -> p j q", j=4)).then_inc(s_ke, 1)
            dve.wait_ge(s_e2, 3)
            for n in range(2 * NC):
                c, hg = divmod(n, 2)
                dve.wait_ge(s_S, n + 1)
                for j in range(4):
                    h = 4 * hg + j
                    Sh = S[:, h * 128:(h + 1) * 128]
                    ins = dve.scalar_tensor_tensor(Sh, Sh, ebl[:, h * NC + c:h * NC + c + 1], m.bank[:, 2 + n % 2, j * 128:(j + 1) * 128],
                                                   ALU.mult, ALU.add)
                ins.then_inc(s_Sd, 1)
                dve.wait_ge(s_Sd, n + 1)
                dve.wait_ge(s_sq, n + 1)
                link(dve.tensor_reduce(rs[:, n % 2, :], sq[:, n % 2, :].rearrange("p (j q) -> p j q", j=4), AX.X, ALU.add))
                dve.tensor_scalar(rs[:, n % 2, :], rs[:, n % 2, :], 1.0 / 128, EPS, ALU.mult, ALU.add).then_inc(s_var, 1)
                dve.wait_ge(s_rstd, n + 1)
                if n >= 2:
                    dve.wait_ge(s_yt, n - 1)
                link(dve.tensor_tensor(y[:, n % 2, :].rearrange("p (j q) -> p j q", j=4),
                                       m.bank[:, n % 2, :].rearrange("p (j q) -> p j q", j=4), bc(rs[:, n % 2, :], 128), ALU.mult))
                if n == 0:
                    dve.wait_ge(s_p, 1)
                dve.tensor_tensor(y[:, n % 2, :], y[:, n % 2, :], g[:, c, hg * 512:(hg + 1) * 512], ALU.mult).then_inc(s_y, 1)

        @block.scalar
        def _(act):
            link = linker(act, s_a)
            act.activation(m.slot(3), m.slot(3), ACT.Silu).then_inc(s_g, 1)
            link(act.activation(q, q, ACT.Silu))
            link(act.activation(k, f, ACT.Sigmoid, scale=-1.0))
            act.activation(f, f, ACT.Sigmoid).then_inc(s_sig, 2)
            act.wait_ge(s_lb, 1)
            act.activation(e8, e8, ACT.Exp).then_inc(s_le, 1)
            act.wait_ge(s_F, 1)
            link(act.activation(f, f, ACT.Sqrt))
            act.activation(f, f, ACT.Ln).then_inc(s_ln, 1)
            for n in range(len(steps)):
                act.wait_ge(s_sub, n + 1)
                cw = slice((n % 2) * 2048, (n % 2 + 1) * 2048)
                act.activation(W[:, cw], W[:, cw], ACT.Exp, scale=2.0).then_inc(s_exp, 1)
            act.wait_ge(s_mul, len(steps))
            act.activation(W, b, ACT.Exp, scale=2.0).then_inc(s_e2, 1)
            act.wait_ge(s_sub, len(steps) + 1)
            act.activation(W, W, ACT.Exp, scale=2.0).then_inc(s_e2, 1)
            act.activation(ebl, b.rearrange("p (i q) -> p i q", q=128)[:, :, 127], ACT.Exp, scale=2.0).then_inc(s_e2, 1)
            act.wait_ge(s_q2, 2)
            for n in range(2 * NC):
                c, hg = divmod(n, 2)
                act.wait_ge(s_o, n + 1)
                act.activation(sq[:, n % 2, :], m.bank[:, n % 2, :], ACT.Square).then_inc(s_sq, 1)
                act.wait_ge(s_var, n + 1)
                link(act.activation(rs[:, n % 2, :], rs[:, n % 2, :], ACT.Ln))
                act.activation(rs[:, n % 2, :], rs[:, n % 2, :], ACT.Exp, scale=-0.5).then_inc(s_rstd, 1)
                if n >= 1:
                    store_y(act, n - 1)
            store_y(act, 2 * NC - 1)

    with ExitStack() as ctx:
        st = Stage(nc, ctx, "bs")
        tmp = m.slot(6).rearrange("p (i h v) -> p i h v", i=8, h=4)
        ks = m.work[:, 1300:1364].rearrange("p (h b) -> p h b", h=BH)
        sqs = m.work[:, 1364:1428]
        r64 = m.work[:, 1428:1492]
        y64 = m.work[:, 1492:1556]
        (s_out, s_v, s_a, s_f, s_g, s_vb, s_t, s_o, s_sq, s_sr, s_var, s_rstd, s_up) = (
            st.sem(n) for n in ("out", "v", "a", "f", "g", "vb", "t", "o", "sq", "sr", "var", "rstd", "up"))
        block = ctx.enter_context(nc.Block())

        @block.sync
        def _(sp):
            sp.dma_start(o["hgrn_p"][0, 0].rearrange("h k v -> k h v"), S.rearrange("p (h v) -> p h v", h=BH)).then_inc(s_out, 16)
            for bb in range(TS):
                sp.wait_ge(s_up, 2 * bb + 2)
                sp.dma_start(o["hgrn_s"][0, bb].rearrange("h k v -> k h v"), Ss[:, bb]).then_inc(s_out, 16)
            sp.wait_ge(s_out, 16 * (TS + 1))

        @block.tensor
        def _(pe):
            for bb in range(TS + 3):
                for n in range(2 * bb, 2 * bb + 2) if bb < TS else ():
                    hg = n % 2
                    if n >= 7:
                        pe.wait_ge(s_t, n - 6)
                    pe.matmul(m.bank[:, n % 7, :], m.ident[0:TS, bb:bb + 1].broadcast_to([TS, 128]), vs[:, hg * 512:(hg + 1) * 512],
                              start=True, stop=True).then_inc(s_vb, 1)
                if bb >= 3:
                    pe.wait_ge(s_up, 2 * (bb - 3) + 2)
                    for h in range(BH):
                        last = pe.matmul(m.bank[:, 7, h * TS + bb - 3:h * TS + bb - 2], Ss[:, bb - 3, h, :], qs[:, h, bb - 3:bb - 2],
                                         start=True, stop=True)
            last.then_inc(s_o, 1)
            pe.wait_ge(s_sq, 1)
            pe.matmul(m.bank[:, 7, 64:128], m.ones[:], sqs, start=True, stop=True).then_inc(s_sr, 1)

        @block.vector
        def _(dve):
            link = linker(dve, s_v)
            dve.wait_ge(s_f, 1)
            link(dve.tensor_tensor(fs, fs, bc(oml, TS), ALU.mult))
            link(dve.tensor_tensor(fs, fs, bc(lb, TS), ALU.add))
            link(dve.tensor_scalar(fs, fs, 1e-30, None, ALU.max))
            link(dve.tensor_tensor(ks, ks, bc(oml, TS), ALU.mult))
            link(dve.tensor_scalar(qs, qs, KSC, None, ALU.mult))
            for bb in range(TS):
                link(dve.tensor_tensor(Ss[:, bb], Ss[:, bb], bc(fs[:, :, bb], 128), ALU.mult))
                for hg in range(2):
                    n = 2 * bb + hg
                    dve.wait_ge(s_vb, n + 1)
                    dve.tensor_tensor(tmp[:, n % 8], m.bank[:, n % 7, :].rearrange("p (h v) -> p h v", h=4),
                                      bc(ks[:, 4 * hg:4 * hg + 4, bb], 128), ALU.mult).then_inc(s_t, 1)
                dve.wait_ge(s_t, 2 * bb + 2)
                for hg in range(2):
                    n = 2 * bb + hg
                    h4 = slice(4 * hg, 4 * hg + 4)
                    dve.tensor_tensor(Ss[:, bb, h4], Ss[:, bb, h4], tmp[:, n % 8], ALU.add).then_inc(s_up, 1)
                dve.wait_ge(s_up, 2 * bb + 2)
            dve.wait_ge(s_sr, 1)
            dve.tensor_scalar(r64, m.bank[:, 7, 64:128], 1.0 / 128, EPS, ALU.mult, ALU.add).then_inc(s_var, 1)
            dve.wait_ge(s_rstd, 1)
            link(dve.tensor_tensor(y64, m.bank[:, 7, 0:64], r64, ALU.mult))
            link(dve.tensor_scalar(y64, y64, ng, None, ALU.mult))
            link(dve.tensor_tensor(m.ybT[:, :, TP:T], y64.rearrange("p (h b) -> p h b", h=BH), gs, ALU.mult))

        @block.scalar
        def _(act):
            link = linker(act, s_a)
            link(act.activation(gs, gs, ACT.Silu))
            link(act.activation(qs, qs, ACT.Silu))
            link(act.activation(ks, fs, ACT.Sigmoid, scale=-1.0))
            act.activation(fs, fs, ACT.Sigmoid).then_inc(s_f, 1)
            act.wait_ge(s_o, 1)
            act.activation(sqs, m.bank[:, 7, 0:64], ACT.Square).then_inc(s_sq, 1)
            act.wait_ge(s_var, 1)
            link(act.activation(r64, r64, ACT.Ln))
            act.activation(r64, r64, ACT.Exp, scale=-0.5).then_inc(s_rstd, 1)


def mixer_c(nc, m, t, o):
    rel = nc.dram_tensor("rel_rows", [CH, CG, 384], F32).ap()
    og = [nc.dram_tensor(f"group{g}_out", [TP, 260], F32).ap() for g in (1, 2)]
    qT = m.slot(0)[:, 0:6 * TP].rearrange("p (i q) -> p i q", i=6)
    kt = m.slot(1)[:, 0:NC * CW].rearrange("p (c d) -> p c d", c=NC)
    vt = m.slot(2)[:, 0:NC * CW].rearrange("p (c d) -> p c d", c=NC)
    news = m.slot(3)[0:TS, 0:3 * CW]
    DIL = (1, 4, 16)

    def by_class(dst, g):
        return dst if g == 0 else dst.rearrange("p (r i) -> p i r", r=DIL[g])

    units = []
    for c in range(0, CW, 256):
        for i in (c // 128, c // 128 + 1):
            for a, b in ((0, 256), (256, TP)):
                dst = qT[:, i, :]
                cls = dst[:, a:b] if i < 2 else dst.rearrange("p (r i) -> p i r", r=DIL[i // 2])[:, a // DIL[i // 2]:b // DIL[i // 2], :]
                units.append(("chan", CQ0 + 128 * i, 128, a, b, [(cls, 128, 0, 256)]))
        units.append(("tok", CQ0 + c, 256, TP, T, [(news[:, c:c + 256], TS, 0, 256)]))
    for c0, dst, s0 in ((CK0, kt, CW), (CV0, vt, 2 * CW)):
        for c in range(0, CW, 256):
            units += tok_units(c0 + c, 256, lambda k, dst=dst, c=c: dst[:, k, c:c + 256])
            units.append(("tok", c0 + c, 256, TP, T, [(news[:, s0 + c:s0 + c + 256], TS, 0, 256)]))
    project(nc, m, t, "pc", CQ0, GT0, units)
    with ExitStack() as ctx:
        m.mixer_memory(ctx, "c")
        mixer_c_steps(nc, m, t, o, rel, og, qT, kt, vt, news, DIL, by_class)


def mixer_c_steps(nc, m, t, o, rel, og, qT, kt, vt, news, DIL, by_class):
    SCALE = CD ** -0.5
    with ExitStack() as ctx:
        st = Stage(nc, ctx, "c")
        kT = m.slot(4)[:, 0:6 * TP].rearrange("p (i q) -> p i q", i=6)
        v1 = m.slot(5)[:, 0:1024].rearrange("p (r d) -> p r d", r=4)
        v2 = m.slot(5)[:, 1024:2048].rearrange("p (r d) -> p r d", r=4)
        rvs = m.slot(5)[0:CH, 2048:2048 + 3 * 384].rearrange("p (g d) -> p g d", g=CG)
        relb = m.slot(3)[0:32, 2304:2304 + CH]
        relm = m.slot(3)[0:CH, 2320:2704]
        hot = m.slot(3)[0:32, 2704:2704 + 3 * 384].rearrange("p (g d) -> p g d", g=CG)
        bf = m.slot(8)[:, 0:2048]
        bf2 = bf[:, 1536:2048].rearrange("p (h j) -> p h j", h=4)
        flip = m.slot(3)[:, 3900:4028]
        b0 = m.slot(6)[:, 0:1024].rearrange("p (h j) -> p h j", h=4)
        b1 = m.slot(6)[:, 1024:1536].rearrange("p (h j) -> p h j", h=4)
        b2 = m.slot(6)[:, 1536:2048].rearrange("p (h j) -> p h j", h=4)
        mx = m.slot(6)[:, 2048:2056].rearrange("p (i h) -> p i h", i=2)
        den = m.slot(6)[:, 2056:2064].rearrange("p (i h) -> p i h", i=2)
        rden = m.slot(6)[:, 2064:2068]
        lmax = m.slot(6)[:, 2100:2116].rearrange("p (c h) -> p c h", c=NC)
        le = m.slot(6)[:, 2116:2164].rearrange("p (g c h) -> p g c h", g=CG, c=NC)
        lsum = m.slot(6)[:, 2164:2180].rearrange("p (c h) -> p c h", c=NC)
        yc = m.slot(6)[:, 2200:3224].rearrange("p (c d) -> p c d", c=NC)
        os_ = [m.slot(7)[:, 1040 * g:1040 * g + 1040].rearrange("p (c d) -> p c d", c=NC) for g in range(3)]
        back = [None] + [m.slot(4)[:, 1040 * g:1040 * g + 1040].rearrange("p (c d) -> p c d", c=NC) for g in range(2)]
        back[0] = os_[0]
        tmp = m.slot(5)[:, 0:1024].rearrange("p (c d) -> p c d", c=NC)
        P = [m.slot(8)[:, 1024 * i:1024 * i + 1024] for i in range(2)]
        pT = [m.slot(8)[:, 2048 + 1024 * i:3072 + 1024 * i].rearrange("p (i q) -> p i q", i=8) for i in range(2)]
        todo = [(g, n) for g in range(CG) for n in range(NC)]
        width = [256 if g == 0 and n > 0 else 128 for g, n in todo]
        nu = len(todo)
        (s_ld, s_kv, s_vl, s_bm, s_rv, s_rvs, s_rvd, s_bl, s_kt, s_ke, s_ka, s_sc, s_rd, s_sub, s_exp, s_tr, s_pe_, s_pv, s_nm,
         s_v, s_a, s_ln, s_og, s_bk, s_lx, s_le, s_yc, s_yt, s_ye, s_den, s_fl, s_fe) = (st.sem(n) for n in (
             "ld", "kv", "vl", "bm", "rv", "rvs", "rvd", "bl", "kt", "ke", "ka", "sc", "rd", "sub", "exp", "tr", "pe", "pv",
             "nm", "v", "a", "ln", "og", "bk", "lx", "le", "yc", "yt", "ye", "den", "fl", "fe"))
        block = ctx.enter_context(nc.Block())

        @block.sync
        def _(sp):
            sp.dma_start(relb, t["rel_bias"]).then_inc(s_ld, 16)
            sp.dma_start(relm, t["c_relmask"][0].partition_broadcast(CH)).then_inc(s_ld, 16)
            sp.dma_start(hot, t["c_buckets"]).then_inc(s_ld, 16)
            sp.dma_start(flip, t["c_flip"]).then_inc(s_ld, 16)
            for g, name in enumerate(("kv128", "kv512", "kv2048")):
                d = slice(256 * g, 256 * g + 256)
                for i, src in enumerate((kt, vt)):
                    if g == 0:
                        sp.dma_start(o[name + "_p"][0, 0, :, i].rearrange("q h d -> q (h d)"), src[:, 3, d]).then_inc(s_kv, 16)
                    else:
                        sp.dma_start(o[name + "_p"][0, 0, :, i].rearrange("(c q) h d -> q c (h d)", c=NC), src[:, :, d])\
                            .then_inc(s_kv, 16)
                    sp.dma_start(o[name + "_s"][0, :, 0, i].rearrange("b h d -> b (h d)"),
                                 news[:, CW * (i + 1) + 256 * g:CW * (i + 1) + 256 * g + 256]).then_inc(s_kv, 16)
            sp.wait_ge(s_rvs, CG)
            sp.dma_start(rel, rvs).then_inc(s_rvd, 16)
            sp.wait_ge(s_rvd, 16)
            sp.wait_ge(s_bm, 1)

            def toeplitz(h, g, first, rows, cols):
                return bass.AP(rel.tensor, rel[h, g, first:first + 1].offset, [[1, rows], [CG * 384, 4], [1, cols]])
            sp.dma_start(bf[:, 0:1024].rearrange("p (h j) -> p h j", h=4), toeplitz(0, 0, 0, 128, 256)).then_inc(s_bl, 16)
            sp.dma_start(bf[:, 1024:1536].rearrange("p (h j) -> p h j", h=4), toeplitz(4, 1, 128, 128, 128)).then_inc(s_bl, 16)
            for r in range(4):
                sp.dma_start(bf2[32 * r:32 * r + 32, :, 96 - 32 * r:128 - 32 * r], toeplitz(8, 2, 224, 32, 32)).then_inc(s_bl, 16)
            sp.wait_ge(s_kv, 16 * 12)
            sp.dma_start(v1, o["kv512_p"][0, 0, :, 1].rearrange("(i r) h d -> i r (h d)", r=4)).then_inc(s_vl, 16)
            vd = o["kv2048_p"][0, 0, :, 1].rearrange("(i j r) h d -> r i j (h d)", r=4, j=4)
            for r in range(4):
                sp.dma_start(v2[32 * r:32 * r + 32], vd[r]).then_inc(s_vl, 16)
            sp.wait_ge(s_nm, 2 * NC)
            sp.wait_ge(s_ln, 2 * NC)
            sp.dma_start(og[0].rearrange("(i r) d -> i r d", r=4), os_[1]).then_inc(s_og, 16)
            sp.wait_ge(s_nm, 3 * NC)
            sp.wait_ge(s_ln, 3 * NC)
            od = og[1].rearrange("(i j r) d -> r i j d", r=4, j=4)
            for r in range(4):
                sp.dma_start(od[r], os_[2][32 * r:32 * r + 32]).then_inc(s_og, 16)
            sp.wait_ge(s_og, 80)
            for g in range(2):
                sp.dma_start(back[1 + g], og[g].rearrange("(c q) d -> q c d", c=NC)).then_inc(s_bk, 16)
            sp.wait_ge(s_bk, 32)

        @block.gpsimd
        def _(pool):
            pool.memset(bf[:, 1536:2048], NEG).then_inc(s_bm, 1)

        @block.tensor
        def _(pe):
            pe.wait_ge(s_ld, 64)
            for g in range(CG):
                pe.matmul(m.bank[0:CH, 5 + g, 0:384], relb, hot[:, g, :], start=True, stop=True).then_inc(s_rv, 1)
            for i in range(6):
                b = i % 4
                if i >= 4:
                    pe.wait_ge(s_ke, i - 3)
                for c in range(NC):
                    last = pe.transpose(m.bank[:, b, c * 128:(c + 1) * 128], kt[:, c, 128 * i:128 * i + 128], m.ident[:])
                last.then_inc(s_kt, 1)
            pe.wait_ge(s_ke, 6)
            pe.wait_ge(s_rvs, CG)
            pe.wait_ge(s_bl, 16 * 6)
            for i in range(4):
                last = pe.matmul(m.bank[:, 4 + i, :], flip, bf[:, i * 512:(i + 1) * 512], start=True, stop=True)
            last.then_inc(s_fl, 1)
            pe.wait_ge(s_fe, 1)

            def scores(u):
                g, n = todo[u]
                L = width[u]
                if u >= 2:
                    pe.wait_ge(s_rd, u - 1)
                first = (n - 1) * 128 if L == 256 else n * 128
                for h in range(4):
                    i, p0 = 2 * g + h // 2, 64 * (h % 2)
                    out = m.bank[:, 2 * (u % 2) + h % 2, h // 2 * L:h // 2 * L + L]
                    last = pe.matmul(out, qT[p0:p0 + 64, i, n * 128:(n + 1) * 128], kT[p0:p0 + 64, i, first:first + L],
                                     start=True, stop=True)
                last.then_inc(s_sc, 1)

            scores(0)
            for u, (g, n) in enumerate(todo):
                if u + 1 < nu:
                    scores(u + 1)
                nb = width[u] // 128
                pe.wait_ge(s_exp, u + 1)
                for h in range(4):
                    for b in range(nb):
                        i = h * nb + b
                        last = pe.transpose(m.bank[:, 4 + i // 4, (i % 4) * 128:(i % 4 + 1) * 128],
                                            P[u % 2][:, i * 128:(i + 1) * 128], m.ident[:])
                last.then_inc(s_tr, 1)
                pe.wait_ge(s_pe_, u + 1)
                if u >= 2:
                    pe.wait_ge(s_nm, u - 1)
                if u == NC:
                    pe.wait_ge(s_vl, 16 * 5)
                for h in range(4):
                    for b in range(nb):
                        vv = (vt[:, n - nb + 1 + b, :], v1[:, n, :], v2[:, n, :])[g]
                        last = pe.matmul(m.bank[:, 6 + u % 2, h * 64:(h + 1) * 64], pT[u % 2][:, h * nb + b, :],
                                         vv[:, h * 64:(h + 1) * 64], start=(b == 0), stop=(b == nb - 1))
                last.then_inc(s_pv, 1)
            pe.wait_ge(s_yc, 1)
            for c in range(NC):
                for j in range(2):
                    last = pe.transpose(m.bank[:, j, c * 128:(c + 1) * 128], yc[:, c, j * 128:(j + 1) * 128], m.ident[:])
            last.then_inc(s_yt, 1)

        @block.vector
        def _(dve):
            link = linker(dve, s_v)
            dve.wait_ge(s_ld, 64)
            for g in range(CG):
                dve.wait_ge(s_rv, g + 1)
                dve.tensor_tensor(rvs[:, g, :], m.bank[0:CH, 5 + g, 0:384], relm, ALU.add).then_inc(s_rvs, 1)
            for i in range(6):
                dve.wait_ge(s_kt, i + 1)
                src = m.bank[:, i % 4, :]
                if i // 2:
                    src = src.rearrange("p (i r) -> p i r", r=DIL[i // 2])
                dve.tensor_copy(by_class(kT[:, i, :], i // 2), src).then_inc(s_ke, 1)
            dve.wait_ge(s_fl, 1)
            dve.tensor_copy(m.slot(6)[:, 0:2048].rearrange("p (i q) -> p i q", i=4), m.bank[:, 4:8, :]).then_inc(s_fe, 1)
            dve.wait_ge(s_fe, 1)

            def shifted(u):
                g, n = todo[u]
                L = width[u]
                bias = ((b0 if L == 256 else b0[:, :, 128:256]), b1, b2)[g]
                p3 = P[u % 2][:, 0:4 * L].rearrange("p (h j) -> p h j", h=4)
                dve.wait_ge(s_sc, u + 1)
                for b in range(2):
                    ins = dve.scalar_tensor_tensor(p3[:, b::2, :], m.bank[:, 2 * (u % 2) + b, 0:2 * L].rearrange("p (h j) -> p h j", j=L),
                                                   SCALE, bias[:, b::2, :], ALU.mult, ALU.add)
                ins.then_inc(s_rd, 1)
                dve.wait_ge(s_rd, u + 1)
                if u >= 2:
                    dve.wait_ge(s_ln, u - 1)
                link(dve.tensor_reduce(mx[:, u % 2, :], p3, AX.X, ALU.max))
                dve.tensor_tensor(p3, p3, bc(mx[:, u % 2, :], L), ALU.subtract).then_inc(s_sub, 1)
                dve.wait_ge(s_sub, u + 1)

            shifted(0)
            for u, (g, n) in enumerate(todo):
                if u + 1 < nu:
                    shifted(u + 1)
                L = width[u]
                p3 = P[u % 2][:, 0:4 * L].rearrange("p (h j) -> p h j", h=4)
                dve.wait_ge(s_exp, u + 1)
                dve.tensor_reduce(den[:, u % 2, :], p3, AX.X, ALU.add).then_inc(s_den, 1)
                dve.wait_ge(s_den, u + 1)
                link(dve.reciprocal(rden, den[:, u % 2, :]))
                dve.wait_ge(s_pv, u + 1)
                dve.tensor_tensor(os_[g][:, n, 0:256].rearrange("p (h d) -> p h d", h=4),
                                  m.bank[:, 6 + u % 2, 0:256].rearrange("p (h d) -> p h d", h=4), bc(rden, CD), ALU.mult)\
                    .then_inc(s_nm, 1)
                dve.wait_ge(s_nm, u + 1)
                dve.wait_ge(s_lx, u + 1)
                link(dve.tensor_tensor(os_[g][:, n, 256:260], den[:, u % 2, :], mx[:, u % 2, :], ALU.add))
                dve.tensor_copy(rden[:, 0:1], mx[:, u % 2, 0:1]).then_inc(s_ln, 1)
            dve.wait_ge(s_bk, 32)
            ls = [back[g][:, :, 256:260] for g in range(3)]
            link(dve.tensor_tensor(lmax, ls[0], ls[1], ALU.max))
            link(dve.tensor_tensor(lmax, lmax, ls[2], ALU.max))
            for g in range(3):
                ins = dve.tensor_tensor(le[:, g], ls[g], lmax, ALU.subtract)
            ins.then_inc(s_le, 1)
            dve.wait_ge(s_le, 2)
            link(dve.tensor_tensor(lsum, le[:, 0], le[:, 1], ALU.add))
            link(dve.tensor_tensor(lsum, lsum, le[:, 2], ALU.add))
            link(dve.reciprocal(lsum, lsum))
            for g in range(3):
                link(dve.tensor_tensor(le[:, g], le[:, g], lsum, ALU.mult))
                for c in range(NC):
                    ov = back[g][:, c, 0:256].rearrange("p (h d) -> p h d", h=4)
                    dst = (yc if g == 0 else tmp)[:, c, :].rearrange("p (h d) -> p h d", h=4)
                    link(dve.tensor_tensor(dst, ov, bc(le[:, g, c, :], CD), ALU.mult))
                if g:
                    link(dve.tensor_tensor(yc, yc, tmp, ALU.add))
            dve.tensor_copy(rden[:, 0:1], lsum[:, 0, 0:1]).then_inc(s_yc, 1)
            dve.wait_ge(s_yt, 1)
            for j in range(2):
                link(dve.tensor_copy(m.ycT[:, j, 0:TP], m.bank[:, j, :]))

        @block.scalar
        def _(act):
            for u in range(nu):
                L = width[u]
                act.wait_ge(s_sub, u + 1)
                act.activation(P[u % 2][:, 0:4 * L], P[u % 2][:, 0:4 * L], ACT.Exp).then_inc(s_exp, 1)
                act.wait_ge(s_tr, u + 1)
                nb = L // 128
                act.copy(pT[u % 2][:, 0:4 * nb, :], m.bank[:, 4:4 + nb, :].rearrange("p b (i q) -> p (b i) q", q=128)).then_inc(s_pe_, 1)
                act.wait_ge(s_nm, u + 1)
                act.activation(den[:, u % 2, :], den[:, u % 2, :], ACT.Ln).then_inc(s_lx, 1)
            act.wait_ge(s_le, 1)
            act.activation(le, le, ACT.Exp).then_inc(s_le, 1)

    with ExitStack() as ctx:
        st = Stage(nc, ctx, "cs")
        kv = [m.slot(s).rearrange("p (b d) -> p b d", b=TS) for s in (4, 5, 6)]
        prod = [m.slot(7)[:, 0:2048], m.slot(7)[:, 2048:4096], m.slot(8)[:, 0:2048]]
        sT = m.slot(8)[:, 2048:2144].rearrange("p (g b h) -> p g b h", g=CG, b=TS)
        pTs = m.slot(8)[:, 2144:2240].rearrange("p (i b) -> p i b", i=CH)
        sm = m.slot(0)[0:TS, 0:CH * 129].rearrange("p (i j) -> p i j", i=CH)
        bias = m.slot(0)[0:TS, 1600:1600 + CH * 129].rearrange("p (i j) -> p i j", i=CH)
        new = m.slot(1)[0:TS, 0:768]
        sc12 = m.slot(1)[0:TS, 768:780]
        mx12 = m.slot(1)[0:TS, 780:792]
        den12 = m.slot(1)[0:TS, 792:804]
        lse12 = m.slot(1)[0:TS, 804:816]
        m4, d4 = m.slot(1)[0:TS, 816:820], m.slot(1)[0:TS, 820:824]
        rd12 = m.slot(1)[0:TS, 824:836]
        tn = m.slot(1)[0:TS, 836:1092]
        half = m.slot(1)[:, 1100:1116]
        (s_b, s_q, s_pr, s_s, s_t, s_sm, s_e, s_p, s_pt, s_w, s_o, s_v, s_l, s_l2) = (st.sem(n) for n in (
            "b", "q", "pr", "s", "t", "sm", "e", "p", "pt", "w", "o", "v", "l", "l2"))
        s_cache = [st.sem(f"cache{g}") for g in range(CG)]
        s_sum = st.sem("sum")
        block = ctx.enter_context(nc.Block())

        @block.gpsimd
        def _(pool):
            pool.wait_ge(s_w, 3)
            pool.tensor_tensor(prod[0], prod[0], prod[1], ALU.add).then_inc(s_sum, 1)

        @block.sync
        def _(sp):
            for g, name in enumerate(("cache_kv_w128", "cache_kv_w512", "cache_kv_w2048")):
                src = t[name][0].rearrange("b (j r) s h d -> j r b (s h d)", r=DIL[g])[:, 0]
                sp.dma_start(kv[g], src).then_inc(s_cache[g], 16)
                sp.dma_start(bias[:, 4 * g:4 * g + 4, :], rel[4 * g:4 * g + 4, g, 127:256].partition_broadcast(TS)).then_inc(s_b, 16)

        @block.tensor
        def _(pe):
            for g in range(CG):
                if g >= 2:
                    pe.wait_ge(s_pr, g - 1)
                for b in range(TS):
                    last = pe.matmul(m.bank[:, 4 * (g % 2) + b // 2, (b % 2) * 256:(b % 2 + 1) * 256],
                                     m.ident[0:TS, b:b + 1].broadcast_to([TS, 128]), news[:, 256 * g:256 * g + 256], start=True, stop=True)
                last.then_inc(s_q, 1)
            pe.wait_ge(s_s, CG)
            for i in range(CH):
                g, h = divmod(i, 4)
                last = pe.transpose(m.bank[0:TS, 4 + i // 4, (i % 4) * 128:(i % 4 + 1) * 128], sT[:, g, :, h], m.ident[:])
            last.then_inc(s_t, 1)
            pe.wait_ge(s_p, 1)
            for i in range(CH):
                last = pe.transpose(m.bank[:, 0, 8 * i:8 * i + 8], sm[:, i, 0:128], m.ident[0:TS, 0:TS])
            last.then_inc(s_pt, 1)
            pe.wait_ge(s_w, CG + 2)
            for j in range(2):
                for b in range(TS):
                    pe.matmul(m.bank[:, 1, 8 * j + b:8 * j + b + 1], prod[0][:, 256 * b + 128 * j:256 * b + 128 * j + 128],
                              m.ones[:, 0:1], start=True, stop=True)
                last = pe.matmul(m.bank[:, 2, 8 * j:8 * j + 8], tn[:, 128 * j:128 * j + 128], m.ident[0:TS, 0:TS], start=True, stop=True)
            last.then_inc(s_o, 1)

        @block.vector
        def _(dve):
            link = linker(dve, s_v)
            for g in range(CG):
                dve.wait_ge(s_cache[g], 16)
                dve.wait_ge(s_q, g + 1)
                for a in range(4):
                    ins = dve.tensor_tensor(prod[g][:, a * 512:(a + 1) * 512].rearrange("p (b d) -> p b d", b=2),
                                            kv[g][:, 2 * a:2 * a + 2, 0:256],
                                            m.bank[:, 4 * (g % 2) + a, :].rearrange("p (b d) -> p b d", b=2), ALU.mult)
                ins.then_inc(s_pr, 1)
                dve.wait_ge(s_pr, g + 1)
                dve.tensor_reduce(sT[:, g].rearrange("p b h -> p (b h)"), prod[g].rearrange("p (i d) -> p i d", d=CD), AX.X, ALU.add)\
                    .then_inc(s_s, 1)
            link(dve.tensor_tensor(new, news[:, 0:CW], news[:, CW:2 * CW], ALU.mult))
            link(dve.tensor_reduce(sc12, new.rearrange("p (i d) -> p i d", d=CD), AX.X, ALU.add))
            dve.wait_ge(s_b, 48)
            link(dve.scalar_tensor_tensor(sm[:, :, 128], sc12, SCALE, bias[:, :, 128], ALU.mult, ALU.add))
            dve.wait_ge(s_t, 1)
            for g in range(CG):
                link(dve.scalar_tensor_tensor(sm[:, 4 * g:4 * g + 4, 0:128], m.bank[0:TS, 4 + g, :].rearrange("p (i j) -> p i j", i=4),
                                              SCALE, bias[:, 4 * g:4 * g + 4, 0:128], ALU.mult, ALU.add))
            link(dve.tensor_reduce(mx12, sm, AX.X, ALU.max))
            dve.tensor_tensor(sm, sm, bc(mx12, 129), ALU.subtract).then_inc(s_sm, 1)
            dve.wait_ge(s_e, 1)
            dve.tensor_reduce(den12, sm, AX.X, ALU.add).then_inc(s_l, 1)
            dve.wait_ge(s_l2, 1)
            link(dve.tensor_tensor(lse12, lse12, mx12, ALU.add))
            link(dve.tensor_reduce(m4, lse12.rearrange("p (g h) -> p h g", g=CG), AX.X, ALU.max))
            dve.tensor_tensor(lse12.rearrange("p (g h) -> p g h", g=CG), lse12.rearrange("p (g h) -> p g h", g=CG),
                              bmid(m4, CG), ALU.subtract).then_inc(s_l, 1)
            dve.wait_ge(s_l2, 2)
            link(dve.tensor_reduce(d4, lse12.rearrange("p (g h) -> p h g", g=CG), AX.X, ALU.add))
            link(dve.reciprocal(d4, d4))
            link(dve.reciprocal(rd12, den12))
            link(dve.tensor_tensor(rd12, rd12, lse12, ALU.mult))
            link(dve.tensor_tensor(rd12.rearrange("p (g h) -> p g h", g=CG), rd12.rearrange("p (g h) -> p g h", g=CG), bmid(d4, CG), ALU.mult))
            dve.tensor_tensor(sm, sm, bc(rd12, 129), ALU.mult).then_inc(s_p, 1)
            dve.wait_ge(s_p, 1)
            link(dve.tensor_tensor(new.rearrange("p (i d) -> p i d", d=CD), news[:, 2 * CW:3 * CW].rearrange("p (i d) -> p i d", d=CD),
                                   bc(sm[:, :, 128], CD), ALU.mult))
            link(dve.tensor_tensor(tn, new[:, 0:256], new[:, 256:512], ALU.add))
            dve.tensor_tensor(tn, tn, new[:, 512:768], ALU.add).then_inc(s_w, 1)
            dve.wait_ge(s_pt, 1)
            link(dve.tensor_copy(pTs, m.bank[:, 0, 0:96].rearrange("p (i b) -> p i b", i=CH)))
            for g in range(CG):
                for b in range(TS):
                    ins = dve.tensor_tensor(prod[g][:, 256 * b:256 * b + 256].rearrange("p (h d) -> p h d", h=4),
                                            kv[g][:, b, 256:512].rearrange("p (h d) -> p h d", h=4), bc(pTs[:, 4 * g:4 * g + 4, b], CD), ALU.mult)
                ins.then_inc(s_w, 1)
            dve.wait_ge(s_w, CG + 1)
            dve.wait_ge(s_sum, 1)
            dve.tensor_tensor(prod[0], prod[0], prod[2], ALU.add).then_inc(s_w, 1)
            dve.wait_ge(s_o, 1)
            link(dve.tensor_copy(half, m.bank[:, 2, 0:16]))
            link(dve.tensor_tensor(m.ycT[:, :, TP:T], m.bank[:, 1, 0:16].rearrange("p (j b) -> p j b", j=2),
                                   half.rearrange("p (j b) -> p j b", j=2), ALU.add))

        @block.scalar
        def _(act):
            act.wait_ge(s_sm, 1)
            act.activation(sm, sm, ACT.Exp).then_inc(s_e, 1)
            act.wait_ge(s_l, 1)
            act.activation(lse12, den12, ACT.Ln).then_inc(s_l2, 1)
            act.wait_ge(s_l, 2)
            act.activation(lse12, lse12, ACT.Exp).then_inc(s_l2, 1)


TILES = [(c * 128, 128) for c in range(NC)] + [(TP, TS)]
NT = len(TILES)
SLOTS_E = 128
PASSES = -(-T // SLOTS_E)
ITEMS = PASSES * NE


def merge(nc, m, t):
    with ExitStack() as ctx:
        st = Stage(nc, ctx, "mg")
        raw = [m.arena[:, 2048 * i:2048 * (i + 1)].rearrange("p (g k n) -> p g k n", g=2, k=KT) for i in range(4)]
        sg = [m.arena[:, 8192 + HALF * i:8192 + HALF * (i + 1)] for i in range(2)]
        tm = m.arena[:, 8192 + 2 * HALF:8192 + 3 * HALF]
        kts = {"a": KT, "b": KT, "c": 2}
        jobs = [(br, ct) for br in "acb" for ct in range(KT)]
        ysrc = {"a": m.yaT, "b": m.ybT, "c": m.ycT}
        yparts = {"a": (m.y_hi, m.y_lo), "b": (m.y_hi, m.y_lo), "c": (m.yc_hi, m.yc_lo)}
        gate_at = {"a": 0, "b": 1, "c": 2}
        s_w = [st.sem(f"w{i}") for i in range(4)]
        s_hi, s_lo, s_wo, s_pe, s_sig, s_prod, s_add = (st.sem(n) for n in ("hi", "lo", "wo", "pe", "sig", "prod", "add"))

        start = [("x", 0, 0), ("w", 0, 0), ("a", 0, 0), ("w", 0, 1), ("x", 0, 1), ("a", 0, 1), ("c", 0, 0), ("c", 0, 1)]

        def splits_at(n):
            return ([("w", n + 1, 0), ("w", n + 1, 1)] if n + 1 < len(jobs) else []) + ([("b", 0, 0), ("b", 0, 1)] if n == KT + 1 else [])
        order = {sp: i + 1 for i, sp in enumerate(start + [q for n in range(len(jobs)) for q in splits_at(n)])}

        def operands(kind, i, h):
            if kind == "w":
                k = kts[jobs[i][0]] if h else KT
                return raw[i % 4][:, h, 0:k, :], m.w_hi[:, i % 2, h, 0:k, :], m.w_lo[:, i % 2, h, 0:k, :]
            cols = slice(h * HALF, (h + 1) * HALF)
            src, (hi, lo) = (m.xT, (m.x_hi, m.x_lo)) if kind == "x" else (ysrc[kind], yparts[kind])
            return src[:, :, cols], hi[:, :, cols], lo[:, :, cols]
        block = ctx.enter_context(nc.Block())

        @block.sync
        def _(sp):
            for n, (br, ct) in enumerate(jobs):
                if n >= 4:
                    sp.wait_ge(s_lo, order[("w", n - 4, 1)])
                c0 = GT0 + gate_at[br] * D + ct * 128
                sp.dma_start(raw[n % 4][:, 0], t["w_in"][0, :, c0:c0 + 128].rearrange("(k p) n -> p k n", p=128)).then_inc(s_w[n % 4], 16)
                sp.dma_start(raw[n % 4][:, 1, 0:kts[br], :],
                             t["w_branch_" + br][0, :, ct * 128:(ct + 1) * 128].rearrange("(k p) n -> p k n", p=128)).then_inc(s_w[n % 4], 16)
            for i, (dst, br) in enumerate(zip(wout_tiles(m), "ab")):
                sp.wait_ge(s_lo, order[(br, 0, 1)])
                sp.dma_start(dst, t["w_out"][0, :, i * 512:(i + 1) * 512].rearrange("(k p) n -> p k n", p=128)).then_inc(s_wo, 16)
            sp.wait_ge(s_wo, 32)

        @block.tensor
        def _(pe):
            for n, (br, ct) in enumerate(jobs):
                for h in range(2):
                    cols = slice(h * HALF, (h + 1) * HALF)
                    if n >= 2:
                        pe.wait_ge(s_prod, 2 * (n - 2) + h + 1)
                    for g in range(2):
                        pe.wait_ge(s_lo, max(order[("w", n, g)], order[(br, 0, h) if g else ("x", 0, h)]))
                        hi, lo = yparts[br] if g else (m.x_hi, m.x_lo)
                        nk = kts[br] if g else KT
                        for k in range(nk):
                            for j, (w, x) in enumerate(((m.w_hi, hi), (m.w_hi, lo), (m.w_lo, hi))):
                                last = pe.matmul(m.bank[:, 4 * (n % 2) + 2 * h + g, 0:HALF], w[:, n % 2, g, k, :], x[:, k, cols],
                                                 start=(k == 0 and j == 0), stop=(k == nk - 1 and j == 2))
                    last.then_inc(s_pe, 1)

        @block.scalar
        def _(act):
            def split(q):
                kind, i, h = q
                if kind == "w" and h == 0:
                    act.wait_ge(s_w[i % 4], 32 * (i // 4 + 1))
                src, hi, lo = operands(*q)
                act.copy(hi, src).then_inc(s_hi, 1)
            for q in start:
                split(q)
            for n in range(len(jobs)):
                if n >= 1:
                    act.wait_ge(s_pe, 2 * n)
                for q in splits_at(n):
                    split(q)
                for h in range(2):
                    i = 2 * n + h
                    act.wait_ge(s_pe, i + 1)
                    if i >= 2:
                        act.wait_ge(s_prod, i - 1)
                    act.activation(sg[h], m.bank[:, 4 * (n % 2) + 2 * h, 0:HALF], ACT.Sigmoid).then_inc(s_sig, 1)

        @block.vector
        def _(dve):
            def split(q):
                src, hi, lo = operands(*q)
                dve.wait_ge(s_hi, order[q])
                dve.tensor_tensor(lo, src, hi.bitcast(F32), ALU.subtract).then_inc(s_lo, 1)
            for q in start:
                split(q)
            for n, (br, ct) in enumerate(jobs):
                if n == 0:
                    dve.wait_ge(s_lo, len(start))
                for q in splits_at(n):
                    split(q)
                for h in range(2):
                    i = 2 * n + h
                    dst = m.xT[:, ct, h * HALF:(h + 1) * HALF]
                    out = dst if br == "a" else tm
                    dve.wait_ge(s_sig, i + 1)
                    dve.tensor_tensor(out, sg[h], m.bank[:, 4 * (n % 2) + 2 * h + 1, 0:HALF], ALU.mult).then_inc(s_prod, 1)
                    dve.wait_ge(s_prod, i + 1)
                    if br != "a":
                        dve.tensor_tensor(dst, dst, tm, ALU.add).then_inc(s_add, 1)
                        dve.wait_ge(s_add, i + 1 - 2 * KT)


def wout_tiles(m):
    return [y[:].rearrange("p k q -> p (k q)")[:, 0:SLOT].rearrange("p (k n) -> p k n", k=KT) for y in (m.yaT, m.ybT)]


def project_out(nc, m, t):
    x1d = nc.dram_tensor("x1_rows", [T, D], F32).ap()
    wo = wout_tiles(m)
    with ExitStack() as ctx:
        st = Stage(nc, ctx, "o")
        xr = m.norm[:, 0:NT * D].rearrange("p (c d) -> p c d", c=NT)
        lng, lnb = m.norm[:, NT * D:NT * D + D], m.norm[:, NT * D + D:NT * D + 2 * D]
        bn = m.norm[:, NT * D + 2 * D:NT * D + 2 * D + 64]
        s_ld, s_mm, s_x, s_out, s_t2, s_e2, s_hi, s_lo = (st.sem(n) for n in ("ld", "mm", "x", "out", "t2", "e2", "hi", "lo"))
        start = [("m", 0, 0), ("w", 0, 0), ("w", 0, 1), ("w", 1, 0), ("w", 1, 1)] + [("m", c, 0) for c in range(1, NT)]
        order = {q: i + 1 for i, q in enumerate(start)}

        def operands(kind, i, j):
            if kind == "w":
                ks = slice(4 * j, 4 * j + 4)
                return wo[i][:, ks, :], m.wo_hi[:, i, ks, :], m.wo_lo[:, i, ks, :]
            a, R = TILES[i]
            return tuple(x[:, :, a:a + R] for x in (m.xT, m.mg_hi, m.mg_lo))
        norm = LayerNorm(st, bn, lng, lnb, xr)
        s_n = norm.s_n
        block = ctx.enter_context(nc.Block())

        def x1_transposes(pe, c):
            R = TILES[c][1]
            pe.wait_ge(s_n, c + 1)
            if c >= 1:
                pe.wait_ge(s_e2, c)
            for k in range(KT):
                last = pe.transpose(m.bank[:, 6 + k // 4, (k % 4) * 128:(k % 4) * 128 + R], xr[0:R, c, k * 128:(k + 1) * 128], m.ident[0:R, 0:R])
            last.then_inc(s_t2, 1)

        def rest(act, c):
            a, R = TILES[c]
            act.wait_ge(s_t2, c + 1)
            act.copy(m.xT[:, :, a:a + R], m.bank[:, 6:8, :].rearrange("p b (j q) -> p (b j) q", j=4)[:, :, 0:R]).then_inc(s_e2, 1)

        @block.sync
        def _(sp):
            sp.dma_start(xr[:, 0:NC, :], t["x_prompt"][0].rearrange("(c p) d -> p c d", p=128)).then_inc(s_ld, 16)
            sp.dma_start(xr[0:TS, NC, :], t["x_sample"][:, 0, :]).then_inc(s_ld, 16)
            sp.dma_start(lng, t["ln1_g"][0].partition_broadcast(128)).then_inc(s_ld, 16)
            sp.dma_start(lnb, t["ln1_b"][0].partition_broadcast(128)).then_inc(s_ld, 16)
            for c, (a, R) in enumerate(TILES):
                sp.wait_ge(s_n, c + 1)
                sp.dma_start(x1d[a:a + R], xr[0:R, c, :]).then_inc(s_out, 16)
            sp.wait_ge(s_out, 16 * NT)

        @block.tensor
        def _(pe):
            for c, (a, R) in enumerate(TILES):
                if c >= 2:
                    pe.wait_ge(s_x, 2 * (c - 1))
                for h in range(2):
                    for k in range(KT):
                        if k % 4 == 0:
                            pe.wait_ge(s_lo, max(order[("m", c, 0)], order[("w", h, k // 4)]))
                        for j, (x, w) in enumerate(((m.mg_hi, m.wo_hi), (m.mg_hi, m.wo_lo), (m.mg_lo, m.wo_hi))):
                            last = pe.matmul(m.bank[0:R, 2 + 2 * (c % 2) + h, :], x[:, k, a:a + R], w[:, h, k, :],
                                             start=(k == 0 and j == 0), stop=(k == KT - 1 and j == 2))
                    last.then_inc(s_mm, 1)
                if c >= 1:
                    x1_transposes(pe, c - 1)
            x1_transposes(pe, NT - 1)

        @block.vector
        def _(dve):
            for q in start:
                src, hi, lo = operands(*q)
                dve.wait_ge(s_hi, order[q])
                dve.tensor_tensor(lo, src, hi.bitcast(F32), ALU.subtract).then_inc(s_lo, 1)
            dve.wait_ge(s_ld, 64)
            for c, (a, R) in enumerate(TILES):
                x = xr[0:R, c, :]
                for h in range(2):
                    dve.wait_ge(s_mm, 2 * c + h + 1)
                    xh = x[:, h * 512:(h + 1) * 512]
                    dve.scalar_tensor_tensor(xh, xh, ALPHA, m.bank[0:R, 2 + 2 * (c % 2) + h, :], ALU.mult, ALU.add).then_inc(s_x, 1)
                dve.wait_ge(s_x, 2 * c + 2)
                norm.statistics(dve, c)
                norm.factors(dve, c)

        @block.scalar
        def _(act):
            for q in start:
                src, hi, lo = operands(*q)
                act.copy(hi, src).then_inc(s_hi, 1)
            for c in range(NT):
                norm.root(act, c)
                norm.scale(act, c)
                if c >= 1:
                    rest(act, c - 1)
            rest(act, NT - 1)

        @block.gpsimd
        def _(pool):
            pool.wait_ge(s_ld, 64)
            for c in range(NT):
                norm.finish(pool, c)

    return x1d


class LayerNorm:

    def __init__(self, st, bn, gain, shift, x):
        self.bn, self.gain, self.shift, self.x = bn, gain, shift, x
        self.s_stat, self.s_var, self.s_rstd, self.s_scale, self.s_xn, self.s_g, self.s_n = (
            st.sem(n) for n in ("lnstat", "lnvar", "lnrstd", "lnscale", "lnx", "lng", "n"))

    def tile(self, c):
        R = TILES[c][1]
        return self.x[0:R, c, :], self.bn[0:R, 16 * (c % 4):16 * (c % 4) + 16], R

    def statistics(self, dve, c):
        x, bn, R = self.tile(c)
        if c >= 4:
            dve.wait_ge(self.s_xn, c - 3)
        for h in range(2):
            dve.bn_stats(bn[:, 6 * h:6 * h + 6], x[:, h * 512:(h + 1) * 512]).then_inc(self.s_stat, 1)
        dve.wait_ge(self.s_stat, 3 * c + 2)
        dve.bn_aggr(bn[:, 12:14], bn[:, 0:12]).then_inc(self.s_stat, 1)
        dve.wait_ge(self.s_stat, 3 * c + 3)
        dve.tensor_scalar(bn[:, 14:15], bn[:, 13:14], EPS, None, ALU.add).then_inc(self.s_var, 1)

    def factors(self, dve, c):
        x, bn, R = self.tile(c)
        dve.wait_ge(self.s_rstd, c + 1)
        dve.reciprocal(bn[:, 15:16], bn[:, 14:15]).then_inc(self.s_scale, 1)
        dve.wait_ge(self.s_scale, 2 * c + 1)
        dve.tensor_scalar(bn[:, 14:15], bn[:, 12:13], bn[:, 15:16], -1.0, ALU.mult, ALU.mult).then_inc(self.s_scale, 1)

    def root(self, act, c):
        x, bn, R = self.tile(c)
        act.wait_ge(self.s_var, c + 1)
        act.activation(bn[:, 14:15], bn[:, 14:15], ACT.Sqrt).then_inc(self.s_rstd, 1)

    def scale(self, act, c):
        x, bn, R = self.tile(c)
        act.wait_ge(self.s_scale, 2 * c + 2)
        act.activation(x, x, ACT.Identity, scale=bn[:, 15:16], bias=bn[:, 14:15]).then_inc(self.s_xn, 1)

    def finish(self, pool, c):
        x, bn, R = self.tile(c)
        pool.wait_ge(self.s_xn, c + 1)
        pool.tensor_tensor(x, x, self.gain[0:R], ALU.mult).then_inc(self.s_g, 1)
        pool.wait_ge(self.s_g, c + 1)
        pool.tensor_tensor(x, x, self.shift[0:R], ALU.add).then_inc(self.s_n, 1)


WEIGHT_ORDER = (0, 1, 4, 2, 5, 3)


def expert_tiles(m):
    return ([m.slot(q).rearrange("p (k n) -> p k n", k=KT) for q in range(4)]
            + [m.slot(4 + h).rearrange("p (f n) -> p f n", f=4) for h in range(2)])


def load_expert_tile(sp, m, t, e, q):
    if q < 4:
        src = t["moe_w1"][0, e, :, q * 512:(q + 1) * 512].rearrange("(k p) n -> p k n", p=128)
    else:
        src = t["moe_w2"][0, e, (q - 4) * 512:(q - 3) * 512, :].rearrange("(f p) n -> p f n", p=128)
    return sp.dma_start(expert_tiles(m)[q], src)


def route(nc, m, t, s_w):
    table = nc.dram_tensor("slot_table", [(ITEMS + 1) * SLOTS_E, 2], U32).ap()
    w = m.work
    gates = w[:, 0:20].rearrange("p (c k) -> p c k", c=NT)
    dest = w[:, 20:40].bitcast(U32).rearrange("p (c k) -> p c k", c=NT)
    counts = w[:, 40:42].bitcast(mybir.dt.int32)
    GT = m.GT
    with ExitStack() as ctx:
        st = Stage(nc, ctx, "r")
        s = m.route
        rw = s[:, 0:256].rearrange("p (k n) -> p k n", k=KT)
        rb, iota = s[:, 256:288], s[:, 288:320]
        tok = s[:, 320:360].bitcast(U32).rearrange("p (c k i) -> p c k i", c=NT, k=TOPK)
        stri = s[:, 500:628]
        lg = s[:, 640:800].rearrange("p (c e) -> p c e", c=NT)
        v8 = s[:, 800:840].rearrange("p (c e) -> p c e", c=NT)
        i8 = s[:, 840:880].bitcast(U32).rearrange("p (c e) -> p c e", c=NT)
        if8 = s[:, 880:920].rearrange("p (c e) -> p c e", c=NT)
        mask = s[:, 1000:1160].rearrange("p (c e) -> p c e", c=NT)
        G = s[:, 1160:1320].rearrange("p (c e) -> p c e", c=NT)
        oh = s[:, 1320:1960].rearrange("p (c k e) -> p c k e", c=NT, k=TOPK)
        pr = s[:, 1960:2088].rearrange("p (k e) -> p k e", k=TOPK)
        rank = s[:, 2090:2094]
        df = s[:, 2094:2098]
        gs = s[:, 2100:2101]
        cm = s[:, 2101:2104]
        ge = s[:, 2104:2108]
        s_ld, s_lg, s_v, s_e, s_ee, s_m, s_rk, s_g, s_gt, s_d, s_sc = (st.sem(n) for n in (
            "ld", "lg", "v", "e", "ee", "m", "rk", "g", "gt", "d", "sc"))
        block = ctx.enter_context(nc.Block())

        @block.sync
        def _(sp):
            sp.dma_start(rw, t["router_w"][0].rearrange("(k p) n -> p k n", p=128)).then_inc(s_ld, 16)
            sp.dma_start(rb, t["router_b"][0].partition_broadcast(128)).then_inc(s_ld, 16)
            sp.dma_start(iota, t["c_iota"][0].partition_broadcast(128)).then_inc(s_ld, 16)
            sp.dma_start(s[:, 320:360].bitcast(U32), t["c_token"]).then_inc(s_ld, 16)
            for q in WEIGHT_ORDER:
                load_expert_tile(sp, m, t, 0, q).then_inc(s_w[q], 16)

        @block.gpsimd
        def _(pool):
            pool.dma_start(table, t["c_empty"]).then_inc(s_sc, 16)
            pool.wait_ge(s_sc, 16)
            pool.wait_ge(s_ld, 64)
            n = 1
            for c, (a, R) in enumerate(TILES):
                pool.wait_ge(s_d, c + 1)
                for k in range(TOPK):
                    pool.indirect_dma_start(out=table, out_offset=bass.IndirectOffsetOnAxis(ap=dest[0:R, c, k:k + 1], axis=0),
                                            in_=tok[0:R, c, k, :], in_offset=None).then_inc(s_sc, 16)
                    n += 1
            pool.wait_ge(s_sc, 16 * n)

        @block.tensor
        def _(pe):
            pe.wait_ge(s_ld, 64)
            for c, (a, R) in enumerate(TILES):
                for k in range(KT):
                    last = pe.matmul(m.bank[0:R, 3 + c, 0:32], m.xT[:, k, a:a + R], rw[:, k, :], start=(k == 0), stop=(k == KT - 1))
                last.then_inc(s_lg, 1)
            pe.wait_ge(s_m, NT + 1)
            for c, (a, R) in enumerate(TILES):
                for b in range(c):
                    pe.matmul(m.bank[0:R, 1, 32 * c:32 * c + 32], m.ones[:, 0:R], mask[:, b, :], start=(b == 0), stop=False)
                pe.matmul(m.bank[0:R, 1, 32 * c:32 * c + 32], stri[0:R, 0:R], mask[0:R, c, :], start=(c == 0), stop=True)
            for c, (a, R) in enumerate(TILES):
                last = pe.matmul(m.bank[:, 2, 0:32], m.ones[0:R, :], mask[0:R, c, :], start=(c == 0), stop=(c == NT - 1))
            last.then_inc(s_rk, 1)
            pe.wait_ge(s_g, NT)
            for c, (a, R) in enumerate(TILES):
                last = pe.transpose(m.bank[0:NE, 3 + c // 4, (c % 4) * 128:(c % 4) * 128 + R], G[0:R, c, :], m.ident[0:R, 0:R])
            last.then_inc(s_gt, 1)

        @block.vector
        def _(dve):
            link = linker(dve, s_v)
            dve.wait_ge(s_ld, 64)
            dve.tensor_tensor(stri, m.tri[:], m.ident[:], ALU.subtract).then_inc(s_m, 1)
            for c, (a, R) in enumerate(TILES):
                dve.wait_ge(s_lg, c + 1)
                link(dve.tensor_tensor(lg[0:R, c], m.bank[0:R, 3 + c, 0:32], rb[0:R], ALU.add))
                link(dve.max(v8[0:R, c], lg[0:R, c]))
                link(dve.max_index(i8[0:R, c], v8[0:R, c], lg[0:R, c]))
                link(dve.tensor_copy(if8[0:R, c], i8[0:R, c]))
                for k in range(TOPK):
                    link(dve.tensor_scalar(oh[0:R, c, k], iota[0:R], if8[0:R, c, k:k + 1], None, ALU.is_equal))
                dve.tensor_reduce(mask[0:R, c], oh[0:R, c].rearrange("p k e -> p e k"), AX.X, ALU.add).then_inc(s_m, 1)
                dve.tensor_scalar(gates[0:R, c], v8[0:R, c, 0:TOPK], v8[0:R, c, 0:1], None, ALU.subtract).then_inc(s_e, 1)
            dve.wait_ge(s_m, NT + 1)
            for c, (a, R) in enumerate(TILES):
                dve.wait_ge(s_ee, c + 1)
                link(dve.tensor_reduce(gs[0:R], gates[0:R, c], AX.X, ALU.add))
                link(dve.reciprocal(gs[0:R], gs[0:R]))
                link(dve.tensor_scalar(gates[0:R, c], gates[0:R, c], gs[0:R], None, ALU.mult))
                link(dve.tensor_scalar(G[0:R, c], oh[0:R, c, 0], gates[0:R, c, 0:1], None, ALU.mult))
                for k in range(1, TOPK):
                    ins = dve.scalar_tensor_tensor(G[0:R, c], oh[0:R, c, k], gates[0:R, c, k:k + 1], G[0:R, c], ALU.mult, ALU.add)
                    if k < TOPK - 1:
                        link(ins)
                ins.then_inc(s_g, 1)
            dve.wait_ge(s_rk, 1)
            for c, (a, R) in enumerate(TILES):
                link(dve.tensor_tensor(pr[0:R], oh[0:R, c], bmid(m.bank[0:R, 1, 32 * c:32 * c + 32], TOPK), ALU.mult))
                link(dve.tensor_reduce(rank[0:R], pr[0:R], AX.X, ALU.add))
                link(dve.scalar_tensor_tensor(df[0:R], if8[0:R, c, 0:TOPK], float(SLOTS_E), rank[0:R], ALU.mult, ALU.add))
                for p in range(1, PASSES):
                    link(dve.tensor_scalar(ge[0:R], rank[0:R], float(p * SLOTS_E), float((NE - 1) * SLOTS_E), ALU.is_ge, ALU.mult))
                    link(dve.tensor_tensor(df[0:R], df[0:R], ge[0:R], ALU.add))
                dve.tensor_copy(dest[0:R, c], df[0:R]).then_inc(s_d, 1)
            link(dve.tensor_reduce(cm[:, 0:1], m.bank[:, 2, 0:32], AX.X, ALU.max))
            link(dve.memset(cm[:, 1:2], 1.0))
            for p in range(1, PASSES):
                link(dve.tensor_scalar(cm[:, 2:3], cm[:, 0:1], float(p * SLOTS_E), None, ALU.is_gt))
                link(dve.tensor_tensor(cm[:, 1:2], cm[:, 1:2], cm[:, 2:3], ALU.add))
            link(dve.tensor_scalar(cm[:, 0:1], cm[:, 1:2], float(NE), None, ALU.mult))
            link(dve.tensor_copy(counts, cm[:, 0:2]))
            dve.wait_ge(s_gt, 1)
            link(dve.tensor_copy(GT[:, 0:512], m.bank[0:NE, 3, :]))
            link(dve.tensor_copy(GT[:, 512:T], m.bank[0:NE, 4, 0:TS]))

        @block.scalar
        def _(act):
            for c, (a, R) in enumerate(TILES):
                act.wait_ge(s_e, c + 1)
                act.activation(gates[0:R, c], gates[0:R, c], ACT.Exp).then_inc(s_ee, 1)
    return table, gates, counts, GT


def experts(nc, m, t, x1d, table, counts, s_w):
    ybuf = nc.dram_tensor("choice_out", [TOPK * T + SLOTS_E, D], F32).ap()
    tiles = expert_tiles(m)
    w1, w2 = tiles[0:4], tiles[4:6]
    flat = m.xT[:].rearrange("p k q -> p (k q)")
    xg = flat[:, 0:1024]
    xgT = flat[:, 1024:2048].rearrange("p (k q) -> p k q", k=KT)
    ysb = flat[:, 2048:3072]
    tb = [flat[:, 3072 + 512 * i:3584 + 512 * i].rearrange("p (g f q) -> p g f q", g=2, f=2) for i in range(2)]
    b1r = flat[0:NE, 2048:2048 + 2 * FF]
    small = m.small
    sg = [small[:, 256 * i:256 * i + 256].rearrange("p (f q) -> p f q", f=2) for i in range(2)]
    b1T = small[:, 512:1024].rearrange("p (i e) -> p i e", e=NE)
    bcur = small[:, 1024:1040].rearrange("p (g f) -> p g f", g=2)
    itok = small[:, 1040:1041].bitcast(U32)
    irow = small[:, 1041:1042].bitcast(U32)
    with ExitStack() as ctx:
        st = Stage(nc, ctx, "e")
        s_done = [st.sem(f"done{q}") for q in range(6)]
        s_split = [st.sem(f"split{h}") for h in range(2)]
        (s_b1, s_bt, s_bc, s_ix, s_go, s_yfree, s_ir, s_g, s_tr, s_xe, s_pre, s_sig, s_act, s_ye, s_st, s_v, s_bq,
         s_whi, s_prod, s_ahi, s_wlo) = (st.sem(n) for n in (
            "b1", "bt", "bc", "ix", "go", "yfree", "ir", "g", "tr", "xe", "pre", "sig", "act", "ye", "st", "v", "bq",
            "whi", "prod", "ahi", "wlo"))

        def half(tile, q):
            h, n = divmod(q, 2)
            return tile[:, 4 * h:4 * h + 4, n * 512:(n + 1) * 512]
        block = ctx.enter_context(nc.Block())

        @block.sync
        def _(sp):
            sp.dma_start(b1r, t["moe_b1"][0]).then_inc(s_b1, 16)
            for q in range(6):
                sp.sem_inc(s_done[q], 1)
            for h in range(2):
                sp.sem_inc(s_split[h], 1)
            items = sp.value_load(counts[0:1, 0:1], min_val=NE, max_val=ITEMS)
            with sp.Fori(1, items) as i:
                for q in WEIGHT_ORDER:
                    sp.wait_ge(s_done[q] if q < 4 else s_split[q - 4], i + 1)
                    load_expert_tile(sp, m, t, i % NE, q).then_inc(s_w[q], 16)

        @block.gpsimd
        def _(pool):
            items = pool.value_load(counts[0:1, 0:1], min_val=NE, max_val=ITEMS)

            def gather(i, number):
                pool.dma_start(itok, table[bass.ds(i * SLOTS_E, SLOTS_E), 0:1], allow_slow_non_contiguous=True).then_inc(s_ix, 16)
                pool.wait_ge(s_ix, number * 16)
                pool.sem_inc(s_go, 1)
                pool.indirect_dma_start(out=xg, out_offset=None, in_=x1d,
                                        in_offset=bass.IndirectOffsetOnAxis(ap=itok, axis=0)).then_inc(s_g, 16)
            gather(0, 1)
            with pool.Fori(0, items) as i:
                pool.wait_ge(s_g, (i + 1) * 16)
                pool.wait_ge(s_tr, i + 1)
                gather(i + 1, i + 2)
                pool.dma_start(irow, table[bass.ds(i * SLOTS_E, SLOTS_E), 1:2], allow_slow_non_contiguous=True).then_inc(s_ir, 16)
                pool.wait_ge(s_ir, (i + 1) * 16)
                pool.wait_ge(s_ye, i * 2 + 3)
                pool.sem_inc(s_go, 1)
                pool.indirect_dma_start(out=ybuf, out_offset=bass.IndirectOffsetOnAxis(ap=irow, axis=0), in_=ysb, in_offset=None)\
                    .then_inc(s_st, 16)
                pool.wait_ge(s_st, (i + 1) * 16)
                pool.sem_inc(s_yfree, 1)
            pool.wait_ge(s_g, items * 16 + 16)

        @block.tensor
        def _(pe):
            items = pe.value_load(counts[0:1, 0:1], min_val=NE, max_val=ITEMS)
            pe.wait_ge(s_b1, 16)
            for g in range(2):
                for f in range(8):
                    last = pe.transpose(m.bank[:, 0, (8 * g + f) * 32:(8 * g + f + 1) * 32],
                                        b1r[:, 256 * f + g:256 * f + 256:2], m.ident[0:NE, 0:NE])
            last.then_inc(s_bt, 1)

            def transposes(number):
                pe.wait_ge(s_g, number * 16)
                for k in range(KT):
                    last = pe.transpose(m.bank[:, 6 + k // 4, (k % 4) * 128:(k % 4 + 1) * 128], xg[:, k * 128:(k + 1) * 128], m.ident[:])
                last.then_inc(s_tr, 1)
            transposes(1)
            pe.wait_ge(s_bc, 1)
            with pe.Fori(0, items) as i:
                pe.wait_ge(s_xe, i + 1)
                for q in range(4):
                    pe.wait_ge(s_w[q], (i + 1) * 16)
                    for g in range(2):
                        for f in range(2):
                            for k in range(KT):
                                last = pe.matmul(m.bank[:, q, (2 * g + f) * 128:(2 * g + f + 1) * 128],
                                                 w1[q][:, k, 256 * f + g:256 * f + 256:2], xgT[:, k, :], start=(k == 0), stop=(k == KT - 1))
                    last.then_inc(s_done[q], 1)
                transposes(i + 2)
                pe.wait_ge(s_ye, i * 2 + 1)
                for h in range(2):
                    pe.wait_ge(s_act, i * 4 + 2 * h + 2)
                    pe.wait_ge(s_split[h], i + 2)
                    for n in range(2):
                        cols = slice(n * 512, (n + 1) * 512)
                        for f in range(4 * h, 4 * h + 4):
                            for j, (a, w) in enumerate(((m.act_hi, m.w2_hi), (m.act_hi, m.w2_lo), (m.act_lo, m.w2_hi))):
                                last = pe.matmul(m.bank[:, 4 + n, :], a[:, f, :], w[:, f, cols],
                                                 start=(f == 0 and j == 0), stop=(f == 7 and j == 2))
                        if h == 1:
                            last.then_inc(s_done[4 + n], 1)

        @block.vector
        def _(dve):
            link = linker(dve, s_v)
            dve.wait_ge(s_bt, 1)
            dve.tensor_copy(b1T, m.bank[:, 0, :].rearrange("p (i e) -> p i e", e=NE)).then_inc(s_bc, 1)
            dve.wait_ge(s_bc, 1)
            passes = dve.value_load(counts[0:1, 1:2], min_val=1, max_val=PASSES)
            with dve.Fori(0, passes) as p:
                with dve.Fori(0, NE) as e:
                    i = p * NE + e
                    dve.tensor_copy(bcur.rearrange("p g f -> p (g f)"), b1T[:, :, e]).then_inc(s_bq, 1)
                    dve.wait_ge(s_bq, i + 1)
                    for q in range(5):
                        if q < 4:
                            tt = tb[q % 2]
                            dve.wait_ge(s_done[q], i + 2)
                            dve.tensor_tensor(tt, m.bank[:, q, :].rearrange("p (g f q) -> p g f q", g=2, f=2),
                                              bc(bcur[:, :, 2 * q:2 * q + 2], 128), ALU.add).then_inc(s_v, 1)
                            dve.wait_ge(s_v, i * 12 + 3 * q + 1)
                            dve.tensor_scalar(tt[:, 0], tt[:, 0], 7.0, None, ALU.min).then_inc(s_pre, 1)
                            dve.tensor_scalar(tt[:, 1], tt[:, 1], 7.0, -7.0, ALU.min, ALU.max).then_inc(s_v, 1)
                            dve.wait_ge(s_pre, i * 4 + q + 1)
                            dve.wait_ge(s_v, i * 12 + 3 * q + 2)
                            dve.scalar_tensor_tensor(tt[:, 1], tt[:, 1], 1.0, tt[:, 0], ALU.add, ALU.mult).then_inc(s_v, 1)
                            dve.wait_ge(s_v, i * 12 + 3 * q + 3)
                        if q > 0:
                            dve.wait_ge(s_sig, i * 4 + q)
                            dve.tensor_tensor(tb[(q - 1) % 2][:, 1], tb[(q - 1) % 2][:, 1], sg[(q - 1) % 2], ALU.mult).then_inc(s_prod, 1)
                        if q < 4:
                            dve.wait_ge(s_whi, i * 4 + q + 1)
                            dve.tensor_tensor(half(m.w2_lo, q), w2[q // 2][:, :, q % 2 * 512:(q % 2 + 1) * 512],
                                              half(m.w2_hi, q).bitcast(F32), ALU.subtract).then_inc((s_wlo, s_split[0], s_wlo, s_split[1])[q], 1)
                        if q > 0:
                            dve.wait_ge(s_prod, i * 4 + q)
                            dve.wait_ge(s_ahi, i * 4 + q)
                            dve.tensor_tensor(m.act_lo[:, 2 * q - 2:2 * q, :], tb[(q - 1) % 2][:, 1],
                                              m.act_hi[:, 2 * q - 2:2 * q, :].bitcast(F32), ALU.subtract).then_inc(s_act, 1)
                            dve.wait_ge(s_act, i * 4 + q)

        @block.scalar
        def _(act):
            items = act.value_load(counts[0:1, 0:1], min_val=NE, max_val=ITEMS)

            def rows_T(number):
                act.wait_ge(s_tr, number)
                act.copy(xgT, m.bank[:, 6:8, :].rearrange("p b (j q) -> p (b j) q", j=4)).then_inc(s_xe, 1)
            act.sem_inc(s_ye, 1)
            act.sem_inc(s_yfree, 1)
            rows_T(1)
            with act.Fori(0, items) as i:
                for q in range(5):
                    if q < 4:
                        if q % 2 == 0:
                            act.wait_ge(s_w[4 + q // 2], (i + 1) * 16)
                        act.copy(half(m.w2_hi, q), w2[q // 2][:, :, q % 2 * 512:(q % 2 + 1) * 512]).then_inc(s_whi, 1)
                        act.wait_ge(s_pre, i * 4 + q + 1)
                        act.activation(sg[q % 2], tb[q % 2][:, 0], ACT.Sigmoid, scale=1.702).then_inc(s_sig, 1)
                    if q > 0:
                        act.wait_ge(s_prod, i * 4 + q)
                        act.copy(m.act_hi[:, 2 * q - 2:2 * q, :], tb[(q - 1) % 2][:, 1]).then_inc(s_ahi, 1)
                rows_T(i + 2)
                act.wait_ge(s_yfree, i + 1)
                for n in range(2):
                    act.wait_ge(s_done[4 + n], i + 2)
                    act.copy(ysb[:, n * 512:(n + 1) * 512], m.bank[:, 4 + n, :]).then_inc(s_ye, 1)
    return ybuf


def combine(nc, m, t, o, x1d, ybuf, gates, GT):
    with ExitStack() as ctx:
        st = Stage(nc, ctx, "f")
        rows = [m.slot(i).rearrange("p (k d) -> p k d", k=TOPK) for i in range(2)]
        x1 = m.arena[:, 2 * SLOT:2 * SLOT + NT * D].rearrange("p (c d) -> p c d", c=NT)
        lng, lnb = m.slot(4)[:, 0:D], m.slot(4)[:, D:2 * D]
        bn = m.slot(4)[:, 2 * D:2 * D + 64]
        b2 = m.slot(5)[0:NE, 0:D]
        s_ld, s_mm, s_v, s_out, s_r = (st.sem(n) for n in ("ld", "mm", "v", "out", "r"))
        norm = LayerNorm(st, bn, lng, lnb, x1)
        s_n = norm.s_n
        s_rows = [st.sem(f"rows{i}") for i in range(2)]
        block = ctx.enter_context(nc.Block())

        def load_rows(sp, c):
            a, R = TILES[c]
            sp.dma_start(rows[c % 2][0:R], ybuf[TOPK * a:TOPK * (a + R)].rearrange("(q k) d -> q k d", k=TOPK)).then_inc(s_rows[c % 2], 16)

        @block.sync
        def _(sp):
            sp.dma_start(x1[:, 0:NC, :], x1d[0:TP].rearrange("(c p) d -> p c d", p=128)).then_inc(s_ld, 16)
            sp.dma_start(x1[0:TS, NC, :], x1d[TP:T]).then_inc(s_ld, 16)
            sp.dma_start(b2, t["moe_b2"][0]).then_inc(s_ld, 16)
            sp.dma_start(lng, t["ln2_g"][0].partition_broadcast(128)).then_inc(s_ld, 16)
            sp.dma_start(lnb, t["ln2_b"][0].partition_broadcast(128)).then_inc(s_ld, 16)
            for c in range(2):
                load_rows(sp, c)
            for c, (a, R) in enumerate(TILES):
                if c + 2 < NT:
                    sp.wait_ge(s_r, c + 1)
                    load_rows(sp, c + 2)
                sp.wait_ge(s_n, c + 1)
                dst = o["y_p"][0, a:a + R] if c < NC else o["y_s"][:, 0, :]
                sp.dma_start(dst, x1[0:R, c, :]).then_inc(s_out, 16)
            sp.wait_ge(s_out, 16 * NT)

        @block.tensor
        def _(pe):
            pe.wait_ge(s_ld, 80)
            for c, (a, R) in enumerate(TILES):
                if c >= 4:
                    pe.wait_ge(s_r, c - 3)
                for h in range(2):
                    last = pe.matmul(m.bank[0:R, 2 * (c % 4) + h, :], GT[:, a:a + R], b2[:, h * 512:(h + 1) * 512], start=True, stop=True)
                last.then_inc(s_mm, 1)

        @block.vector
        def _(dve):
            link = linker(dve, s_v)
            dve.wait_ge(s_ld, 80)
            for c, (a, R) in enumerate(TILES):
                x = x1[0:R, c, :]
                dve.wait_ge(s_mm, c + 1)
                link(dve.scalar_tensor_tensor(x.rearrange("p (h n) -> p h n", h=2), x.rearrange("p (h n) -> p h n", h=2), ALPHA,
                                              m.bank[0:R, 2 * (c % 4):2 * (c % 4) + 2, :], ALU.mult, ALU.add))
                dve.wait_ge(s_rows[c % 2], 16 * (c // 2 + 1))
                for k in range(TOPK):
                    ins = dve.scalar_tensor_tensor(x, rows[c % 2][0:R, k, :], gates[0:R, c, k:k + 1], x, ALU.mult, ALU.add)
                    if k < TOPK - 1:
                        link(ins)
                ins.then_inc(s_r, 1)
                dve.wait_ge(s_r, c + 1)
                norm.statistics(dve, c)
                norm.factors(dve, c)

        @block.scalar
        def _(act):
            for c in range(NT):
                norm.root(act, c)
                norm.scale(act, c)

        @block.gpsimd
        def _(pool):
            pool.wait_ge(s_ld, 80)
            for c in range(NT):
                norm.finish(pool, c)


def decoder_layer(nc, t, o):
    with ExitStack() as ctx:
        m = Mem(nc, ctx)
        with ExitStack() as stream:
            m.branch_memory(stream)
            with ExitStack() as mixers:
                m.low_memory(mixers)
                load_x(nc, m, t)
                mixer_a(nc, m, t, o)
                mixer_b(nc, m, t, o)
                mixer_c(nc, m, t, o)
            with ExitStack() as merging:
                m.merge_memory(merging)
                merge(nc, m, t)
            with ExitStack() as norm:
                m.norm_memory(norm)
                x1d = project_out(nc, m, t)
        with ExitStack() as moe:
            m.moe_memory(moe)
            st = Stage(nc, moe, "ew")
            s_w = [st.sem(f"w{q}") for q in range(6)]
            table, gates, counts, GT = route(nc, m, t, s_w)
            ybuf = experts(nc, m, t, x1d, table, counts, s_w)
            combine(nc, m, t, o, x1d, ybuf, gates, GT)


def constants():
    import numpy as np
    i = np.arange(128)
    c = {"c_ident": np.eye(128, dtype=np.float32), "c_tri": (i[:, None] <= i[None, :]).astype(np.float32),
         "c_ones": np.ones((128, 128), np.float32), "c_headexp": np.repeat(np.eye(AH, dtype=np.float32), AP_, axis=1),
         "c_flip": np.ascontiguousarray(np.eye(128, dtype=np.float32)[::-1]), "c_reset": (np.arange(TP) % 128 != 0).astype(np.float32)[None],
         "c_iota": np.arange(NE, dtype=np.float32)[None]}
    masks = np.zeros((128, len(LEVELS), 128), np.uint32)
    for n, z in enumerate(LEVELS):
        masks[:, n, :] = (i[:, None] // z == i[None, :] // z) & (i[:, None] % z < z // 2) & (i[None, :] % z >= z // 2)
    c["c_masks"] = masks
    rel = 255 - np.arange(384)
    valid = (rel >= 0) & (rel <= 128)
    hot = np.zeros((32, CG, 384), np.float32)
    for g, dil in enumerate((1, 4, 16)):
        d = np.maximum(rel, 0) * dil
        large = 16 + (np.log(np.maximum(d, 1).astype(np.float32) / 16) / np.float32(np.log(128)) * 16).astype(np.int32)
        bucket = np.where(d < 16, d, np.clip(large, 0, 31))
        hot[bucket[valid], g, np.arange(384)[valid]] = 1
    c["c_buckets"] = hot
    c["c_relmask"] = np.where(valid, 0, NEG).astype(np.float32)[None]
    token = np.zeros((128, NT, TOPK, 2), np.uint32)
    for n, (a, R) in enumerate(TILES):
        token[:R, n, :, 0] = a + np.arange(R)[:, None]
        token[:R, n, :, 1] = TOPK * (a + np.arange(R)[:, None]) + np.arange(TOPK)
    c["c_token"] = token.reshape(128, -1)
    empty = np.zeros(((ITEMS + 1) * SLOTS_E, 2), np.uint32)
    empty[:, 1] = TOPK * T + np.arange(len(empty)) % SLOTS_E
    c["c_empty"] = empty
    return c


INPUTS = ["x_prompt", "x_sample", "state_conv", "state_ssm", "state_hgrn", "cache_kv_w128", "cache_kv_w512", "cache_kv_w2048",
          "w_in", "conv_w", "conv_b", "dt_bias", "a_log", "d_skip", "ssm_norm_g", "hgrn_lb", "hgrn_norm_g", "rel_bias",
          "w_branch_a", "w_branch_b", "w_branch_c", "w_out", "ln1_g", "ln1_b", "router_w", "router_b",
          "moe_w1", "moe_b1", "moe_w2", "moe_b2", "ln2_g", "ln2_b"]
OUTPUTS = [("y_p", (1, TP, D)), ("y_s", (TS, 1, D)), ("conv_p", (1, 1, 3, ACH)), ("conv_s", (1, TS, 3, ACH)),
           ("ssm_p", (1, 1, AH, AP_, AN)), ("ssm_s", (1, TS, AH, AP_, AN)), ("hgrn_p", (1, 1, BH, BK, 128)),
           ("hgrn_s", (1, TS, BH, BK, 128)), ("kv128_p", (1, 1, 128, 2, 4, CD)), ("kv128_s", (1, TS, 1, 2, 4, CD)),
           ("kv512_p", (1, 1, TP, 2, 4, CD)), ("kv512_s", (1, TS, 1, 2, 4, CD)), ("kv2048_p", (1, 1, TP, 2, 4, CD)),
           ("kv2048_s", (1, TS, 1, 2, 4, CD))]


def kernel(**inputs):
    import numpy as np
    import concourse.bacc as bacc
    from concourse.bass_utils import run_bass_kernel_spmd

    nc = bacc.Bacc("TRN2", target_bir_lowering=False, num_devices=1)
    data = {n: np.ascontiguousarray(inputs[n]) for n in INPUTS} | constants()
    t = {n: nc.dram_tensor(f"in_{n}", a.shape, mybir.dt.from_np(a.dtype), kind="ExternalInput").ap() for n, a in data.items()}
    o = {n: nc.dram_tensor(f"out_{n}", shape, F32, kind="ExternalOutput").ap() for n, shape in OUTPUTS}
    decoder_layer(nc, t, o)
    r = run_bass_kernel_spmd(nc, [{f"in_{n}": a for n, a in data.items()}], core_ids=[0])
    return tuple(r.results[0][f"out_{n}"] for n, _ in OUTPUTS)
```
